# Optimizing a Trainium2 kernel written in Bass

```python
import math
import jax, jax.numpy as jnp
from jax import lax
import numpy as np

D_MODEL = 1024
BATCH = 1
SEQ = 256
DEPTH = 2

CHUNK = 64
N_META = 16
Q_BLOCK = 128
EPS = 1e-6
ROPE_THETA = 10000.0

RET_HEADS = 4
RET_QK_DIM = 128
RET_V_DIM = 128
RET_QK_W = RET_HEADS * RET_QK_DIM
RET_WIDTH = RET_HEADS * RET_V_DIM

MLA_HEADS = 4
MLA_NOPE = 128
MLA_ROPE = 64
MLA_V = 128
MLA_Q_RANK = 256
MLA_KV_RANK = 128
MLA_WIDTH = MLA_HEADS * MLA_V

MIX_WIDTH = RET_WIDTH + MLA_WIDTH
IN_SIZES = (RET_QK_W, RET_QK_W, RET_WIDTH, RET_WIDTH, MLA_Q_RANK, MLA_KV_RANK, MLA_ROPE)
D_IN = sum(IN_SIZES)
IN_SPLITS = tuple(int(s) for s in np.cumsum(IN_SIZES)[:-1])

D_FF = 3584
N_EXPERTS = 8
TOP_K = 2
N_DENSE = (DEPTH + 1) // 2
N_MOE = DEPTH // 2

kernel_name = "hybrid_retention_mla_moe_chunk_causal"

def rms_norm(x, g):
    xf = x.astype(jnp.float32)
    y = xf * lax.rsqrt(jnp.mean(xf * xf, axis=-1, keepdims=True) + EPS)
    return (y * g.astype(jnp.float32)).astype(x.dtype)

def head_rms(t):
    tf = t.astype(jnp.float32)
    return (tf * lax.rsqrt(jnp.mean(tf * tf, axis=-1, keepdims=True) + EPS)).astype(t.dtype)

def to_heads(t, h):
    b, l, _ = t.shape
    return t.reshape(b, l, h, -1).transpose(0, 2, 1, 3)

def from_heads(t):
    b, h, l, d = t.shape
    return t.transpose(0, 2, 1, 3).reshape(b, l, h * d)

def rope(t, pos):
    d = t.shape[-1]
    inv = ROPE_THETA ** (-jnp.arange(0, d, 2, dtype=jnp.float32) / d)
    ang = pos[:, None] * inv[None, :]
    cos, sin = jnp.cos(ang), jnp.sin(ang)
    tf = t.astype(jnp.float32)
    t1, t2 = tf[..., : d // 2], tf[..., d // 2:]
    out = jnp.concatenate([t1 * cos - t2 * sin, t1 * sin + t2 * cos], axis=-1)
    return out.astype(t.dtype)

def chunk_end(p):
    if p < N_META:
        return N_META
    return N_META + ((p - N_META) // CHUNK + 1) * CHUNK

def retention(q, k, v):
    b, h, l, dk = q.shape
    dv = v.shape[-1]
    dt = q.dtype
    pad = (-N_META) % CHUNK
    padw = ((0, 0), (0, 0), (pad, 0), (0, 0))
    q, k, v = jnp.pad(q, padw), jnp.pad(k, padw), jnp.pad(v, padw)
    lp = l + pad
    nc = lp // CHUNK
    qc = q.reshape(b, h, nc, CHUNK, dk)
    kc = k.reshape(b, h, nc, CHUNK, dk)
    vc = v.reshape(b, h, nc, CHUNK, dv)

    log_gamma = jnp.log1p(-jnp.exp2(-5.0 - jnp.arange(h, dtype=jnp.float32)))
    idx = jnp.arange(CHUNK, dtype=jnp.float32)
    dist = jnp.abs(idx[:, None] - idx[None, :])
    decay_in = jnp.exp(log_gamma[:, None, None] * dist).astype(dt)
    xi = jnp.exp(log_gamma[:, None] * (idx + 1.0)).astype(dt)
    zeta = jnp.exp(log_gamma[:, None] * (CHUNK - 1.0 - idx)).astype(dt)
    g_chunk = jnp.exp(log_gamma * CHUNK).astype(dt)

    scores = jnp.einsum('bhncd,bhnsd->bhncs', qc, kc) * decay_in[None, :, None]
    y_intra = jnp.einsum('bhncs,bhnse->bhnce', scores, vc)

    kv_chunk = jnp.einsum('bhnsd,bhnse->bhnde', kc * zeta[None, :, None, :, None], vc)

    def step(state, kv):
        return g_chunk[None, :, None, None] * state + kv, state

    s0 = jnp.zeros((b, h, dk, dv), dt)
    _, s_prev = lax.scan(step, s0, jnp.moveaxis(kv_chunk, 2, 0))
    y_inter = jnp.einsum('bhncd,nbhde->bhnce', qc, s_prev) * xi[None, :, None, :, None]
    y = (y_intra + y_inter).reshape(b, h, lp, dv)
    return y[:, :, pad:]

def latent_attention(c_q, c_kv, k_rope, q_norm, w_uq, kv_norm, w_ukv, pos, chunk_ids):
    l = c_q.shape[1]
    q = to_heads(rms_norm(c_q, q_norm) @ w_uq, MLA_HEADS)
    q_nope, q_pe = q[..., :MLA_NOPE], rope(q[..., MLA_NOPE:], pos)
    kv = to_heads(rms_norm(c_kv, kv_norm) @ w_ukv, MLA_HEADS)
    k_nope, v = kv[..., :MLA_NOPE], kv[..., MLA_NOPE:]
    k_pe = rope(k_rope, pos)
    scale = (MLA_NOPE + MLA_ROPE) ** -0.5
    outs = []
    for q0 in range(0, l, Q_BLOCK):
        q1 = min(q0 + Q_BLOCK, l)
        kend = min(chunk_end(q1 - 1), l)
        s = (jnp.einsum('bhqd,bhkd->bhqk', q_nope[:, :, q0:q1], k_nope[:, :, :kend])
             + jnp.einsum('bhqd,bkd->bhqk', q_pe[:, :, q0:q1], k_pe[:, :kend])) * scale
        mask = chunk_ids[q0:q1, None] >= chunk_ids[None, :kend]
        s = jnp.where(mask, s.astype(jnp.float32), -jnp.inf)
        p = jax.nn.softmax(s, axis=-1).astype(v.dtype)
        outs.append(jnp.einsum('bhqk,bhkd->bhqd', p, v[:, :, :kend]))
    return jnp.concatenate(outs, axis=2)

def swiglu(h, w_gate, w_up, w_down):
    return (jax.nn.silu(h @ w_gate) * (h @ w_up)) @ w_down

def moe_swiglu(h, router_w, w_gate, w_up, w_down):
    logits = (h @ router_w).astype(jnp.float32)
    top_val, top_idx = lax.top_k(logits, TOP_K)
    gates = jax.nn.softmax(top_val, axis=-1)
    gate_dense = jnp.sum(jax.nn.one_hot(top_idx, N_EXPERTS, dtype=jnp.float32) * gates[..., None], axis=-2)
    gate_dense = gate_dense.astype(h.dtype)
    out = jnp.zeros_like(h)
    for e in range(N_EXPERTS):
        out = out + gate_dense[..., e:e + 1] * swiglu(h, w_gate[e], w_up[e], w_down[e])
    return out

def setup_inputs(seed: int = 0) -> dict:
    key = jax.random.key(seed)
    ks = jax.random.split(key, 24)
    f32 = jnp.float32

    def nrm(k, shape, fan_in):
        return jax.random.normal(k, shape, f32) * (fan_in ** -0.5)

    def gain(k, shape):
        return 1.0 + 0.02 * jax.random.normal(k, shape, f32)

    return {
        "x": jax.random.normal(ks[0], (BATCH, SEQ, D_MODEL), f32),
        "meta_tokens": jax.random.normal(ks[1], (N_META, D_MODEL), f32),
        "attn_norm": gain(ks[2], (DEPTH, D_MODEL)),
        "w_in": nrm(ks[3], (DEPTH, D_MODEL, D_IN), D_MODEL),
        "q_norm": gain(ks[4], (DEPTH, MLA_Q_RANK)),
        "w_uq": nrm(ks[5], (DEPTH, MLA_Q_RANK, MLA_HEADS * (MLA_NOPE + MLA_ROPE)), MLA_Q_RANK),
        "kv_norm": gain(ks[6], (DEPTH, MLA_KV_RANK)),
        "w_ukv": nrm(ks[7], (DEPTH, MLA_KV_RANK, MLA_HEADS * (MLA_NOPE + MLA_V)), MLA_KV_RANK),
        "ret_out_gain": gain(ks[8], (DEPTH, RET_WIDTH)),
        "mla_out_gain": gain(ks[9], (DEPTH, MLA_WIDTH)),
        "w_out": nrm(ks[10], (DEPTH, MIX_WIDTH, D_MODEL), MIX_WIDTH),
        "ffn_norm": gain(ks[11], (DEPTH, D_MODEL)),
        "dense_w_gate": nrm(ks[12], (N_DENSE, D_MODEL, D_FF), D_MODEL),
        "dense_w_up": nrm(ks[13], (N_DENSE, D_MODEL, D_FF), D_MODEL),
        "dense_w_down": nrm(ks[14], (N_DENSE, D_FF, D_MODEL), D_FF),
        "router_w": nrm(ks[15], (N_MOE, D_MODEL, N_EXPERTS), D_MODEL),
        "moe_w_gate": nrm(ks[16], (N_MOE, N_EXPERTS, D_MODEL, D_FF), D_MODEL),
        "moe_w_up": nrm(ks[17], (N_MOE, N_EXPERTS, D_MODEL, D_FF), D_MODEL),
        "moe_w_down": nrm(ks[18], (N_MOE, N_EXPERTS, D_FF, D_MODEL), D_FF),
        "final_norm": gain(ks[19], (D_MODEL,)),
    }

def reference(x, meta_tokens, attn_norm, w_in, q_norm, w_uq, kv_norm, w_ukv,
              ret_out_gain, mla_out_gain, w_out, ffn_norm, dense_w_gate, dense_w_up,
              dense_w_down, router_w, moe_w_gate, moe_w_up, moe_w_down, final_norm):
    b = x.shape[0]
    meta = jnp.broadcast_to(meta_tokens.astype(x.dtype)[None], (b, N_META, x.shape[-1]))
    h_res = jnp.concatenate([meta, x], axis=1)
    l = h_res.shape[1]
    p_int = jnp.arange(l, dtype=jnp.int32)
    pos = p_int.astype(jnp.float32)
    chunk_ids = jnp.where(p_int < N_META, 0, 1 + (p_int - N_META) // CHUNK)

    for layer in range(DEPTH):
        hn = rms_norm(h_res, attn_norm[layer])
        proj = hn @ w_in[layer]
        r_q, r_k, r_v, r_g, c_q, c_kv, k_rope = jnp.split(proj, IN_SPLITS, axis=-1)

        rq = rope(to_heads(r_q, RET_HEADS), pos) * (RET_QK_DIM ** -0.5)
        rk = rope(to_heads(r_k, RET_HEADS), pos)
        rv = to_heads(r_v, RET_HEADS)
        y_ret = from_heads(head_rms(retention(rq, rk, rv)))
        y_ret = y_ret * ret_out_gain[layer] * jax.nn.silu(r_g)

        y_mla = latent_attention(c_q, c_kv, k_rope, q_norm[layer], w_uq[layer],
                                 kv_norm[layer], w_ukv[layer], pos, chunk_ids)
        y_mla = from_heads(head_rms(y_mla)) * mla_out_gain[layer]

        mixed = jnp.concatenate([y_ret, y_mla], axis=-1) @ w_out[layer]
        h_res = h_res + mixed

        hn = rms_norm(h_res, ffn_norm[layer])
        li = layer // 2
        if layer % 2 == 0:
            ff = swiglu(hn, dense_w_gate[li], dense_w_up[li], dense_w_down[li])
        else:
            ff = moe_swiglu(hn, router_w[li], moe_w_gate[li], moe_w_up[li], moe_w_down[li])
        h_res = h_res + ff

    out = rms_norm(h_res, final_norm)
    return out[:, N_META:]


_drawn_inputs = setup_inputs


def setup_inputs(seed=0):
    import zlib

    import numpy as np

    out = dict(_drawn_inputs(seed))
    spreads = {}
    factors = {'ret_out_gain': 4.641, 'final_norm': 8.163, 'q_norm': 3.572, 'ffn_norm': 3.396}
    for name, (base, spread) in spreads.items():
        noise = np.random.default_rng([zlib.crc32(name.encode()), seed]).standard_normal(out[name].shape)
        drawn = base * np.exp(spread * noise) if base else spread * noise
        out[name] = __import__('jax').numpy.asarray(drawn.astype(out[name].dtype))
    for name, factor in factors.items():
        out[name] = (out[name] * factor).astype(out[name].dtype)
    return out
```

```python
from contextlib import ExitStack

import numpy as np

import concourse.bass as bass
from concourse import mybir

F32 = mybir.dt.float32
I32 = mybir.dt.int32
ALU = mybir.AluOpType
ACT = mybir.ActivationFunctionType
AX = mybir.AxisListType

P = 128
D = 1024
DK = D // P
META = 16
FRAMES = 256
L = META + FRAMES
CHUNK = 64
EPS = 1e-6
HEADS = 4
QR, KVR = 256, 128
ROPE = 64
SCALE = (P + ROPE) ** -0.5
DFF = 3584
EXPERTS = 8
CAP = 96
BIG = 1e30

UNIT = 2048
SLOTS = 14
UQ_COLS, UKV_COLS = 1536, 1024
DECAY, MASK = 384, 416
T1_COLS, T2_COLS = HEADS * DECAY + MASK, HEADS * L
ATTN_UNITS = 18
CHUNKS = DFF // 256
FFN_UNITS = 3 * CHUNKS
DENSE_AT = ATTN_UNITS
ATTN1_AT = ATTN_UNITS + FFN_UNITS
MOE_AT = 2 * ATTN_UNITS + FFN_UNITS
N_UNITS = MOE_AT + EXPERTS * FFN_UNITS
U_UQ, U_UKV, U_RV, U_RG, U_T1, U_T2, U_WO = 6, 7, 8, 10, 12, 13, 14

G_ATTN, G_FFN, G_RET, G_MLA, G_Q, G_KV, G_COLS = 0, 16, 32, 40, 48, 52, 54
C_COS, C_SIN, C_COS64, C_SIN64 = 0, L, 2 * L, 3 * L
C_ID = 4 * L
C_ONES, C_TRI, C_SW, C_SW64, C_IOTA = C_ID + P, C_ID + 2 * P, C_ID + 3 * P, C_ID + 4 * P, C_ID + 5 * P
C_LOW = C_IOTA + CAP
C_COLS = C_LOW + EXPERTS * EXPERTS

TILES = [(META, P), (META + P, P), (0, META)]

OUTS = (["ckv", "kpe", "cq0", "cq1", "q0", "sckv", "scq", "q1", "q2", "q3", "k0", "k1", "k2", "k3",
         "qpe0", "qpe1", "qn0", "qn1", "qn2", "qn3", "kn0", "kn1", "kn2", "kn3", "v0", "v1", "v2",
         "rv0", "rv1", "rv2", "g0", "g1", "g2", "g3", "yM0", "yM1", "yM2", "yM3", "sM0", "sM1", "yR0",
         "sM2", "sM3", "yR1", "yR2", "sR0", "sR1", "yR3", "sR2", "sR3"])
N_OUTS = len(OUTS)
ROPES = ["kpe", "q0", "q1", "q2", "q3", "k0", "k1", "k2", "k3", "qpe0", "qpe1"]
N_ROPES = len(ROPES)


def ffn_order():
    order = [("g", 0), ("u", 0)]
    for c in range(1, CHUNKS):
        order += [("g", c), ("u", c), ("d", c - 1)]
    return order + [("d", CHUNKS - 1)]


FFN_ORDER = ffn_order()
FFN_POS = {key: n for n, key in enumerate(FFN_ORDER)}


def build(nc, stream, h0, gains, router_w, fnorm, consts, out):
    with ExitStack() as ctx:
        def sb(name, shape, dt=F32):
            return ctx.enter_context(nc.sbuf_tensor(name, shape, dt))

        def sem(name):
            return ctx.enter_context(nc.semaphore(name))

        ring = sb("ring", [P, SLOTS, UNIT])
        hT = sb("hT", [P, DK, L])
        hn = sb("hn", [P, DK, L])
        mix = hn
        sq = sb("sq", [P, 8 * L])
        sq3 = sq[:, :].rearrange("p (k t) -> p k t", k=8)
        scratch = sb("scratch", [P, 13860])
        g_sb = sb("g_sb", [P, G_COLS])
        c_sb = sb("c_sb", [P, C_COLS])
        rw_sb = sb("rw_sb", [P, DK, EXPERTS])
        eps_sb = sb("eps_sb", [P, 1])
        nmx = sb("nmx", [P, HEADS, 3])
        sums = sb("sums", [P, HEADS, 3])
        rounds_sb = sb("rounds_sb", [P, 1], I32)
        fn_sb = sb("fn_sb", [P, D])

        at = [0]

        def carve(n):
            a = scratch[:, at[0]:at[0] + n]
            at[0] += n
            assert at[0] <= 13860, at[0]
            return a

        def carve3(a, b):
            return carve(a * b).rearrange("p (a b) -> p a b", a=a)

        qT, kT, rg = carve3(HEADS, L), carve3(HEADS, L), carve3(HEADS, L)
        qn, kn = carve3(HEADS, L), carve3(HEADS, L)
        rv, vm = carve3(3, 512), carve3(3, 512)
        qpe, kpe, ckv, cq = carve3(2, L), carve(L), carve(L), carve3(2, L)
        raw = carve3(3, L)
        rot = carve(L)
        std = carve3(HEADS, L)
        STx, STy = carve3(2, DECAY), carve3(2, L)

        at[0] = 0
        a_dense = [carve3(2, L), carve3(2, L)]
        sil_dense = carve3(2, L)
        at[0] = 0
        acc = carve3(2, D)
        hn_tok = carve3(2, D)
        xg = carve3(DK, CAP)
        a_moe = [carve3(2, CAP), carve3(2, CAP)]
        sil_moe = [carve3(2, CAP), carve3(2, CAP)]
        yT = carve3(DK, CAP)
        ye = carve(D)
        G, GW = carve3(2, CAP), carve3(2, CAP)
        GWT = carve(FRAMES)
        route = carve3(EXPERTS + 1, 4)
        cur, nxt = carve(4), carve(4)
        logit, sel, pos, gate = carve3(2, EXPERTS), carve3(2, EXPERTS), carve3(2, EXPERTS), carve3(2, EXPERTS)
        cmp_a, cmp_b = carve3(2 * EXPERTS, EXPERTS), carve3(2 * EXPERTS, EXPERTS)
        rank = carve3(2, EXPERTS)
        oh1, oh2 = carve3(2, EXPERTS), carve3(2, EXPERTS)
        v12 = carve3(2, 4)
        cnt = carve(4)
        fin = carve3(2, 2)
        res = carve3(2, D)

        bank = [ctx.enter_context(nc.psum_tensor(f"bank{i}", [P, 512], F32)) for i in range(8)]

        slot_in = [sem(f"slot_in{i}") for i in range(SLOTS)]
        units_used = sem("units_used")
        const_in, x_in, fn_in, out_stored = sem("const_in"), sem("x_in"), sem("fn_in"), sem("out_stored")
        round_shifted = sem("round_shifted")
        ones_set = sem("ones_set")
        sq_ready, ms_done, std_ready, hn_ready, h_added = (
            sem("sq_ready"), sem("ms_done"), sem("std_ready"), sem("hn_ready"), sem("h_added"))
        out_done, out_free = sem("out_done"), sem("out_free")
        swap_done, swap_read, rope_done = sem("swap_done"), sem("swap_read"), sem("rope_done")
        c_ready = sem("c_ready")
        sc_done, sc_free, p1_ready, exp_done, p2_ready = (
            sem("sc_done"), sem("sc_free"), sem("p1_ready"), sem("exp_done"), sem("p2_ready"))
        pt_done, pt_free, rs_done, decayed = sem("pt_done"), sem("pt_free"), sem("rs_done"), sem("decayed")
        silu_g, mix_ready, wo_done = sem("silu_g"), sem("mix_ready"), sem("wo_done")
        gu_done, silu_done, a_ready, d_done = sem("gu_done"), sem("silu_done"), sem("a_ready"), sem("d_done")
        link_sem = sem("vector_link")
        lg_done, sel_ready, pos_done = sem("lg_done"), sem("sel_ready"), sem("pos_done")
        gexp_in, gexp_out = sem("gexp_in"), sem("gexp_out")
        tok_done, tok_free = sem("tok_done"), sem("tok_free")
        rounds_ready = sem("rounds_ready")
        e_gu, e_silu, e_a = sem("e_gu"), sem("e_silu"), sem("e_a")
        y_evac, yt_done, ye_ready, sc_out, acc_added = (
            sem("y_evac"), sem("yt_done"), sem("ye_ready"), sem("sc_out"), sem("acc_added"))
        gwt_in, gwt_done, gwt_ready, g_ready, gt_done, xg_ready = (
            sem("gw_ready"), sem("gwt_done"), sem("gwt_ready"), sem("g_ready"), sem("gt_done"), sem("xg_ready"))
        e_link = sem("expert_link")
        fsq, fstd, res_ready = sem("final_squares"), sem("final_std"), sem("res_ready")

        def col(c, n=P):
            return c_sb[:, c:c + n]

        ident, ones, tri = col(C_ID), col(C_ONES), col(C_TRI)

        def gain(c):
            return g_sb[:, c:c + 1]

        def slot(unit):
            return ring[:, unit % SLOTS, :]

        def arrived(eng, unit):
            eng.wait_ge(slot_in[unit % SLOTS], 16 * (unit // SLOTS + 1))

        def base_of(layer):
            return 0 if layer == 0 else ATTN1_AT

        def o_(name, layer):
            return layer * N_OUTS + OUTS.index(name)

        def norm_bank(n):
            return bank[0 if n == 2 else 7]

        def p_of(h):
            return sq[:, h * 2 * L:h * 2 * L + MASK + META]

        used_cols = {U_UQ: UQ_COLS, U_UKV: UKV_COLS, U_T1: T1_COLS, U_T2: T2_COLS}

        block = ctx.enter_context(nc.Block())

        @block.sync
        def _(sp):
            def load(n, cols=UNIT):
                if n >= SLOTS:
                    sp.wait_ge(units_used, n - SLOTS + 1)
                sp.dma_start(ring[:, n % SLOTS, 0:cols], stream[n, :, 0:cols]).then_inc(slot_in[n % SLOTS], 16)

            sp.dma_start(hT[:, :, :], h0).then_inc(x_in, 16)
            sp.dma_start(c_sb[:, :], consts).then_inc(const_in, 16)
            sp.dma_start(g_sb[:, :], gains).then_inc(const_in, 16)
            sp.dma_start(rw_sb[:, :, :], router_w).then_inc(const_in, 16)
            sp.dma_start(fn_sb[:, :], fnorm).then_inc(fn_in, 16)
            for n in range(MOE_AT):
                b = n - ATTN1_AT if n >= ATTN1_AT else n
                load(n, used_cols.get(b, UNIT) if b < ATTN_UNITS else UNIT)

            def load_round(r):
                with sp.Fori(0, EXPERTS) as e:
                    it = r * EXPERTS + e
                    for m in range(FFN_UNITS):
                        s = (MOE_AT + m) % SLOTS
                        sp.wait_ge(units_used, it * FFN_UNITS + (MOE_AT + m - SLOTS + 1))
                        sp.dma_start(ring[:, s, :], stream[e * FFN_UNITS + (MOE_AT + m), :, :]).then_inc(slot_in[s], 16)

            load_round(0)
            sp.wait_ge(rounds_ready, 1)
            rounds = sp.value_load(rounds_sb[0:1, 0:1], min_val=1, max_val=3)
            with sp.If(rounds > 1):
                with sp.Fori(1, rounds) as r:
                    load_round(r)
            with sp.Else():
                sp.nop()
            for j in range(2):
                sp.wait_ge(res_ready, j + 1)
                sp.dma_start(out[j * P:(j + 1) * P, :], res[:, j, :]).then_inc(out_stored, 16)
            sp.wait_ge(out_stored, 32)

        @block.gpsimd
        def _(pool):
            nc.gpsimd.memset(eps_sb[:], EPS).then_inc(ones_set, 1)
            nc.gpsimd.memset(nmx[:], 0.0).then_inc(ones_set, 1)
            nc.gpsimd.memset(sums[:], 1.0).then_inc(ones_set, 1)

        @block.tensor
        def _(pe):
            pending = [0]

            def mm(dst, lhsT, rhs, start, stop, inc=None, by=1, loose=False):
                i = nc.tensor.matmul(dst, lhsT, rhs, start=start, stop=stop, skip_group_check=loose)
                if inc is not None:
                    i.then_inc(inc, by)
                elif pending[0]:
                    i.then_inc(units_used, pending[0])
                    pending[0] = 0
                return i

            def norm(n):
                for k in range(DK):
                    if k % 4 == 0:
                        pe.wait_ge(sq_ready, 2 * n + k // 4 + 1)
                    mm(norm_bank(n)[:, 0:L], ones, sq3[:, k, :], k == 0, k == DK - 1, ms_done if k == DK - 1 else None)

            def attention(layer):
                u0 = base_of(layer)

                def rot_bank(name, cols=L):
                    o = o_(name, layer)
                    if o >= 4:
                        pe.wait_ge(out_free, o - 3)
                    return bank[o % 4][:, 0:cols]

                def proj(name, unit, half, first=False):
                    dst = rot_bank(name)
                    arrived(pe, u0 + unit)
                    w = slot(u0 + unit).rearrange("p (k c) -> p k c", k=DK)
                    for k in range(DK):
                        if first:
                            pe.wait_ge(hn_ready, 16 * layer + k + 1)
                        mm(dst, w[:, k, half * P:(half + 1) * P], hn[:, k, :], k == 0, k == DK - 1,
                           out_done if k == DK - 1 else None)
                    if half:
                        pending[0] += 1

                def swap(r):
                    pe.wait_ge(out_free, o_(ROPES[r], layer) + 1)
                    if r >= 2:
                        pe.wait_ge(swap_read, layer * N_ROPES + r - 1)
                    m = col(C_SW64) if "pe" in ROPES[r] else col(C_SW)
                    mm(bank[4 + r % 2][:, 0:L], m, raw[:, r % 3, :], True, True, swap_done)

                def ones_sum(name, srcs):
                    dst = rot_bank(name)
                    for i, s in enumerate(srcs):
                        mm(dst, ones, s, i == 0, i == len(srcs) - 1, out_done if i == len(srcs) - 1 else None)

                def up_q(name, tile):
                    dst = rot_bank(name)
                    if tile == 0:
                        arrived(pe, u0 + U_UQ)
                        pe.wait_ge(c_ready, 3 * layer + 3)
                    w = slot(u0 + U_UQ)[:, 0:UQ_COLS].rearrange("p (k c) -> p k c", k=2)
                    for k in range(2):
                        mm(dst, w[:, k, tile * P:(tile + 1) * P], cq[:, k, :], k == 0, k == 1, out_done if k else None)

                def tok_rows(src, t):
                    p0, n = TILES[t]
                    return src[:, p0:p0 + n]

                def v_rows(dst, t):
                    return dst[0:TILES[t][1], :]

                def latent_scores(h):
                    dst = bank[6 + h % 2]
                    if h >= 2:
                        pe.wait_ge(sc_free, HEADS * layer + h - 1)
                    if h == 0:
                        pe.wait_ge(rope_done, N_ROPES * (layer + 1))
                        pe.wait_ge(out_free, o_("kn3", layer) + 1)
                    lo = 64 * (h % 2)
                    for t, (c0, n) in enumerate([(0, META + P), (META + P, L), (MASK, META)]):
                        rows = TILES[t][1]
                        d = dst[0:rows, c0:c0 + n]
                        mm(d, tok_rows(qn[:, h, :], t), kn[:, h, 0:n], True, False)
                        mm(d, tok_rows(qpe[lo:lo + 64, h // 2, :], t), kpe[lo:lo + 64, 0:n], False, True,
                           sc_done if t == 2 else None)

                def pair(u):
                    if u == 0:
                        pe.wait_ge(swap_read, N_ROPES * (layer + 1))
                    elif u == 1:
                        pe.wait_ge(sc_free, HEADS * (layer + 1))
                    elif u < 6:
                        pe.wait_ge(pt_free, HEADS * layer + u - 1)
                    else:
                        pe.wait_ge(decayed, HEADS * layer + u - 5)
                    return bank[4 + 2 * (u % 2)], bank[5 + 2 * (u % 2)]

                def prob_transposes(h):
                    x, y = pair(h)
                    pe.wait_ge(p2_ready, HEADS * layer + h + 1)
                    p = p_of(h)
                    a, b, m = p[:, 0:META + P], p[:, META + P:MASK], p[0:META, MASK:MASK + META]
                    nc.tensor.transpose(x[:, 0:P], a[:, META:META + P], ident)
                    nc.tensor.transpose(x[:, P:2 * P], b[:, META:META + P], ident)
                    nc.tensor.transpose(x[:, 2 * P:3 * P], b[:, META + P:L], ident)
                    nc.tensor.transpose(y[0:META, 0:META], m, ident[0:META, 0:META])
                    nc.tensor.transpose(y[0:META, META:META + P], a[:, 0:META], ident)
                    nc.tensor.transpose(y[0:META, META + P:L], b[:, 0:META], ident).then_inc(pt_done, 1)

                def retention_scores(h):
                    x, y = pair(HEADS + h)
                    mm(x[:, 0:2 * P], kT[:, h, META:META + P], qT[:, h, META:L], True, True)
                    mm(x[:, 2 * P:3 * P], kT[:, h, META + P:L], qT[:, h, META + P:L], True, True)
                    mm(y[0:META, 0:L], kT[:, h, 0:META], qT[:, h, :], True, True, rs_done)

                def weigh(name, u, vals):
                    h = u % HEADS
                    dst = rot_bank(name)
                    if u < HEADS:
                        pe.wait_ge(pt_free, HEADS * layer + h + 1)
                    else:
                        pe.wait_ge(decayed, HEADS * layer + h + 1)
                    if u == 0:
                        pe.wait_ge(out_free, o_("rv2", layer) + 1)
                    if u == 2 * HEADS - 1:
                        pending[0] += 2
                    c = slice(h * P, (h + 1) * P)
                    s = u % 2
                    mm(dst, vals[0:META, 2, c], STy[0:META, s, :], True, False)
                    mm(dst[:, META:L], vals[:, 0, c], STx[:, s, 0:2 * P], False, False)
                    mm(dst[:, META + P:L], vals[:, 1, c], STx[:, s, 2 * P:3 * P], False, True, out_done)

                proj("ckv", 0, 0, first=True)
                proj("kpe", 0, 1)
                proj("cq0", 1, 0)
                swap(0)
                proj("cq1", 1, 1)
                proj("q0", 2, 0)
                pe.wait_ge(out_free, o_("cq1", layer) + 1)
                ones_sum("sckv", [sq3[:, 0, :]])
                ones_sum("scq", [sq3[:, 1, :], sq3[:, 2, :]])
                for r, name in enumerate(ROPES[2:9], start=1):
                    proj(name, 2 + r // 2, r % 2)
                    swap(r)
                up_q("qpe0", 0)
                swap(8)
                up_q("qpe1", 1)
                swap(9)
                for h in range(HEADS):
                    up_q(f"qn{h}", 2 + h)
                    if h == 0:
                        swap(10)
                pending[0] += 1
                arrived(pe, u0 + U_UKV)
                w = slot(u0 + U_UKV)
                for h in range(HEADS):
                    dst = rot_bank(f"kn{h}")
                    mm(dst, w[:, h * P:(h + 1) * P], ckv, True, True, out_done)
                for t in range(3):
                    dst = v_rows(rot_bank(f"v{t}", 512), t)
                    mm(dst, tok_rows(ckv, t), w[:, 512:1024], True, True, out_done)
                pending[0] += 1
                latent_scores(0)
                latent_scores(1)
                for t in range(3):
                    dst = v_rows(rot_bank(f"rv{t}", 512), t)
                    for k in range(DK):
                        unit = u0 + U_RV + k // 4
                        if t == 0 and k % 4 == 0:
                            arrived(pe, unit)
                        w = slot(unit).rearrange("p (k c) -> p k c", k=4)
                        mm(dst, tok_rows(hn[:, k, :], t), w[:, k % 4, :], k == 0, k == DK - 1,
                           out_done if k == DK - 1 else None)
                    if t < 2:
                        latent_scores(2 + t)
                pending[0] += 2
                for h in range(HEADS):
                    proj(f"g{h}", U_RG + h // 2, h % 2)
                prob_transposes(0)
                prob_transposes(1)
                weigh("yM0", 0, vm)
                prob_transposes(2)
                weigh("yM1", 1, vm)
                prob_transposes(3)
                weigh("yM2", 2, vm)
                retention_scores(0)
                weigh("yM3", 3, vm)
                retention_scores(1)

                def head_sum(name, src, of):
                    pe.wait_ge(out_free, o_(of, layer) + 1)
                    ones_sum(name, [src])

                head_sum("sM0", sq3[:, 0, :], "yM0")
                head_sum("sM1", sq3[:, 2, :], "yM1")
                weigh("yR0", 4, rv)
                retention_scores(2)
                head_sum("sM2", sq3[:, 4, :], "yM2")
                head_sum("sM3", sq3[:, 6, :], "yM3")
                weigh("yR1", 5, rv)
                retention_scores(3)
                weigh("yR2", 6, rv)
                head_sum("sR0", sq3[:, 1, :], "yR0")
                head_sum("sR1", sq3[:, 3, :], "yR1")
                weigh("yR3", 7, rv)
                head_sum("sR2", sq3[:, 5, :], "yR2")
                head_sum("sR3", sq3[:, 7, :], "yR3")

                pe.wait_ge(out_free, (layer + 1) * N_OUTS)
                added = 0 if layer == 0 else 8 + 8 * CHUNKS

                def wo(d, ks, last):
                    w = slot(u0 + U_WO + d // 2).rearrange("p (k c) -> p k c", k=DK)
                    for k in ks:
                        end = last and k == ks[-1]
                        mm(bank[d % 4][:, 0:L], w[:, k, (d % 2) * P:(d % 2 + 1) * P], mix[:, k, :], k == 4, end,
                           wo_done if end else None)

                pe.wait_ge(mix_ready, 8 * layer + 4)
                for d in range(4):
                    if d % 2 == 0:
                        arrived(pe, u0 + U_WO + d // 2)
                    wo(d, [4, 5, 6, 7], False)
                pe.wait_ge(mix_ready, 8 * layer + 8)
                for d in range(4):
                    wo(d, [0, 1, 2, 3], True)
                    if d % 2:
                        pending[0] += 1
                for d in range(4, 8):
                    pe.wait_ge(h_added, added + d - 3)
                    if d % 2 == 0:
                        arrived(pe, u0 + U_WO + d // 2)
                    wo(d, [4, 5, 6, 7, 0, 1, 2, 3], True)
                    if d % 2:
                        pending[0] += 1

            def dense():
                def gate_up(c):
                    if c >= 1:
                        pe.wait_ge(a_ready, c)
                    for j, kind in enumerate("gu"):
                        unit = DENSE_AT + FFN_POS[kind, c]
                        arrived(pe, unit)
                        w = slot(unit).rearrange("p (k c) -> p k c", k=DK)
                        for f in range(2):
                            for k in range(DK):
                                if c == 0 and j == 0 and f == 0:
                                    pe.wait_ge(hn_ready, 8 + k + 1)
                                last = f == 1 and k == DK - 1 and j == 1
                                mm(bank[2 * j + f][:, 0:L], w[:, k, f * P:(f + 1) * P], hn[:, k, :],
                                   k == 0, k == DK - 1, gu_done if last else None)
                        pending[0] += 1

                def down(c):
                    unit = DENSE_AT + FFN_POS["d", c]
                    arrived(pe, unit)
                    pe.wait_ge(a_ready, c + 1)
                    w = slot(unit).rearrange("p (f n) -> p f n", f=2)
                    for d in range(DK):
                        if c or d >= 4:
                            pe.wait_ge(h_added, 8 + c * DK + d - 3)
                        for f in range(2):
                            mm(bank[4 + d % 4][:, 0:L], w[:, f, d * P:(d + 1) * P], a_dense[c % 2][:, f, :],
                               f == 0, f == 1, d_done if f == 1 else None)
                    pending[0] += 1

                gate_up(0)
                for c in range(1, CHUNKS):
                    gate_up(c)
                    down(c - 1)
                down(CHUNKS - 1)

            def routing():
                for t in range(2):
                    p0 = TILES[t][0]
                    for k in range(DK):
                        if t == 0:
                            pe.wait_ge(hn_ready, 24 + k + 1)
                        mm(bank[0][:, t * EXPERTS:(t + 1) * EXPERTS], hn[:, k, p0:p0 + P], rw_sb[:, k, :],
                           k == 0, k == DK - 1, lg_done if t == 1 and k == DK - 1 else None)
                for src, half, t in [(s, h, t) for s in (0, 1) for t in range(2) for h in range(2)]:
                    n = src * 4 + t * 2 + half
                    if n >= 2:
                        pe.wait_ge(tok_free, n - 1)
                    p0 = TILES[t][0]
                    for i in range(4):
                        k = half * 4 + i
                        x = nc.tensor.transpose(bank[4 + n % 2][:, i * P:(i + 1) * P],
                                                (hT, hn)[src][:, k, p0:p0 + P], ident)
                    x.then_inc(tok_done, 1)
                pe.wait_ge(sel_ready, 1)
                b = bank[1]
                mm(b[:, 0:8], tri, sel[:, 0, :], True, True)
                mm(b[:, 8:16], ones, sel[:, 0, :], True, False)
                mm(b[:, 8:16], tri, sel[:, 1, :], False, True)
                mm(b[:, 16:24], ones, sel[:, 0, :], True, False)
                mm(b[:, 16:24], ones, sel[:, 1, :], False, True, pos_done)

            def gather(n):
                pe.wait_ge(g_ready, n + 1)
                for d in range(DK):
                    for t in range(2):
                        mm(bank[4 + d // 4][:, (d % 4) * CAP:(d % 4 + 1) * CAP], hn_tok[:, t, d * P:(d + 1) * P],
                           G[:, t, :], t == 0, t == 1, gt_done if d == DK - 1 and t == 1 else None)

            def scatter_turn(it):
                pe.wait_ge(y_evac, it + 1)
                pe.wait_ge(acc_added, it * 4 + 1)
                for d in range(DK):
                    x = nc.tensor.transpose(bank[6 + d // 4][0:CAP, (d % 4) * P:(d % 4 + 1) * P], yT[:, d, :], ident)
                x.then_inc(yt_done, 1)

            def scatter_out(it, j):
                t, half = j // 2, j % 2
                if j == 0:
                    pe.wait_ge(ye_ready, it + 1)
                    pe.wait_ge(gwt_ready, it + 1)
                if j >= 2:
                    pe.wait_ge(acc_added, it * 4 + j)
                mm(bank[6 + half][:, :], GWT[0:CAP, t * P:(t + 1) * P], ye[0:CAP, half * 512:(half + 1) * 512],
                   True, True, sc_out)

            def expert(it):
                def ready(m):
                    pe.wait_ge(slot_in[(MOE_AT + m) % SLOTS],
                               it * (16 * FFN_UNITS // SLOTS) + 16 * ((MOE_AT + m) // SLOTS + 1))
                    return ring[:, (MOE_AT + m) % SLOTS, :]

                def gate_up(c):
                    if c >= 2:
                        pe.wait_ge(e_a, it * CHUNKS + c - 1)
                    for j, kind in enumerate("gu"):
                        w = ready(FFN_POS[kind, c]).rearrange("p (k c) -> p k c", k=DK)
                        for f in range(2):
                            for k in range(DK):
                                last = f == 1 and k == DK - 1 and j == 1
                                s = 2 * j + f
                                mm(bank[c % 2][:, s * CAP:(s + 1) * CAP], w[:, k, f * P:(f + 1) * P], xg[:, k, :],
                                   k == 0, k == DK - 1, e_gu if last else None)
                        pending[0] += 1

                def down(c):
                    w = ready(FFN_POS["d", c]).rearrange("p (f n) -> p f n", f=2)
                    pe.wait_ge(e_a, it * CHUNKS + c + 1)
                    if c == 0:
                        pe.wait_ge(y_evac, it + 1)
                    for f in range(2):
                        for d in range(DK):
                            last = f == 1 and d == DK - 1
                            mm(bank[2 + d // 4][:, (d % 4) * CAP:(d % 4 + 1) * CAP], w[:, f, d * P:(d + 1) * P],
                               a_moe[c % 2][:, f, :], c == 0 and f == 0 and d % 4 == 0,
                               c == CHUNKS - 1 and f == 1, units_used if last else None, loose=True)

                pe.wait_ge(xg_ready, it + 1)
                gate_up(0)
                gate_up(1)
                scatter_turn(it)
                down(0)
                gate_up(2)
                scatter_out(it, 0)
                scatter_out(it, 1)
                down(1)
                gate_up(3)
                scatter_out(it, 2)
                scatter_out(it, 3)
                down(2)
                for c in range(4, CHUNKS):
                    gate_up(c)
                    if c == 8:
                        pe.wait_ge(gwt_in, it + 1)
                        for t in range(2):
                            x = nc.tensor.transpose(bank[4][0:CAP, t * P:(t + 1) * P], GW[:, t, :], ident)
                        x.then_inc(gwt_done, 1)
                    if c == CHUNKS - 1:
                        pe.wait_ge(gwt_ready, it + 2)
                        gather(it + 1)
                    down(c - 1)
                down(CHUNKS - 1)

            pe.wait_ge(const_in, 48)
            norm(0)
            attention(0)
            norm(1)
            dense()
            norm(2)
            attention(1)
            norm(3)
            routing()
            gather(0)
            pe.wait_ge(rounds_ready, 1)
            rounds = pe.value_load(rounds_sb[0:1, 0:1], min_val=1, max_val=3)
            with pe.Fori(0, rounds) as r:
                with pe.Fori(0, EXPERTS) as e:
                    expert(r * EXPERTS + e)
            assert pending[0] == 0
            its = rounds * EXPERTS
            scatter_turn(its)
            for j in range(4):
                scatter_out(its, j)

        @block.scalar
        def _(act):
            A = nc.scalar.activation

            def norm(n):
                for half in range(2):
                    if n == 0:
                        act.wait_ge(x_in, 16)
                    else:
                        total = [0, 8, 8 + 8 * CHUNKS, 16 + 8 * CHUNKS][n]
                        act.wait_ge(h_added, total - 4 + 4 * half)
                    A(sq3[:, 4 * half:4 * half + 4, :], hT[:, 4 * half:4 * half + 4, :], ACT.Square).then_inc(sq_ready, 1)
                act.wait_ge(ms_done, n + 1)
                act.wait_ge(ones_set, 3)
                A(std[:, 0, :], norm_bank(n)[:, 0:L], ACT.Sqrt, bias=eps_sb[:, 0:1], scale=1.0 / D).then_inc(std_ready, 1)

            def attention(layer):
                def src(name, rows=P, cols=L):
                    o = o_(name, layer)
                    act.wait_ge(out_done, o + 1)
                    return bank[o % 4][0:rows, 0:cols]

                def keep(name, dst, rows=P, cols=L):
                    A(dst, src(name, rows, cols), ACT.Copy).then_inc(out_free, 1)

                def keep_square(name, dst, sq_dst):
                    s = src(name)
                    A(dst, s, ACT.Copy)
                    A(sq_dst, s, ACT.Square).then_inc(out_free, 1)

                def root(name, dst, n):
                    A(dst, src(name), ACT.Sqrt, bias=eps_sb[:, 0:1], scale=1.0 / n).then_inc(out_free, 1)

                def keep_raw(name):
                    r = ROPES.index(name)
                    if r >= 3:
                        act.wait_ge(rope_done, layer * N_ROPES + r - 2)
                    keep(name, raw[:, r % 3, :])

                def exps(h):
                    act.wait_ge(p1_ready, HEADS * layer + h + 1)
                    p = p_of(h)
                    for t, (rows, c0, c1) in enumerate([(P, 0, META + P), (P, META + P, MASK), (META, MASK, MASK + META)]):
                        x = A(p[0:rows, c0:c1], p[0:rows, c0:c1], ACT.Exp, bias=nmx[0:rows, h, t:t + 1], scale=SCALE,
                              accum_out=sums[0:rows, h, t:t + 1])
                    x.then_inc(exp_done, 1)

                def tables(h):
                    act.wait_ge(pt_done, HEADS * layer + h + 1)
                    x, y = bank[4 + 2 * (h % 2)], bank[5 + 2 * (h % 2)]
                    A(STx[:, h % 2, :], x[:, 0:3 * P], ACT.Copy)
                    A(STy[0:META, h % 2, :], y[0:META, 0:L], ACT.Copy).then_inc(pt_free, 1)

                keep_square("ckv", ckv, sq3[:, 0, :])
                keep_raw("kpe")
                keep_square("cq0", cq[:, 0, :], sq3[:, 1, :])
                keep_square("cq1", cq[:, 1, :], sq3[:, 2, :])
                keep_raw("q0")
                root("sckv", std[:, 0, :], KVR)
                root("scq", std[:, 1, :], QR)
                for name in ROPES[2:]:
                    keep_raw(name)
                for h in range(HEADS):
                    keep(f"qn{h}", qn[:, h, :])
                for h in range(HEADS):
                    keep(f"kn{h}", kn[:, h, :])
                for t, (_, rows) in enumerate(TILES):
                    keep(f"v{t}", vm[0:rows, t, :], rows, 512)
                exps(0)
                exps(1)
                for t, (_, rows) in enumerate(TILES):
                    keep(f"rv{t}", rv[0:rows, t, :], rows, 512)
                    if t < 2:
                        exps(2 + t)
                for h in range(HEADS):
                    keep(f"g{h}", rg[:, h, :])
                tables(0)
                tables(1)
                for h in range(HEADS):
                    keep_square(f"yM{h}", mix[:, 4 + h, :], sq3[:, 2 * h, :])
                    if h < 2:
                        tables(h + 2)
                act.wait_ge(out_free, o_("g3", layer) + 1)
                A(rg[:, :, :], rg[:, :, :], ACT.Silu).then_inc(silu_g, 1)
                for name in OUTS[OUTS.index("sM0"):]:
                    h = int(name[2])
                    if name[0] == "y":
                        keep_square(name, mix[:, h, :], sq3[:, 2 * h + 1, :])
                    elif name[1] == "M":
                        root(name, std[:, h, :], P)
                    else:
                        root(name, sq3[:, 2 * h, :], P)

            def dense():
                for c in range(CHUNKS):
                    act.wait_ge(gu_done, c + 1)
                    for f in range(2):
                        x = A(sil_dense[:, f, :], bank[f][:, 0:L], ACT.Silu)
                    x.then_inc(silu_done, 1)

            def turn_copies():
                for n in range(0, 8):
                    src, t, half = n // 4, n // 2 % 2, n % 2
                    act.wait_ge(tok_done, n + 1)
                    A((acc, hn_tok)[src][:, t, half * 512:(half + 1) * 512], bank[4 + n % 2][:, :], ACT.Copy).then_inc(tok_free, 1)

            def scatter_copy(it):
                act.wait_ge(yt_done, it + 1)
                A(ye[0:CAP, 0:512], bank[6][0:CAP, :], ACT.Copy)
                A(ye[0:CAP, 512:1024], bank[7][0:CAP, :], ACT.Copy).then_inc(ye_ready, 1)

            def expert(it):
                for c in range(CHUNKS):
                    act.wait_ge(e_gu, it * CHUNKS + c + 1)
                    A(sil_moe[c % 2], bank[c % 2][:, 0:2 * CAP].rearrange("p (a b) -> p a b", a=2), ACT.Silu).then_inc(e_silu, 1)
                    if c == 1:
                        scatter_copy(it)
                act.wait_ge(units_used, it * FFN_UNITS + (MOE_AT + FFN_UNITS))
                for b in range(2):
                    x = A(yT[:, 4 * b:4 * b + 4, :], bank[2 + b][:, 0:4 * CAP].rearrange("p (a b) -> p a b", a=4), ACT.Copy)
                x.then_inc(y_evac, 1)

            norm(0)
            attention(0)
            norm(1)
            dense()
            norm(2)
            attention(1)
            norm(3)
            turn_copies()
            act.wait_ge(gexp_in, 1)
            A(v12[:, :, 2:3], v12[:, :, 2:3], ACT.Exp).then_inc(gexp_out, 1)
            act.wait_ge(rounds_ready, 1)
            rounds = act.value_load(rounds_sb[0:1, 0:1], min_val=1, max_val=3)
            with act.Fori(0, rounds) as r:
                with act.Fori(0, EXPERTS) as e:
                    expert(r * EXPERTS + e)
            its = rounds * EXPERTS
            scatter_copy(its)
            act.wait_ge(acc_added, its * 4 + 5)
            for t in range(2):
                A(res[:, t, :], acc[:, t, :], ACT.Square, accum_out=fin[:, t, 0:1]).then_inc(fsq, 1)
            act.wait_ge(fsq, 2)
            A(fin[:, :, 1], fin[:, :, 0], ACT.Sqrt, bias=eps_sb[:, 0:1], scale=1.0 / D).then_inc(fstd, 1)

        @block.vector
        def _(dve):
            V = nc.vector
            chain = [0]

            def link(ins):
                chain[0] += 1
                ins.then_inc(link_sem, 1)
                dve.wait_ge(link_sem, chain[0])

            def norm(n):
                dve.wait_ge(std_ready, n + 1)
                link(V.reciprocal(std[:, 0, :], std[:, 0, :]))
                g0 = (G_ATTN if n % 2 == 0 else G_FFN) + DK * (n // 2)
                for k in range(DK):
                    V.scalar_tensor_tensor(out=hn[:, k, :], in0=hT[:, k, :], scalar=gain(g0 + k), in1=std[:, 0, :],
                                           op0=ALU.mult, op1=ALU.mult).then_inc(hn_ready, 1)

            def attention(layer):
                u0 = base_of(layer)

                def rope(r):
                    name = ROPES[r]
                    if name == "kpe":
                        dst = kpe
                    elif name.startswith("qpe"):
                        dst = qpe[:, int(name[3]), :]
                    else:
                        dst = (qT if name[0] == "q" else kT)[:, int(name[1]), :]
                    cos, sin = (C_COS64, C_SIN64) if "pe" in name else (C_COS, C_SIN)
                    dve.wait_ge(out_free, o_(name, layer) + 1)
                    V.tensor_tensor(dst, raw[:, r % 3, :], col(cos, L), ALU.mult).then_inc(link_sem, 1)
                    chain[0] += 1
                    dve.wait_ge(swap_done, layer * N_ROPES + r + 1)
                    if layer or r:
                        dve.wait_ge(rope_done, layer * N_ROPES + r)
                    V.tensor_tensor(rot, bank[4 + r % 2][:, 0:L], col(sin, L), ALU.mult).then_inc(swap_read, 1)
                    dve.wait_ge(link_sem, chain[0])
                    dve.wait_ge(swap_read, layer * N_ROPES + r + 1)
                    V.tensor_tensor(dst, dst, rot, ALU.add).then_inc(rope_done, 1)

                def latent_norm():
                    dve.wait_ge(out_free, o_("scq", layer) + 1)
                    link(V.reciprocal(std[:, 0:2, :], std[:, 0:2, :]))
                    for x, g, s in [(ckv, G_KV + layer, 0), (cq[:, 0, :], G_Q + 2 * layer, 1), (cq[:, 1, :], G_Q + 2 * layer + 1, 1)]:
                        V.scalar_tensor_tensor(out=x, in0=x, scalar=gain(g), in1=std[:, s, :],
                                               op0=ALU.mult, op1=ALU.mult).then_inc(c_ready, 1)

                def mask_max(h):
                    dve.wait_ge(sc_done, HEADS * layer + h + 1)
                    ps, p = bank[6 + h % 2], p_of(h)
                    mask = slot(u0 + U_T1)[:, HEADS * DECAY:HEADS * DECAY + MASK]
                    link(V.tensor_tensor(p[:, 0:MASK], ps[:, 0:MASK], mask, ALU.add))
                    V.tensor_copy(p[0:META, MASK:MASK + META], ps[0:META, MASK:MASK + META]).then_inc(sc_free, 1)
                    dve.wait_ge(sc_free, HEADS * layer + h + 1)
                    for t, (rows, c0, c1) in enumerate([(P, 0, META + P), (P, META + P, MASK), (META, MASK, MASK + META)]):
                        link(V.tensor_reduce(nmx[0:rows, h, t:t + 1], p[0:rows, c0:c1], axis=AX.X, op=ALU.max))
                    V.tensor_scalar(nmx[:, h, :], nmx[:, h, :], -SCALE, None, ALU.mult).then_inc(p1_ready, 1)

                def normalise(h):
                    dve.wait_ge(exp_done, HEADS * layer + h + 1)
                    link(V.reciprocal(sums[:, h, :], sums[:, h, :]))
                    p = p_of(h)
                    for t, (rows, c0, c1) in enumerate([(P, 0, META + P), (P, META + P, MASK), (META, MASK, MASK + META)]):
                        x = V.tensor_scalar(p[0:rows, c0:c1], p[0:rows, c0:c1], sums[0:rows, h, t:t + 1], None, ALU.mult)
                    x.then_inc(p2_ready, 1)

                def decay(h):
                    dve.wait_ge(rs_done, HEADS * layer + h + 1)
                    s = h % 2
                    t1, t2 = slot(u0 + U_T1), slot(u0 + U_T2)
                    V.tensor_tensor(STx[:, s, :], bank[4 + 2 * s][:, 0:3 * P], t1[:, h * DECAY:(h + 1) * DECAY], ALU.mult)
                    V.tensor_tensor(STy[0:META, s, :], bank[5 + 2 * s][0:META, 0:L], t2[0:META, h * L:(h + 1) * L],
                                    ALU.mult).then_inc(decayed, 1)

                rope(0)
                rope(1)
                latent_norm()
                for r in range(2, N_ROPES):
                    rope(r)
                dve.wait_ge(ones_set, 3)
                arrived(dve, u0 + U_T1)
                for h in range(HEADS):
                    mask_max(h)
                for h in range(HEADS):
                    normalise(h)
                arrived(dve, u0 + U_T2)
                decay(0)
                decay(1)
                decay(2)
                dve.wait_ge(out_free, o_("sM3", layer) + 1)
                link(V.reciprocal(std[:, :, :], std[:, :, :]))
                for h in range(HEADS):
                    m = mix[:, 4 + h, :]
                    V.scalar_tensor_tensor(out=m, in0=m, scalar=gain(G_MLA + 4 * layer + h), in1=std[:, h, :],
                                           op0=ALU.mult, op1=ALU.mult).then_inc(mix_ready, 1)
                decay(3)
                dve.wait_ge(silu_g, layer + 1)
                dve.wait_ge(out_free, o_("yR3", layer) + 1)
                for h in range(HEADS):
                    m = mix[:, h, :]
                    x = V.scalar_tensor_tensor(out=m, in0=m, scalar=gain(G_RET + 4 * layer + h), in1=rg[:, h, :],
                                               op0=ALU.mult, op1=ALU.mult)
                dve.wait_ge(out_free, o_("sR3", layer) + 1)
                dev = sq3[:, 0:8:2, :]
                link(x)
                link(V.reciprocal(dev, dev))
                V.tensor_tensor(mix[:, 0:4, :], mix[:, 0:4, :], dev, ALU.mult).then_inc(mix_ready, 4)
                for d in range(DK):
                    dve.wait_ge(wo_done, DK * layer + d + 1)
                    V.tensor_tensor(hT[:, d, :], hT[:, d, :], bank[d % 4][:, 0:L], ALU.add).then_inc(h_added, 1)

            def dense():
                def down(c):
                    for d in range(DK):
                        dve.wait_ge(d_done, c * DK + d + 1)
                        if d == 0:
                            dve.wait_ge(h_added, 8 + c * DK)
                        V.tensor_tensor(hT[:, d, :], hT[:, d, :], bank[4 + d % 4][:, 0:L], ALU.add).then_inc(h_added, 1)

                for c in range(CHUNKS):
                    dve.wait_ge(silu_done, c + 1)
                    for f in range(2):
                        x = V.tensor_tensor(a_dense[c % 2][:, f, :], bank[2 + f][:, 0:L], sil_dense[:, f, :], ALU.mult)
                    x.then_inc(a_ready, 1)
                    if c:
                        down(c - 1)
                down(CHUNKS - 1)

            def routing():
                E = EXPERTS
                dve.wait_ge(lg_done, 1)
                link(V.tensor_copy(logit, bank[0][:, 0:2 * E].rearrange("p (t e) -> p t e", t=2)))
                for t in range(2):
                    la = logit[:, t, :].unsqueeze(1).to_broadcast([P, E, E])
                    lb = logit[:, t, :].unsqueeze(2).to_broadcast([P, E, E])
                    low = col(C_LOW, E * E).rearrange("p (a b) -> p a b", a=E)
                    ca, cb = cmp_a[:, t * E:(t + 1) * E, :], cmp_b[:, t * E:(t + 1) * E, :]
                    V.tensor_tensor(ca, la, lb, ALU.is_gt)
                    link(V.tensor_tensor(cb, la, lb, ALU.is_equal))
                    link(V.tensor_tensor(cb, cb, low, ALU.mult))
                    link(V.tensor_tensor(ca, ca, cb, ALU.add))
                    link(V.tensor_reduce(rank[:, t, :], ca, axis=AX.X, op=ALU.add))
                V.tensor_scalar(sel, rank, 2.0, None, ALU.is_lt).then_inc(sel_ready, 1)
                V.tensor_scalar(oh1, rank, 0.0, None, ALU.is_equal)
                link(V.tensor_scalar(oh2, rank, 1.0, None, ALU.is_equal))
                for i, oh in ((0, oh1), (1, oh2)):
                    link(V.tensor_tensor(gate, oh, logit, ALU.mult))
                    link(V.tensor_reduce(v12[:, :, i:i + 1], gate, axis=AX.X, op=ALU.add))
                V.tensor_tensor(v12[:, :, 2:3], v12[:, :, 1:2], v12[:, :, 0:1], ALU.subtract).then_inc(gexp_in, 1)
                dve.wait_ge(gexp_out, 1)
                link(V.tensor_scalar(v12[:, :, 3:4], v12[:, :, 2:3], 1.0, None, ALU.add))
                link(V.reciprocal(v12[:, :, 3:4], v12[:, :, 3:4]))
                link(V.tensor_tensor(v12[:, :, 2:3], v12[:, :, 2:3], v12[:, :, 3:4], ALU.mult))
                for t in range(2):
                    link(V.tensor_scalar(oh1[:, t, :], oh1[:, t, :], v12[:, t, 3:4], None, ALU.mult))
                    link(V.scalar_tensor_tensor(out=gate[:, t, :], in0=oh2[:, t, :], scalar=v12[:, t, 2:3], in1=oh1[:, t, :],
                                                op0=ALU.mult, op1=ALU.add))
                link(V.tensor_scalar(oh2, sel, -4096.0, 4096.0, ALU.mult, ALU.add))
                dve.wait_ge(pos_done, 1)
                for t in range(2):
                    V.tensor_tensor(route[:, 0:E, t], oh2[:, t, :], bank[1][:, t * E:(t + 1) * E], ALU.add).then_inc(link_sem, 1)
                    V.tensor_copy(route[:, 0:E, 2 + t], gate[:, t, :]).then_inc(link_sem, 1)
                    chain[0] += 2
                link(V.tensor_reduce(cnt[:, 0:1], bank[1][:, 16:24], axis=AX.X, op=ALU.max))
                V.tensor_scalar(route[:, E, 0:2], route[:, 0, 0:2], -float(CAP), None, ALU.add).then_inc(link_sem, 1)
                V.tensor_copy(route[:, E, 2:4], route[:, 0, 2:4]).then_inc(link_sem, 1)
                chain[0] += 2
                V.tensor_scalar(cnt[:, 1:2], cnt[:, 0:1], float(CAP), 1.0, ALU.is_gt, ALU.add)
                link(V.tensor_scalar(cnt[:, 2:3], cnt[:, 0:1], 2.0 * CAP, None, ALU.is_gt))
                V.tensor_tensor(rounds_sb[:, 0:1], cnt[:, 1:2], cnt[:, 2:3], ALU.add).then_inc(rounds_ready, 1)

            def one_hot(lk, entry):
                lk(V.tensor_copy(nxt, entry))
                V.tensor_scalar(G[:, 0, :], col(C_IOTA, CAP), nxt[:, 0:1], None, ALU.is_equal)
                return V.tensor_scalar(G[:, 1, :], col(C_IOTA, CAP), nxt[:, 1:2], None, ALU.is_equal)

            def take(n):
                dve.wait_ge(gt_done, n + 1)
                for b in range(2):
                    x = V.tensor_copy(xg[:, 4 * b:4 * b + 4, :], bank[4 + b][:, 0:4 * CAP].rearrange("p (a b) -> p a b", a=4))
                x.then_inc(xg_ready, 1)

            def add_out(it, j):
                dve.wait_ge(sc_out, it * 4 + j + 1)
                t, half = j // 2, j % 2
                a = acc[:, t, half * 512:(half + 1) * 512]
                V.tensor_tensor(a, a, bank[6 + half][:, :], ALU.add).then_inc(acc_added, 1)

            LINKS = 2

            def expert(it, e):
                n = [0]

                def lk(ins):
                    n[0] += 1
                    ins.then_inc(e_link, 1)
                    dve.wait_ge(e_link, it * LINKS + n[0])

                lk(V.tensor_copy(cur, route[:, e, :]))
                for t in range(2):
                    x = V.tensor_scalar(GW[:, t, :], col(C_IOTA, CAP), cur[:, t:t + 1], cur[:, 2 + t:3 + t], ALU.is_equal, ALU.mult)
                x.then_inc(gwt_in, 1)
                for c in range(CHUNKS):
                    dve.wait_ge(e_silu, it * CHUNKS + c + 1)
                    V.tensor_tensor(a_moe[c % 2], bank[c % 2][:, 2 * CAP:4 * CAP].rearrange("p (a b) -> p a b", a=2),
                                    sil_moe[c % 2], ALU.mult).then_inc(e_a, 1)
                    if c in (2, 3):
                        add_out(it, 2 * (c - 2))
                        add_out(it, 2 * (c - 2) + 1)
                    if c == 8:
                        dve.wait_ge(gwt_done, it + 1)
                        V.tensor_copy(GWT[0:CAP, :], bank[4][0:CAP, 0:FRAMES]).then_inc(gwt_ready, 1)
                        one_hot(lk, route[:, e + 1, :]).then_inc(g_ready, 1)
                assert n[0] == LINKS
                take(it + 1)

            link(V.memset(rot, 0.0))
            norm(0)
            attention(0)
            norm(1)
            dense()
            norm(2)
            attention(1)
            norm(3)
            routing()
            dve.wait_ge(tok_free, 8)
            V.memset(yT, 0.0).then_inc(y_evac, 1)
            V.memset(GWT[0:CAP, :], 0.0).then_inc(gwt_ready, 1)
            V.memset(ye[:, :], 0.0).then_inc(acc_added, 1)
            one_hot(link, route[:, 0, :]).then_inc(g_ready, 1)
            take(0)
            dve.wait_ge(rounds_ready, 1)
            rounds = dve.value_load(rounds_sb[0:1, 0:1], min_val=1, max_val=3)
            with dve.Fori(0, rounds) as r:
                with dve.Fori(0, EXPERTS) as e:
                    expert(r * EXPERTS + e, e)
                V.tensor_scalar(route[:, :, 0:2], route[:, :, 0:2], -float(CAP), None, ALU.add).then_inc(round_shifted, 1)
                dve.wait_ge(round_shifted, r + 1)
            its = rounds * EXPERTS
            for j in range(4):
                add_out(its, j)
            dve.wait_ge(fstd, 1)
            link(V.reciprocal(fin[:, :, 1], fin[:, :, 1]))
            dve.wait_ge(fn_in, 16)
            for t in range(2):
                V.scalar_tensor_tensor(out=res[:, t, :], in0=acc[:, t, :], scalar=fin[:, t, 1:2], in1=fn_sb[:, :],
                                       op0=ALU.mult, op1=ALU.mult).then_inc(res_ready, 1)


def _tables():
    f = np.float32
    pos = np.arange(L, dtype=f)

    def angles(dim):
        inv = f(10000.0) ** (-np.arange(0, dim, 2, dtype=f) / f(dim))
        ang = (pos[:, None] * inv[None, :]).astype(f)
        return np.cos(ang).astype(f).T, np.sin(ang).astype(f).T

    c = np.zeros((P, C_COLS), f)
    cos, sin = angles(P)
    c[:, C_COS:C_COS + L], c[:, C_SIN:C_SIN + L] = np.tile(cos, (2, 1)), np.tile(sin, (2, 1))
    cos, sin = angles(ROPE)
    c[:, C_COS64:C_COS64 + L], c[:, C_SIN64:C_SIN64 + L] = np.tile(cos, (4, 1)), np.tile(sin, (4, 1))
    c[:, C_ID:C_ID + P] = np.eye(P)
    c[:, C_ONES:C_ONES + P] = 1.0
    c[:, C_TRI:C_TRI + P] = np.triu(np.ones((P, P)), 1)

    def swap(half):
        m = np.zeros((P, P), f)
        for b in range(0, P, 2 * half):
            for i in range(half):
                m[b + half + i, b + i] = -1.0
                m[b + i, b + half + i] = 1.0
        return m

    c[:, C_SW:C_SW + P], c[:, C_SW64:C_SW64 + P] = swap(P // 2), swap(ROPE // 2)
    c[:, C_IOTA:C_IOTA + CAP] = np.arange(CAP)
    c[:, C_LOW:] = np.tril(np.ones((EXPERTS, EXPERTS)), -1).ravel()

    gamma = np.log1p(-np.exp2(-5.0 - np.arange(HEADS, dtype=np.float64)))
    t1, t2 = np.zeros((P, T1_COLS), f), np.zeros((P, T2_COLS), f)
    j = np.arange(P)
    i = np.arange(2 * P)
    allowed = i[None, :] // CHUNK >= j[:, None] // CHUNK
    for h in range(HEADS):
        w = np.exp(gamma[h] * np.abs(i[None, :] - j[:, None])) * allowed * P ** -0.5
        t1[:, h * DECAY:h * DECAY + 2 * P] = w
        t1[:, h * DECAY + 2 * P:(h + 1) * DECAY] = w[:, :P]
        a = np.arange(L)
        t2[:META, h * L:(h + 1) * L] = np.exp(gamma[h] * np.abs(a[None, :] - np.arange(META)[:, None])) * P ** -0.5
    block = np.where(j[:, None] // CHUNK >= j[None, :] // CHUNK, 0.0, -BIG)
    m = t1[:, HEADS * DECAY:]
    m[:, META:META + P] = block
    m[:, META + P + META + P:] = block
    return c, t1, t2


def kernel(**inputs):
    import numpy as _np
    import concourse.bacc as _bacc
    from concourse import mybir as _mybir
    from concourse.bass_utils import run_bass_kernel_spmd as _run

    x = {k: _np.asarray(v) for k, v in inputs.items()}
    consts, t1, t2 = _tables()
    units = _np.zeros((N_UNITS, P, UNIT), _np.float32)

    def cols(w):
        return w.reshape(DK, P, 256).transpose(1, 0, 2).reshape(P, UNIT)

    for layer in range(2):
        at = 0 if layer == 0 else ATTN1_AT
        rq, rk, rv, rg, cq, ckv, kr = _np.split(x["w_in"][layer], [512, 1024, 1536, 2048, 2304, 2432], axis=1)
        units[at] = cols(_np.concatenate([ckv, kr, kr], axis=1))
        units[at + 1] = cols(cq)
        for i in range(2):
            units[at + 2 + i] = cols(rq[:, 256 * i:256 * (i + 1)])
            units[at + 4 + i] = cols(rk[:, 256 * i:256 * (i + 1)])
            units[at + U_RV + i] = rv[512 * i:512 * (i + 1)].reshape(4, P, 512).transpose(1, 0, 2).reshape(P, UNIT)
            units[at + U_RG + i] = cols(rg[:, 256 * i:256 * (i + 1)])
        uq = x["w_uq"][layer].reshape(QR, HEADS, P + ROPE)
        uq = _np.concatenate([uq[:, :, P:].reshape(QR, HEADS * ROPE), uq[:, :, :P].reshape(QR, HEADS * P)], axis=1)
        units[at + U_UQ, :, :UQ_COLS] = uq.reshape(2, P, 768).transpose(1, 0, 2).reshape(P, UQ_COLS)
        ukv = x["w_ukv"][layer].reshape(KVR, HEADS, 2, P).transpose(0, 2, 1, 3)
        units[at + U_UKV, :, :UKV_COLS] = ukv.reshape(KVR, UKV_COLS)
        units[at + U_T1, :, :T1_COLS], units[at + U_T2, :, :T2_COLS] = t1, t2
        for i in range(4):
            units[at + U_WO + i] = cols(x["w_out"][layer][:, 256 * i:256 * (i + 1)])

    def ffn(at, gate, up, down):
        for n, (kind, c) in enumerate(FFN_ORDER):
            if kind == "d":
                units[at + n] = down[256 * c:256 * (c + 1)].reshape(2, P, D).transpose(1, 0, 2).reshape(P, UNIT)
            else:
                units[at + n] = cols((gate if kind == "g" else up)[:, 256 * c:256 * (c + 1)])

    ffn(DENSE_AT, x["dense_w_gate"][0], x["dense_w_up"][0], x["dense_w_down"][0])
    for e in range(EXPERTS):
        ffn(MOE_AT + e * FFN_UNITS, x["moe_w_gate"][0, e], x["moe_w_up"][0, e], x["moe_w_down"][0, e])

    def lanes(v):
        return v.reshape(-1, P).T

    gains = _np.concatenate([lanes(x[n]) for n in ("attn_norm", "ffn_norm", "ret_out_gain", "mla_out_gain", "q_norm", "kv_norm")], axis=1)
    h0 = _np.concatenate([x["meta_tokens"], x["x"][0]], axis=0).T.reshape(DK, P, L).transpose(1, 0, 2)
    arrays = {
        "stream": units, "h0": h0, "gains": gains,
        "router_w": x["router_w"][0].reshape(DK, P, EXPERTS).transpose(1, 0, 2),
        "fnorm": _np.broadcast_to(x["final_norm"], (P, D)), "consts": consts,
    }
    arrays = {k: _np.ascontiguousarray(v) for k, v in arrays.items()}
    nc = _bacc.Bacc("TRN2", target_bir_lowering=False, num_devices=1)
    args = [nc.dram_tensor(k, v.shape, _mybir.dt.float32, kind="ExternalInput").ap() for k, v in arrays.items()]
    args.append(nc.dram_tensor("out", (FRAMES, D), _mybir.dt.float32, kind="ExternalOutput").ap())
    build(nc, *args)
    r = _run(nc, [arrays], core_ids=[0])
    return _np.asarray(r.results[0]["out"]).reshape(1, FRAMES, D)
```

```python
from contextlib import ExitStack

import numpy as np

import concourse.bass as bass
from concourse import mybir

F32 = mybir.dt.float32
F32R = mybir.dt.float32r
I32 = mybir.dt.int32
ALU = mybir.AluOpType
ACT = mybir.ActivationFunctionType
AX = mybir.AxisListType

P = 128
D = 1024
DK = D // P
META = 16
FRAMES = 256
L = META + FRAMES
CHUNK = 64
EPS = 1e-6
HEADS = 4
QR, KVR = 256, 128
ROPE = 64
SCALE = (P + ROPE) ** -0.5
DFF = 3584
EXPERTS = 8
CAP = 128
BIG = 1e30

UNIT = 2048
SLOTS = 6
HSLOTS = 3
UQ_COLS, UKV_COLS = 1536, 1024
DECAY, MASK = 384, 416
T1_COLS, T2_COLS = HEADS * DECAY + MASK, HEADS * L
ATTN_UNITS = 18
CHUNKS = DFF // 256
FFN_UNITS = 3 * CHUNKS
DENSE_AT = ATTN_UNITS
ATTN1_AT = ATTN_UNITS + FFN_UNITS
MOE_AT = 2 * ATTN_UNITS + FFN_UNITS
N_UNITS = MOE_AT + EXPERTS * FFN_UNITS
MOE_CHUNKS = DFF // 512
U_UQ, U_UKV, U_RV, U_RG, U_T1, U_T2, U_WO = 6, 7, 8, 10, 12, 13, 14

G_ATTN, G_FFN, G_RET, G_MLA, G_Q, G_KV, G_COLS = 0, 16, 32, 40, 48, 52, 54
C_COS, C_SIN, C_COS64, C_SIN64 = 0, L, 2 * L, 3 * L
C_ID = 4 * L
C_ONES, C_TRI, C_SW, C_SW64, C_IOTA = C_ID + P, C_ID + 2 * P, C_ID + 3 * P, C_ID + 4 * P, C_ID + 5 * P
C_LOW = C_IOTA + CAP
C_COLS = C_LOW + EXPERTS * EXPERTS

TILES = [(META, P), (META + P, P), (0, META)]

OUTS = (["ckv", "kpe", "cq0", "cq1", "q0", "sckv", "scq", "q1", "q2", "q3", "k0", "k1", "k2", "k3",
         "qpe0", "qpe1", "qn0", "qn1", "qn2", "qn3", "kn0", "kn1", "kn2", "kn3", "v0", "v1", "v2",
         "rv0", "rv1", "rv2", "g0", "g1", "g2", "g3", "yM0", "yM1", "yM2", "yM3", "sM0", "sM1", "yR0",
         "sM2", "sM3", "yR1", "yR2", "sR0", "sR1", "yR3", "sR2", "sR3"])
N_OUTS = len(OUTS)
ROPES = ["kpe", "q0", "q1", "q2", "q3", "k0", "k1", "k2", "k3", "qpe0", "qpe1"]
N_ROPES = len(ROPES)


DIRECT = (U_UQ, U_UKV, U_T1, U_T2)


def ffn_order():
    order = [("g", 0), ("u", 0)]
    for c in range(1, CHUNKS):
        order += [("g", c), ("u", c), ("d", c - 1)]
    return order + [("d", CHUNKS - 1)]


def moe_order():
    order = [(kind, 0, i) for kind in "gu" for i in range(2)]
    for c in range(1, MOE_CHUNKS):
        order += [(kind, c, i) for kind in "gu" for i in range(2)] + [("d", c - 1, i) for i in range(2)]
    return order + [("d", MOE_CHUNKS - 1, i) for i in range(2)]


FFN_ORDER = ffn_order()
FFN_POS = {key: n for n, key in enumerate(FFN_ORDER)}
MOE_ORDER = moe_order()


def is_direct(n):
    return (n - (ATTN1_AT if n >= ATTN1_AT else 0)) in DIRECT


SPLIT_OF = {}
DIRECT_OF = {}
for _n in range(MOE_AT):
    _t = DIRECT_OF if is_direct(_n) else SPLIT_OF
    _t[_n] = len(_t)
MOE_SPLIT = len(SPLIT_OF)
UNIT_OF = {v: k for k, v in SPLIT_OF.items()}


def build(nc, stream, h0, gains, router_w, fnorm, consts, out):
    with ExitStack() as ctx:
        def sb(name, shape, dt=F32):
            return ctx.enter_context(nc.sbuf_tensor(name, shape, dt))

        def sem(name):
            return ctx.enter_context(nc.semaphore(name))

        ring = sb("ring", [P, SLOTS, UNIT])
        w_hi = sb("w_hi", [P, HSLOTS, UNIT], F32R)
        w_lo = sb("w_lo", [P, HSLOTS, UNIT], F32R)
        hT = sb("hT", [P, DK, L])
        sq = sb("sq", [P, 8 * L])
        sq3 = sq[:, :].rearrange("p (k t) -> p k t", k=8)
        scratch = sb("scratch", [P, 13700])
        parts = sb("parts", [P, 24 * L], F32R)
        hi = parts[:, 0:8 * L].rearrange("p (k t) -> p k t", k=8)
        lo = parts[:, 8 * L:16 * L].rearrange("p (k t) -> p k t", k=8)
        ad = parts[:, 16 * L:24 * L].rearrange("p (b f t) -> p b f t", b=4, f=2)
        ad_hi, ad_lo = [ad[:, 0], ad[:, 1]], [ad[:, 2], ad[:, 3]]
        x_hi = parts[:, 0:DK * CAP].rearrange("p (k c) -> p k c", k=DK)
        x_lo = parts[:, DK * CAP:2 * DK * CAP].rearrange("p (k c) -> p k c", k=DK)
        ae = parts[:, 2 * DK * CAP:4 * DK * CAP].rearrange("p (b n) -> p b n", b=4)
        ae_hi, ae_lo = [ae[:, 0, :], ae[:, 1, :]], [ae[:, 2, :], ae[:, 3, :]]
        g_sb = sb("g_sb", [P, G_COLS])
        c_sb = sb("c_sb", [P, C_COLS])
        rw_sb = sb("rw_sb", [P, DK, EXPERTS])
        eps_sb = sb("eps_sb", [P, 1])
        nmx = sb("nmx", [P, HEADS, 3])
        sums = sb("sums", [P, HEADS, 3])
        rounds_sb = sb("rounds_sb", [P, 1], I32)
        fn_sb = sb("fn_sb", [P, D])

        at = [0]

        def carve(n):
            a = scratch[:, at[0]:at[0] + n]
            at[0] += n
            assert at[0] <= 13700, at[0]
            return a

        def carve3(a, b):
            return carve(a * b).rearrange("p (a b) -> p a b", a=a)

        qT, kT, rg = carve3(HEADS, L), carve3(HEADS, L), carve3(HEADS, L)
        qn, kn = carve3(HEADS, L), carve3(HEADS, L)
        rv, vm = carve3(3, 512), carve3(3, 512)
        qpe, kpe, ckv, cq = carve3(2, L), carve(L), carve(L), carve3(2, L)
        raw = carve3(3, L)
        rot = carve(L)
        std = carve3(HEADS, L)
        STx, STy = carve3(2, DECAY), carve3(2, L)

        at[0] = 0
        a_dense, sil_dense = carve3(2, L), carve3(2, L)
        at[0] = 0
        acc = carve3(2, D)
        hn_tok = carve3(2, D)
        sil_moe, a_moe = carve(512), carve(512)
        ye = carve(D)
        G, GW = carve3(2, CAP), carve3(2, CAP)
        GWT = carve(FRAMES)
        route = carve3(EXPERTS + 1, 4)
        cur, nxt = carve(4), carve(4)
        logit, sel, pos, gate = carve3(2, EXPERTS), carve3(2, EXPERTS), carve3(2, EXPERTS), carve3(2, EXPERTS)
        cmp_a, cmp_b = carve3(2 * EXPERTS, EXPERTS), carve3(2 * EXPERTS, EXPERTS)
        rank = carve3(2, EXPERTS)
        oh1, oh2 = carve3(2, EXPERTS), carve3(2, EXPERTS)
        v12 = carve3(2, 4)
        cnt = carve(4)
        fin = carve3(2, 2)
        res = carve3(2, D)

        bank = [ctx.enter_context(nc.psum_tensor(f"bank{i}", [P, 512], F32)) for i in range(8)]

        slot_in = [sem(f"slot_in{i}") for i in range(SLOTS)]
        direct_used, split_hi, split_lo, w_used = sem("direct_used"), sem("split_hi"), sem("split_lo"), sem("w_used")
        hnf_ready, hi_ready, af_ready, mixf_ready, mix_hi = (
            sem("hnf_ready"), sem("hi_ready"), sem("af_ready"), sem("mixf_ready"), sem("mix_hi"))
        a_hi_ready = sem("a_hi_ready")
        const_in, x_in, fn_in, out_stored = sem("const_in"), sem("x_in"), sem("fn_in"), sem("out_stored")
        round_shifted = sem("round_shifted")
        ones_set = sem("ones_set")
        sq_ready, ms_done, std_ready, hn_ready, h_added = (
            sem("sq_ready"), sem("ms_done"), sem("std_ready"), sem("hn_ready"), sem("h_added"))
        out_done, out_free = sem("out_done"), sem("out_free")
        swap_done, swap_read, rope_done = sem("swap_done"), sem("swap_read"), sem("rope_done")
        c_ready = sem("c_ready")
        sc_done, sc_free, p1_ready, exp_done, p2_ready = (
            sem("sc_done"), sem("sc_free"), sem("p1_ready"), sem("exp_done"), sem("p2_ready"))
        pt_done, pt_free, rs_done, decayed = sem("pt_done"), sem("pt_free"), sem("rs_done"), sem("decayed")
        silu_g, mix_ready, wo_done = sem("silu_g"), sem("mix_ready"), sem("wo_done")
        gu_done, silu_done, a_ready, d_done = sem("gu_done"), sem("silu_done"), sem("a_ready"), sem("d_done")
        link_sem = sem("vector_link")
        lg_done, sel_ready, pos_done = sem("lg_done"), sem("sel_ready"), sem("pos_done")
        gexp_in, gexp_out = sem("gexp_in"), sem("gexp_out")
        tok_done, tok_free = sem("tok_done"), sem("tok_free")
        rounds_ready = sem("rounds_ready")
        e_gu, e_silu, e_a = sem("e_gu"), sem("e_silu"), sem("e_a")
        e_af, at_done, e_ahi, e_xhi, y_zero = sem("e_af"), sem("at_done"), sem("e_ahi"), sem("e_xhi"), sem("y_zero")
        ye_ready, sc_out, acc_added = sem("ye_ready"), sem("sc_out"), sem("acc_added")
        gwt_in, gwt_done, gwt_ready, g_ready, gt_done, xg_ready = (
            sem("gw_ready"), sem("gwt_done"), sem("gwt_ready"), sem("g_ready"), sem("gt_done"), sem("xg_ready"))
        e_link = sem("expert_link")
        fsq, fstd, res_ready = sem("final_squares"), sem("final_std"), sem("res_ready")

        def col(c, n=P):
            return c_sb[:, c:c + n]

        ident, ones, tri = col(C_ID), col(C_ONES), col(C_TRI)

        def gain(c):
            return g_sb[:, c:c + 1]

        def slot(unit):
            return ring[:, unit % SLOTS, :]

        def arrived(eng, unit):
            eng.wait_ge(slot_in[unit % SLOTS], 16 * (unit // SLOTS + 1))

        def split(eng, unit):
            n = SPLIT_OF[unit]
            eng.wait_ge(split_lo, n + 1)
            return w_hi[:, n % HSLOTS, :], w_lo[:, n % HSLOTS, :]

        def base_of(layer):
            return 0 if layer == 0 else ATTN1_AT

        def o_(name, layer):
            return layer * N_OUTS + OUTS.index(name)

        def norm_bank(n):
            return bank[0 if n == 2 else 7]

        def p_of(h):
            return sq[:, h * 2 * L:h * 2 * L + MASK + META]

        used_cols = {U_UQ: UQ_COLS, U_UKV: UKV_COLS, U_T1: T1_COLS, U_T2: T2_COLS}

        block = ctx.enter_context(nc.Block())

        @block.sync
        def _(sp):
            def load(n, cols=UNIT):
                if n >= SLOTS:
                    old = n - SLOTS
                    if is_direct(old):
                        sp.wait_ge(direct_used, DIRECT_OF[old] + 1)
                    else:
                        sp.wait_ge(split_lo, SPLIT_OF[old] + 1)
                sp.dma_start(ring[:, n % SLOTS, 0:cols], stream[n, :, 0:cols]).then_inc(slot_in[n % SLOTS], 16)

            sp.dma_start(hT[:, :, :], h0).then_inc(x_in, 16)
            for n in range(3):
                load(n)
            sp.dma_start(c_sb[:, :], consts).then_inc(const_in, 16)
            sp.dma_start(g_sb[:, :], gains).then_inc(const_in, 16)
            sp.dma_start(rw_sb[:, :, :], router_w).then_inc(const_in, 16)
            sp.dma_start(fn_sb[:, :], fnorm).then_inc(fn_in, 16)
            for n in range(3, MOE_AT):
                b = n - ATTN1_AT if n >= ATTN1_AT else n
                load(n, used_cols.get(b, UNIT) if b < ATTN_UNITS else UNIT)

            def load_round(r):
                with sp.Fori(0, EXPERTS) as e:
                    it = r * EXPERTS + e
                    for m in range(FFN_UNITS):
                        slot_no = (MOE_AT + m) % SLOTS
                        sp.wait_ge(split_lo, it * FFN_UNITS + (MOE_SPLIT + m - SLOTS + 1))
                        sp.dma_start(ring[:, slot_no, :], stream[e * FFN_UNITS + (MOE_AT + m), :, :]).then_inc(slot_in[slot_no], 16)

            sp.wait_ge(direct_used, len(DIRECT_OF))
            load_round(0)
            sp.wait_ge(rounds_ready, 1)
            rounds = sp.value_load(rounds_sb[0:1, 0:1], min_val=1, max_val=2)
            with sp.If(rounds > 1):
                with sp.Fori(1, rounds) as r:
                    load_round(r)
            with sp.Else():
                sp.nop()
            for j in range(2):
                sp.wait_ge(res_ready, j + 1)
                sp.dma_start(out[j * P:(j + 1) * P, :], res[:, j, :]).then_inc(out_stored, 16)
            sp.wait_ge(out_stored, 32)

        @block.gpsimd
        def _(pool):
            nc.gpsimd.memset(eps_sb[:], EPS).then_inc(ones_set, 1)
            nc.gpsimd.memset(nmx[:], 0.0).then_inc(ones_set, 1)
            nc.gpsimd.memset(sums[:], 1.0).then_inc(ones_set, 1)

        @block.tensor
        def _(pe):
            used_up = []

            def release(i, inc):
                if inc is not None:
                    i.then_inc(inc, 1)
                elif used_up:
                    i.then_inc(*used_up.pop(0))
                return i

            def mm(dst, lhsT, rhs, start, stop, inc=None):
                return release(nc.tensor.matmul(dst, lhsT, rhs, start=start, stop=stop), inc)

            def turn(dst, src, inc=None):
                n = src.shape[0]
                return release(nc.tensor.transpose(dst, src, ident[0:n, 0:n]), inc)

            def mm3(dst, sta, mov, start, stop, inc=None):
                mm(dst, sta[0], mov[0], start, False)
                mm(dst, sta[1], mov[0], False, False)
                mm(dst, sta[0], mov[1], False, stop, inc)

            def norm(n):
                for k in range(DK):
                    if k % 4 == 0:
                        pe.wait_ge(sq_ready, 2 * n + k // 4 + 1)
                    mm(norm_bank(n)[:, 0:L], ones, sq3[:, k, :], k == 0, k == DK - 1, ms_done if k == DK - 1 else None)

            def attention(layer):
                u0 = base_of(layer)

                def rot_bank(name, cols=L):
                    o = o_(name, layer)
                    if o >= 4:
                        pe.wait_ge(out_free, o - 3)
                    return bank[o % 4][:, 0:cols]

                def proj(name, unit, half, first=False):
                    dst = rot_bank(name)
                    w = [x.rearrange("p (k c) -> p k c", k=DK)[:, :, half * P:(half + 1) * P] for x in split(pe, u0 + unit)]
                    for k in range(DK):
                        if first and k % 2 == 0:
                            pe.wait_ge(hn_ready, 4 * layer * 2 + k // 2 + 1)
                        mm3(dst, [x[:, k, :] for x in w], [hi[:, k, :], lo[:, k, :]], k == 0, k == DK - 1,
                            out_done if k == DK - 1 else None)
                    if half:
                        used_up.append((w_used, 1))

                def swap(r):
                    pe.wait_ge(out_free, o_(ROPES[r], layer) + 1)
                    if r >= 2:
                        pe.wait_ge(swap_read, layer * N_ROPES + r - 1)
                    m = col(C_SW64) if "pe" in ROPES[r] else col(C_SW)
                    mm(bank[4 + r % 2][:, 0:L], m, raw[:, r % 3, :], True, True, swap_done)

                def ones_sum(name, srcs):
                    dst = rot_bank(name)
                    for i, x in enumerate(srcs):
                        mm(dst, ones, x, i == 0, i == len(srcs) - 1, out_done if i == len(srcs) - 1 else None)

                def up_q(name, tile):
                    dst = rot_bank(name)
                    if tile == 0:
                        arrived(pe, u0 + U_UQ)
                        pe.wait_ge(c_ready, 3 * layer + 3)
                    w = slot(u0 + U_UQ)[:, 0:UQ_COLS].rearrange("p (k c) -> p k c", k=2)
                    for k in range(2):
                        mm(dst, w[:, k, tile * P:(tile + 1) * P], cq[:, k, :], k == 0, k == 1, out_done if k else None)

                def tok_rows(src, t):
                    p0, n = TILES[t]
                    return src[:, p0:p0 + n]

                def latent_scores(h):
                    dst = bank[6 + h % 2]
                    if h >= 2:
                        pe.wait_ge(sc_free, HEADS * layer + h - 1)
                    if h == 0:
                        pe.wait_ge(rope_done, N_ROPES * (layer + 1))
                        pe.wait_ge(out_free, o_("kn3", layer) + 1)
                    x = 64 * (h % 2)
                    for t, (c0, n) in enumerate([(0, META + P), (META + P, L), (MASK, META)]):
                        d = dst[0:TILES[t][1], c0:c0 + n]
                        mm(d, tok_rows(qn[:, h, :], t), kn[:, h, 0:n], True, False)
                        mm(d, tok_rows(qpe[x:x + 64, h // 2, :], t), kpe[x:x + 64, 0:n], False, True,
                           sc_done if t == 2 else None)

                def pair(u):
                    if u == 0:
                        pe.wait_ge(swap_read, N_ROPES * (layer + 1))
                    elif u == 1:
                        pe.wait_ge(sc_free, HEADS * (layer + 1))
                    elif u < 6:
                        pe.wait_ge(pt_free, HEADS * layer + u - 1)
                    else:
                        pe.wait_ge(decayed, HEADS * layer + u - 5)
                    return bank[4 + 2 * (u % 2)], bank[5 + 2 * (u % 2)]

                def prob_transposes(h):
                    x, y = pair(h)
                    pe.wait_ge(p2_ready, HEADS * layer + h + 1)
                    p = p_of(h)
                    a, b, m = p[:, 0:META + P], p[:, META + P:MASK], p[0:META, MASK:MASK + META]
                    turn(x[:, 0:P], a[:, META:META + P])
                    turn(x[:, P:2 * P], b[:, META:META + P])
                    turn(x[:, 2 * P:3 * P], b[:, META + P:L])
                    turn(y[0:META, 0:META], m)
                    turn(y[0:META, META:META + P], a[:, 0:META])
                    turn(y[0:META, META + P:L], b[:, 0:META], pt_done)

                def retention_scores(h):
                    x, y = pair(HEADS + h)
                    mm(x[:, 0:2 * P], kT[:, h, META:META + P], qT[:, h, META:L], True, True)
                    mm(x[:, 2 * P:3 * P], kT[:, h, META + P:L], qT[:, h, META + P:L], True, True)
                    mm(y[0:META, 0:L], kT[:, h, 0:META], qT[:, h, :], True, True, rs_done)

                def weigh(name, u, vals):
                    h = u % HEADS
                    dst = rot_bank(name)
                    if u < HEADS:
                        pe.wait_ge(pt_free, HEADS * layer + h + 1)
                    else:
                        pe.wait_ge(decayed, HEADS * layer + h + 1)
                    if u == 0:
                        pe.wait_ge(out_free, o_("rv2", layer) + 1)
                    if u == 2 * HEADS - 1:
                        used_up.append((direct_used, 2))
                    c = slice(h * P, (h + 1) * P)
                    b = u % 2
                    mm(dst, vals[0:META, 2, c], STy[0:META, b, :], True, False)
                    mm(dst[:, META:L], vals[:, 0, c], STx[:, b, 0:2 * P], False, False)
                    mm(dst[:, META + P:L], vals[:, 1, c], STx[:, b, 2 * P:3 * P], False, True, out_done)

                def head_sum(name, src, of):
                    pe.wait_ge(out_free, o_(of, layer) + 1)
                    ones_sum(name, [src])

                proj("ckv", 0, 0, first=True)
                proj("kpe", 0, 1)
                proj("cq0", 1, 0)
                swap(0)
                proj("cq1", 1, 1)
                proj("q0", 2, 0)
                pe.wait_ge(out_free, o_("cq1", layer) + 1)
                ones_sum("sckv", [sq3[:, 0, :]])
                ones_sum("scq", [sq3[:, 1, :], sq3[:, 2, :]])
                for r, name in enumerate(ROPES[2:9], start=1):
                    proj(name, 2 + r // 2, r % 2)
                    swap(r)
                up_q("qpe0", 0)
                swap(8)
                up_q("qpe1", 1)
                swap(9)
                for h in range(HEADS):
                    up_q(f"qn{h}", 2 + h)
                    if h == 0:
                        swap(10)
                used_up.append((direct_used, 1))
                arrived(pe, u0 + U_UKV)
                w = slot(u0 + U_UKV)
                for h in range(HEADS):
                    mm(rot_bank(f"kn{h}"), w[:, h * P:(h + 1) * P], ckv, True, True, out_done)
                for t in range(3):
                    dst = rot_bank(f"v{t}", 512)[0:TILES[t][1], :]
                    mm(dst, tok_rows(ckv, t), w[:, 512:1024], True, True, out_done)
                used_up.append((direct_used, 1))
                latent_scores(0)
                latent_scores(1)
                for t in range(3):
                    p0 = TILES[t][0]
                    dst = rot_bank(f"rv{t}", 512)
                    for k in range(DK):
                        w = [x.rearrange("p (k c) -> p k c", k=4)[:, k % 4, :] for x in split(pe, u0 + U_RV + k // 4)]
                        mm3(dst, [hi[:, k, p0:p0 + P], lo[:, k, p0:p0 + P]], w, k == 0, k == DK - 1,
                            out_done if k == DK - 1 else None)
                    if t < 2:
                        latent_scores(2 + t)
                used_up.append((w_used, 2))
                for h in range(HEADS):
                    proj(f"g{h}", U_RG + h // 2, h % 2)
                prob_transposes(0)
                prob_transposes(1)
                weigh("yM0", 0, vm)
                prob_transposes(2)
                weigh("yM1", 1, vm)
                prob_transposes(3)
                weigh("yM2", 2, vm)
                retention_scores(0)
                weigh("yM3", 3, vm)
                retention_scores(1)
                head_sum("sM0", sq3[:, 0, :], "yM0")
                head_sum("sM1", sq3[:, 2, :], "yM1")
                weigh("yR0", 4, rv)
                retention_scores(2)
                head_sum("sM2", sq3[:, 4, :], "yM2")
                head_sum("sM3", sq3[:, 6, :], "yM3")
                weigh("yR1", 5, rv)
                retention_scores(3)
                weigh("yR2", 6, rv)
                head_sum("sR0", sq3[:, 1, :], "yR0")
                head_sum("sR1", sq3[:, 3, :], "yR1")
                weigh("yR3", 7, rv)
                head_sum("sR2", sq3[:, 5, :], "yR2")
                head_sum("sR3", sq3[:, 7, :], "yR3")

                pe.wait_ge(out_free, (layer + 1) * N_OUTS)
                added = 0 if layer == 0 else 8 + 8 * CHUNKS

                def wo(d, k, last):
                    w = [x.rearrange("p (k c) -> p k c", k=DK)[:, k, (d % 2) * P:(d % 2 + 1) * P]
                         for x in split(pe, u0 + U_WO + d // 2)]
                    mm3(bank[d % 4][:, 0:L], w, [hi[:, k, :], lo[:, k, :]], k == 4, last, wo_done if last else None)

                pe.wait_ge(mix_ready, 5 * layer + 1)
                for d in range(4):
                    for k in range(4, 8):
                        wo(d, k, False)
                for d in range(4):
                    for k in range(4):
                        if d == 0:
                            pe.wait_ge(mix_ready, 5 * layer + 2 + k)
                        wo(d, k, k == 3)
                    if d % 2:
                        used_up.append((w_used, 1))
                for d in range(4, 8):
                    pe.wait_ge(h_added, added + d - 3)
                    for k in (4, 5, 6, 7, 0, 1, 2, 3):
                        wo(d, k, k == 3)
                    if d % 2:
                        used_up.append((w_used, 1))

            def dense():
                def gate_up(c):
                    if c >= 1:
                        pe.wait_ge(af_ready, c)
                    for j, kind in enumerate("gu"):
                        w = [x.rearrange("p (k c) -> p k c", k=DK) for x in split(pe, DENSE_AT + FFN_POS[kind, c])]
                        for f in range(2):
                            for k in range(DK):
                                if c == 0 and j == 0 and f == 0 and k % 2 == 0:
                                    pe.wait_ge(hn_ready, 4 + k // 2 + 1)
                                last = f == 1 and k == DK - 1 and j == 1
                                mm3(bank[2 * j + f][:, 0:L], [x[:, k, f * P:(f + 1) * P] for x in w],
                                    [hi[:, k, :], lo[:, k, :]], k == 0, k == DK - 1, gu_done if last else None)
                        used_up.append((w_used, 1))

                def down(c):
                    w = [x.rearrange("p (f n) -> p f n", f=2) for x in split(pe, DENSE_AT + FFN_POS["d", c])]
                    pe.wait_ge(a_ready, c + 1)
                    for d in range(DK):
                        if c or d >= 4:
                            pe.wait_ge(h_added, 8 + c * DK + d - 3)
                        for f in range(2):
                            mm3(bank[4 + d % 4][:, 0:L], [x[:, f, d * P:(d + 1) * P] for x in w],
                                [ad_hi[c % 2][:, f, :], ad_lo[c % 2][:, f, :]], f == 0, f == 1, d_done if f == 1 else None)
                    used_up.append((w_used, 1))

                gate_up(0)
                for c in range(1, CHUNKS):
                    gate_up(c)
                    down(c - 1)
                down(CHUNKS - 1)

            def routing():
                for t in range(2):
                    p0 = TILES[t][0]
                    for k in range(DK):
                        if t == 0:
                            pe.wait_ge(hnf_ready, 24 + k + 1)
                        mm(bank[0][:, t * EXPERTS:(t + 1) * EXPERTS], sq3[:, k, p0:p0 + P], rw_sb[:, k, :],
                           k == 0, k == DK - 1, lg_done if t == 1 and k == DK - 1 else None)
                for n in range(8):
                    src, t, half = n // 4, n // 2 % 2, n % 2
                    if n >= 2:
                        pe.wait_ge(tok_free, n - 1)
                    p0 = TILES[t][0]
                    for i in range(4):
                        turn(bank[4 + n % 2][:, i * P:(i + 1) * P], (hT, sq3)[src][:, half * 4 + i, p0:p0 + P],
                             tok_done if i == 3 else None)
                pe.wait_ge(sel_ready, 1)
                b = bank[1]
                mm(b[:, 0:8], tri, sel[:, 0, :], True, True)
                mm(b[:, 8:16], ones, sel[:, 0, :], True, False)
                mm(b[:, 8:16], tri, sel[:, 1, :], False, True)
                mm(b[:, 16:24], ones, sel[:, 0, :], True, False)
                mm(b[:, 16:24], ones, sel[:, 1, :], False, True, pos_done)

            def gather(n):
                pe.wait_ge(g_ready, n + 1)
                for d in range(DK):
                    for t in range(2):
                        mm(bank[7 - d // 4][:, (d % 4) * CAP:(d % 4 + 1) * CAP], hn_tok[:, t, d * P:(d + 1) * P],
                           G[:, t, :], t == 0, t == 1, gt_done if d == DK - 1 and t == 1 else None)

            def scatter_out(it, j):
                t, half = j // 2, j % 2
                if j == 0:
                    pe.wait_ge(ye_ready, it + 1)
                    pe.wait_ge(gwt_ready, it + 1)
                if j >= 2:
                    pe.wait_ge(acc_added, it * 4 + j)
                mm(bank[7 - half][:, :], GWT[:, t * P:(t + 1) * P], ye[:, half * 512:(half + 1) * 512],
                   True, True, sc_out)

            def expert(it):
                def ready(key):
                    m = MOE_SPLIT + MOE_ORDER.index(key)
                    pe.wait_ge(split_lo, it * FFN_UNITS + (m + 1))
                    return w_hi[:, m % HSLOTS, :], w_lo[:, m % HSLOTS, :]

                def into(kind, c):
                    dst = bank[(0 if kind == "g" else 2) + c % 2]
                    for i in range(2):
                        w = [x.rearrange("p (k c) -> p k c", k=4) for x in ready((kind, c, i))]
                        for kk in range(4):
                            k = 4 * i + kk
                            last = k == DK - 1
                            mm3(dst[:, :], [x_hi[:, k, :], x_lo[:, k, :]], [x[:, kk, :] for x in w], k == 0, last,
                                e_gu if last and kind == "u" else None)
                        used_up.append((w_used, 1))

                def turn_hidden(c):
                    pe.wait_ge(e_af, it * MOE_CHUNKS + c + 1)
                    if c == 0:
                        pe.wait_ge(acc_added, it * 4 + 5)
                    for f in range(4):
                        turn(bank[6 if c < MOE_CHUNKS - 1 else 3][:, f * CAP:(f + 1) * CAP], a_moe[:, f * P:(f + 1) * P],
                             at_done if f == 3 else None)

                def down(c):
                    for i in range(2):
                        w = [x.rearrange("p (f n) -> p f n", f=2) for x in ready(("d", c, i))]
                        if i == 0:
                            pe.wait_ge(e_a, it * MOE_CHUNKS + c + 1)
                        for ff in range(2):
                            f = 2 * i + ff
                            a = [x[c % 2][:, f * CAP:(f + 1) * CAP] for x in (ae_hi, ae_lo)]
                            for half in range(2):
                                end = c == MOE_CHUNKS - 1 and f == 3
                                mm3(bank[4 + half][:, :], a, [x[:, ff, half * 512:(half + 1) * 512] for x in w],
                                    c == 0 and f == 0, end, w_used if end and half == 1 else None)
                        if not (c == MOE_CHUNKS - 1 and i == 1):
                            used_up.append((w_used, 1))

                pe.wait_ge(xg_ready, it + 1)
                into("g", 0)
                scatter_out(it, 0)
                scatter_out(it, 1)
                into("u", 0)
                scatter_out(it, 2)
                scatter_out(it, 3)
                for c in range(1, MOE_CHUNKS):
                    into("g", c)
                    if c == 3:
                        pe.wait_ge(gwt_in, it + 1)
                        for t in range(2):
                            turn(bank[7][:, t * P:(t + 1) * P], GW[:, t, :], gwt_done if t else None)
                    turn_hidden(c - 1)
                    into("u", c)
                    if c == MOE_CHUNKS - 1:
                        pe.wait_ge(gwt_ready, it + 2)
                        pe.wait_ge(e_a, it * MOE_CHUNKS + c)
                        gather(it + 1)
                        turn_hidden(c)
                    down(c - 1)
                down(MOE_CHUNKS - 1)
                assert not used_up

            pe.wait_ge(const_in, 48)
            norm(0)
            attention(0)
            norm(1)
            dense()
            norm(2)
            attention(1)
            norm(3)
            routing()
            gather(0)
            pe.wait_ge(rounds_ready, 1)
            rounds = pe.value_load(rounds_sb[0:1, 0:1], min_val=1, max_val=2)
            with pe.Fori(0, rounds) as r:
                with pe.Fori(0, EXPERTS) as e:
                    expert(r * EXPERTS + e)
            its = rounds * EXPERTS
            for j in range(4):
                scatter_out(its, j)

        @block.scalar
        def _(act):
            A = nc.scalar.activation

            def high(n):
                arrived(act, UNIT_OF[n])
                if n >= HSLOTS:
                    act.wait_ge(w_used, n - HSLOTS + 1)
                A(w_hi[:, n % HSLOTS, :], slot(UNIT_OF[n]), ACT.Copy).then_inc(split_hi, 1)

            def norm(n, between=(), after=()):
                for half in range(2):
                    if n == 0:
                        act.wait_ge(x_in, 16)
                    else:
                        total = [0, 8, 8 + 8 * CHUNKS, 16 + 8 * CHUNKS][n]
                        act.wait_ge(h_added, total - 4 + 4 * half)
                    A(sq3[:, 4 * half:4 * half + 4, :], hT[:, 4 * half:4 * half + 4, :], ACT.Square).then_inc(sq_ready, 1)
                    for u in (after if half else between):
                        high(u)
                act.wait_ge(ms_done, n + 1)
                act.wait_ge(ones_set, 3)
                A(std[:, 0, :], norm_bank(n)[:, 0:L], ACT.Sqrt, bias=eps_sb[:, 0:1], scale=1.0 / D).then_inc(std_ready, 1)
                if n < 3:
                    for k in range(0, DK, 2):
                        act.wait_ge(hnf_ready, n * DK + k + 2)
                        A(hi[:, k:k + 2, :], sq3[:, k:k + 2, :], ACT.Copy).then_inc(hi_ready, 1)

            def attention(layer):
                def src(name, rows=P, cols=L):
                    o = o_(name, layer)
                    act.wait_ge(out_done, o + 1)
                    return bank[o % 4][0:rows, 0:cols]

                b = SPLIT_OF[base_of(layer)]

                def keep(name, dst, rows=P, cols=L):
                    A(dst, src(name, rows, cols), ACT.Copy).then_inc(out_free, 1)

                def keep_square(name, dst, sq_dst):
                    s = src(name)
                    A(dst, s, ACT.Copy)
                    A(sq_dst, s, ACT.Square).then_inc(out_free, 1)

                def root(name, dst, n):
                    A(dst, src(name), ACT.Sqrt, bias=eps_sb[:, 0:1], scale=1.0 / n).then_inc(out_free, 1)

                def keep_raw(name):
                    r = ROPES.index(name)
                    if r >= 3:
                        act.wait_ge(rope_done, layer * N_ROPES + r - 2)
                    keep(name, raw[:, r % 3, :])

                def exps(h):
                    act.wait_ge(p1_ready, HEADS * layer + h + 1)
                    p = p_of(h)
                    for t, (rows, c0, c1) in enumerate([(P, 0, META + P), (P, META + P, MASK), (META, MASK, MASK + META)]):
                        x = A(p[0:rows, c0:c1], p[0:rows, c0:c1], ACT.Exp, bias=nmx[0:rows, h, t:t + 1], scale=SCALE,
                              accum_out=sums[0:rows, h, t:t + 1])
                    x.then_inc(exp_done, 1)

                def tables(h):
                    act.wait_ge(pt_done, HEADS * layer + h + 1)
                    x, y = bank[4 + 2 * (h % 2)], bank[5 + 2 * (h % 2)]
                    A(STx[:, h % 2, :], x[:, 0:3 * P], ACT.Copy)
                    A(STy[0:META, h % 2, :], y[0:META, 0:L], ACT.Copy).then_inc(pt_free, 1)

                keep_square("ckv", ckv, sq3[:, 0, :])
                keep_raw("kpe")
                high(b + 3)
                keep_square("cq0", cq[:, 0, :], sq3[:, 1, :])
                keep_square("cq1", cq[:, 1, :], sq3[:, 2, :])
                high(b + 4)
                keep_raw("q0")
                root("sckv", std[:, 0, :], KVR)
                root("scq", std[:, 1, :], QR)
                for name in ROPES[2:]:
                    keep_raw(name)
                    if name in ("q1", "q3", "k1", "k3"):
                        high(b + 5 + ["q1", "q3", "k1", "k3"].index(name))
                for h in range(HEADS):
                    keep(f"qn{h}", qn[:, h, :])
                for h in range(HEADS):
                    keep(f"kn{h}", kn[:, h, :])
                for t, (_, rows) in enumerate(TILES):
                    keep(f"v{t}", vm[0:rows, t, :], rows, 512)
                exps(0)
                exps(1)
                for t, (_, rows) in enumerate(TILES):
                    keep(f"rv{t}", rv[0:rows, t, :], rows, 512)
                    if t < 2:
                        exps(2 + t)
                high(b + 9)
                high(b + 10)
                for h in range(HEADS):
                    keep(f"g{h}", rg[:, h, :])
                    if h % 2:
                        high(b + 11 + h // 2)
                tables(0)
                tables(1)
                for h in range(HEADS):
                    keep_square(f"yM{h}", qn[:, h, :], sq3[:, 2 * h, :])
                    if h < 2:
                        tables(h + 2)
                act.wait_ge(out_free, o_("g3", layer) + 1)
                A(rg[:, :, :], rg[:, :, :], ACT.Silu).then_inc(silu_g, 1)
                for name in OUTS[OUTS.index("sM0"):]:
                    h = int(name[2])
                    if name[0] == "y":
                        keep_square(name, qT[:, h, :], sq3[:, 2 * h + 1, :])
                    elif name[1] == "M":
                        root(name, std[:, h, :], P)
                    else:
                        root(name, sq3[:, 2 * h, :], P)
                act.wait_ge(mixf_ready, 5 * layer + 1)
                A(hi[:, 4:8, :], qn[:, :, :], ACT.Copy).then_inc(mix_hi, 1)
                for h in range(HEADS):
                    act.wait_ge(mixf_ready, 5 * layer + 2 + h)
                    A(hi[:, h, :], qT[:, h, :], ACT.Copy).then_inc(mix_hi, 1)
                high(b + 13)
                if layer == 0:
                    high(b + 14)

            def dense():
                for m, (kind, c) in enumerate(FFN_ORDER):
                    n = SPLIT_OF[DENSE_AT] + m + HSLOTS
                    if kind == "u":
                        act.wait_ge(gu_done, c + 1)
                        A(sil_dense[:, 0, :], bank[0][:, 0:L], ACT.Silu)
                        A(sil_dense[:, 1, :], bank[1][:, 0:L], ACT.Silu).then_inc(silu_done, 1)
                    if m < FFN_UNITS - 1:
                        high(n)
                    if kind == "u":
                        act.wait_ge(af_ready, c + 1)
                        A(ad_hi[c % 2], a_dense, ACT.Copy).then_inc(a_hi_ready, 1)

            def turn_copies():
                for n in range(0, 8):
                    src, t, half = n // 4, n // 2 % 2, n % 2
                    act.wait_ge(tok_done, n + 1)
                    A((acc, hn_tok)[src][:, t, half * 512:(half + 1) * 512], bank[4 + n % 2][:, :], ACT.Copy).then_inc(tok_free, 1)

            def scatter_copy(it):
                act.wait_ge(w_used, it * FFN_UNITS + MOE_SPLIT)
                A(ye[:, 0:512], bank[4][:, :], ACT.Copy)
                A(ye[:, 512:1024], bank[5][:, :], ACT.Copy).then_inc(ye_ready, 1)

            def take(n):
                act.wait_ge(gt_done, n + 1)
                for j in range(2):
                    A(x_hi[:, 4 * j:4 * j + 4, :], bank[7 - j][:, :].rearrange("p (a b) -> p a b", a=4), ACT.Copy).then_inc(e_xhi, 1)

            def expert(it):
                def high_of(m):
                    n, u = MOE_SPLIT + m, MOE_AT + m
                    act.wait_ge(slot_in[u % SLOTS], it * (16 * FFN_UNITS // SLOTS) + 16 * (u // SLOTS + 1))
                    act.wait_ge(w_used, it * FFN_UNITS + (n - HSLOTS + 1))
                    A(w_hi[:, n % HSLOTS, :], ring[:, u % SLOTS, :], ACT.Copy).then_inc(split_hi, 1)

                def hidden(c):
                    act.wait_ge(at_done, it * MOE_CHUNKS + c + 1)
                    A(ae_hi[c % 2], bank[6 if c < MOE_CHUNKS - 1 else 3][:, :], ACT.Copy).then_inc(e_ahi, 1)

                for m in range(HSLOTS):
                    high_of(m)
                scatter_copy(it)
                for m, (kind, c, i) in enumerate(MOE_ORDER[:-HSLOTS]):
                    if (kind, i) == ("u", 1):
                        act.wait_ge(e_gu, it * MOE_CHUNKS + c + 1)
                        A(sil_moe, bank[c % 2][:, :], ACT.Silu).then_inc(e_silu, 1)
                    high_of(m + HSLOTS)
                    if (kind, i) == ("g", 1) and c:
                        hidden(c - 1)
                    if (kind, c, i) == ("u", MOE_CHUNKS - 1, 1):
                        take(it + 1)
                        hidden(c)

            for n in range(HSLOTS):
                high(n)
            norm(0)
            attention(0)
            norm(1, between=(SPLIT_OF[DENSE_AT] + 1,), after=(SPLIT_OF[DENSE_AT] + 2,))
            dense()
            norm(2, after=(SPLIT_OF[ATTN1_AT] + 2,))
            attention(1)
            norm(3)
            turn_copies()
            act.wait_ge(gexp_in, 1)
            A(v12[:, :, 2:3], v12[:, :, 2:3], ACT.Exp).then_inc(gexp_out, 1)
            take(0)
            act.wait_ge(y_zero, 1)
            act.wait_ge(rounds_ready, 1)
            rounds = act.value_load(rounds_sb[0:1, 0:1], min_val=1, max_val=2)
            with act.Fori(0, rounds) as r:
                with act.Fori(0, EXPERTS) as e:
                    expert(r * EXPERTS + e)
            its = rounds * EXPERTS
            scatter_copy(its)
            act.wait_ge(acc_added, its * 4 + 5)
            for t in range(2):
                A(res[:, t, :], acc[:, t, :], ACT.Square, accum_out=fin[:, t, 0:1]).then_inc(fsq, 1)
            act.wait_ge(fsq, 2)
            A(fin[:, :, 1], fin[:, :, 0], ACT.Sqrt, bias=eps_sb[:, 0:1], scale=1.0 / D).then_inc(fstd, 1)

        @block.vector
        def _(dve):
            V = nc.vector
            chain = [0]

            def link(ins):
                chain[0] += 1
                ins.then_inc(link_sem, 1)
                dve.wait_ge(link_sem, chain[0])

            def low(n):
                dve.wait_ge(split_hi, n + 1)
                V.tensor_tensor(w_lo[:, n % HSLOTS, :], slot(UNIT_OF[n]), w_hi[:, n % HSLOTS, :].bitcast(F32),
                                ALU.subtract).then_inc(split_lo, 1)

            def norm(n):
                dve.wait_ge(std_ready, n + 1)
                link(V.reciprocal(std[:, 0, :], std[:, 0, :]))
                g0 = (G_ATTN if n % 2 == 0 else G_FFN) + DK * (n // 2)

                def rest(k):
                    dve.wait_ge(hi_ready, n * 4 + k // 2 + 1)
                    V.tensor_tensor(lo[:, k:k + 2, :], sq3[:, k:k + 2, :], hi[:, k:k + 2, :].bitcast(F32),
                                    ALU.subtract).then_inc(hn_ready, 1)

                for k in range(DK):
                    V.scalar_tensor_tensor(out=sq3[:, k, :], in0=hT[:, k, :], scalar=gain(g0 + k), in1=std[:, 0, :],
                                           op0=ALU.mult, op1=ALU.mult).then_inc(hnf_ready, 1)
                    if n < 3 and k % 2 and k > 1:
                        rest(k - 3)
                if n < 3:
                    rest(DK - 2)

            def attention(layer):
                u0 = base_of(layer)
                b = SPLIT_OF[u0]

                def rope(r):
                    name = ROPES[r]
                    if name == "kpe":
                        dst = kpe
                    elif name.startswith("qpe"):
                        dst = qpe[:, int(name[3]), :]
                    else:
                        dst = (qT if name[0] == "q" else kT)[:, int(name[1]), :]
                    cos, sin = (C_COS64, C_SIN64) if "pe" in name else (C_COS, C_SIN)
                    dve.wait_ge(out_free, o_(name, layer) + 1)
                    V.tensor_tensor(dst, raw[:, r % 3, :], col(cos, L), ALU.mult).then_inc(link_sem, 1)
                    chain[0] += 1
                    dve.wait_ge(swap_done, layer * N_ROPES + r + 1)
                    if layer or r:
                        dve.wait_ge(rope_done, layer * N_ROPES + r)
                    V.tensor_tensor(rot, bank[4 + r % 2][:, 0:L], col(sin, L), ALU.mult).then_inc(swap_read, 1)
                    dve.wait_ge(link_sem, chain[0])
                    dve.wait_ge(swap_read, layer * N_ROPES + r + 1)
                    V.tensor_tensor(dst, dst, rot, ALU.add).then_inc(rope_done, 1)

                def latent_norm():
                    dve.wait_ge(out_free, o_("scq", layer) + 1)
                    link(V.reciprocal(std[:, 0:2, :], std[:, 0:2, :]))
                    for x, g, s in [(ckv, G_KV + layer, 0), (cq[:, 0, :], G_Q + 2 * layer, 1), (cq[:, 1, :], G_Q + 2 * layer + 1, 1)]:
                        V.scalar_tensor_tensor(out=x, in0=x, scalar=gain(g), in1=std[:, s, :],
                                               op0=ALU.mult, op1=ALU.mult).then_inc(c_ready, 1)

                def mask_max(h):
                    dve.wait_ge(sc_done, HEADS * layer + h + 1)
                    ps, p = bank[6 + h % 2], p_of(h)
                    mask = slot(u0 + U_T1)[:, HEADS * DECAY:HEADS * DECAY + MASK]
                    link(V.tensor_tensor(p[:, 0:MASK], ps[:, 0:MASK], mask, ALU.add))
                    V.tensor_copy(p[0:META, MASK:MASK + META], ps[0:META, MASK:MASK + META]).then_inc(sc_free, 1)
                    dve.wait_ge(sc_free, HEADS * layer + h + 1)
                    for t, (rows, c0, c1) in enumerate([(P, 0, META + P), (P, META + P, MASK), (META, MASK, MASK + META)]):
                        link(V.tensor_reduce(nmx[0:rows, h, t:t + 1], p[0:rows, c0:c1], axis=AX.X, op=ALU.max))
                    V.tensor_scalar(nmx[:, h, :], nmx[:, h, :], -SCALE, None, ALU.mult).then_inc(p1_ready, 1)

                def normalise(h):
                    dve.wait_ge(exp_done, HEADS * layer + h + 1)
                    link(V.reciprocal(sums[:, h, :], sums[:, h, :]))
                    p = p_of(h)
                    for t, (rows, c0, c1) in enumerate([(P, 0, META + P), (P, META + P, MASK), (META, MASK, MASK + META)]):
                        x = V.tensor_scalar(p[0:rows, c0:c1], p[0:rows, c0:c1], sums[0:rows, h, t:t + 1], None, ALU.mult)
                    x.then_inc(p2_ready, 1)

                def decay(h):
                    dve.wait_ge(rs_done, HEADS * layer + h + 1)
                    s = h % 2
                    t1, t2 = slot(u0 + U_T1), slot(u0 + U_T2)
                    V.tensor_tensor(STx[:, s, :], bank[4 + 2 * s][:, 0:3 * P], t1[:, h * DECAY:(h + 1) * DECAY], ALU.mult)
                    V.tensor_tensor(STy[0:META, s, :], bank[5 + 2 * s][0:META, 0:L], t2[0:META, h * L:(h + 1) * L],
                                    ALU.mult).then_inc(decayed, 1)

                rope(0)
                low(b + 3)
                latent_norm()
                low(b + 4)
                rope(1)
                low(b + 5)
                rope(2)
                rope(3)
                low(b + 6)
                rope(4)
                rope(5)
                low(b + 7)
                rope(6)
                rope(7)
                low(b + 8)
                for r in range(8, N_ROPES):
                    rope(r)
                dve.wait_ge(ones_set, 3)
                arrived(dve, u0 + U_T1)
                for h in range(HEADS):
                    mask_max(h)
                for h in range(HEADS):
                    normalise(h)
                for n in range(9, 13):
                    low(b + n)
                arrived(dve, u0 + U_T2)
                decay(0)
                decay(1)
                decay(2)
                decay(3)
                for h in range(HEADS):
                    m = qn[:, h, :]
                    dve.wait_ge(out_free, o_(f"sM{h}", layer) + 1)
                    link(V.reciprocal(std[:, h, :], std[:, h, :]))
                    x = V.scalar_tensor_tensor(out=m, in0=m, scalar=gain(G_MLA + 4 * layer + h), in1=std[:, h, :],
                                               op0=ALU.mult, op1=ALU.mult)
                x.then_inc(mixf_ready, 1)
                dve.wait_ge(silu_g, layer + 1)
                dve.wait_ge(out_free, o_("yR3", layer) + 1)
                for h in range(HEADS):
                    m = qT[:, h, :]
                    x = V.scalar_tensor_tensor(out=m, in0=m, scalar=gain(G_RET + 4 * layer + h), in1=rg[:, h, :],
                                               op0=ALU.mult, op1=ALU.mult)
                link(x)

                def rest(j):
                    dve.wait_ge(mix_hi, 5 * layer + j + 1)
                    s = slice(4, 8) if j == 0 else slice(j - 1, j)
                    full = qn[:, :, :] if j == 0 else qT[:, j - 1:j, :]
                    V.tensor_tensor(lo[:, s, :], full, hi[:, s, :].bitcast(F32), ALU.subtract).then_inc(mix_ready, 1)

                for h in range(HEADS):
                    dev = sq3[:, 2 * h, :]
                    dve.wait_ge(out_free, o_(f"sR{h}", layer) + 1)
                    link(V.reciprocal(dev, dev))
                    V.tensor_tensor(qT[:, h, :], qT[:, h, :], dev, ALU.mult).then_inc(mixf_ready, 1)
                    rest(h)
                rest(HEADS)
                for d in range(DK):
                    dve.wait_ge(wo_done, DK * layer + d + 1)
                    V.tensor_tensor(hT[:, d, :], hT[:, d, :], bank[d % 4][:, 0:L], ALU.add).then_inc(h_added, 1)
                    if d == 1 or (d % 2 and layer == 0):
                        low(b + 13 + d // 2)

            def dense():
                def add(c, ds):
                    for d in ds:
                        dve.wait_ge(d_done, c * DK + d + 1)
                        if d == 0:
                            dve.wait_ge(h_added, 8 + c * DK)
                        V.tensor_tensor(hT[:, d, :], hT[:, d, :], bank[4 + d % 4][:, 0:L], ALU.add).then_inc(h_added, 1)

                for m, (kind, c) in enumerate(FFN_ORDER):
                    n = SPLIT_OF[DENSE_AT] + m + HSLOTS
                    if kind == "u":
                        dve.wait_ge(silu_done, c + 1)
                        if c:
                            dve.wait_ge(a_ready, c)
                        V.tensor_tensor(a_dense[:, 0, :], bank[2][:, 0:L], sil_dense[:, 0, :], ALU.mult)
                        V.tensor_tensor(a_dense[:, 1, :], bank[3][:, 0:L], sil_dense[:, 1, :], ALU.mult).then_inc(af_ready, 1)
                        if c:
                            add(c - 1, range(4))
                    if m == FFN_UNITS - 1:
                        add(c, range(DK))
                    low(n)
                    if kind == "u":
                        dve.wait_ge(a_hi_ready, c + 1)
                        V.tensor_tensor(ad_lo[c % 2], a_dense, ad_hi[c % 2].bitcast(F32), ALU.subtract).then_inc(a_ready, 1)
                        if c:
                            add(c - 1, range(4, 8))

            def routing():
                E = EXPERTS
                dve.wait_ge(lg_done, 1)
                link(V.tensor_copy(logit, bank[0][:, 0:2 * E].rearrange("p (t e) -> p t e", t=2)))
                for t in range(2):
                    la = logit[:, t, :].unsqueeze(1).to_broadcast([P, E, E])
                    lb = logit[:, t, :].unsqueeze(2).to_broadcast([P, E, E])
                    low = col(C_LOW, E * E).rearrange("p (a b) -> p a b", a=E)
                    ca, cb = cmp_a[:, t * E:(t + 1) * E, :], cmp_b[:, t * E:(t + 1) * E, :]
                    V.tensor_tensor(ca, la, lb, ALU.is_gt)
                    link(V.tensor_tensor(cb, la, lb, ALU.is_equal))
                    link(V.tensor_tensor(cb, cb, low, ALU.mult))
                    link(V.tensor_tensor(ca, ca, cb, ALU.add))
                    link(V.tensor_reduce(rank[:, t, :], ca, axis=AX.X, op=ALU.add))
                V.tensor_scalar(sel, rank, 2.0, None, ALU.is_lt).then_inc(sel_ready, 1)
                V.tensor_scalar(oh1, rank, 0.0, None, ALU.is_equal)
                link(V.tensor_scalar(oh2, rank, 1.0, None, ALU.is_equal))
                for i, oh in ((0, oh1), (1, oh2)):
                    link(V.tensor_tensor(gate, oh, logit, ALU.mult))
                    link(V.tensor_reduce(v12[:, :, i:i + 1], gate, axis=AX.X, op=ALU.add))
                V.tensor_tensor(v12[:, :, 2:3], v12[:, :, 1:2], v12[:, :, 0:1], ALU.subtract).then_inc(gexp_in, 1)
                dve.wait_ge(gexp_out, 1)
                link(V.tensor_scalar(v12[:, :, 3:4], v12[:, :, 2:3], 1.0, None, ALU.add))
                link(V.reciprocal(v12[:, :, 3:4], v12[:, :, 3:4]))
                link(V.tensor_tensor(v12[:, :, 2:3], v12[:, :, 2:3], v12[:, :, 3:4], ALU.mult))
                for t in range(2):
                    link(V.tensor_scalar(oh1[:, t, :], oh1[:, t, :], v12[:, t, 3:4], None, ALU.mult))
                    link(V.scalar_tensor_tensor(out=gate[:, t, :], in0=oh2[:, t, :], scalar=v12[:, t, 2:3], in1=oh1[:, t, :],
                                                op0=ALU.mult, op1=ALU.add))
                link(V.tensor_scalar(oh2, sel, -4096.0, 4096.0, ALU.mult, ALU.add))
                dve.wait_ge(pos_done, 1)
                for t in range(2):
                    V.tensor_tensor(route[:, 0:E, t], oh2[:, t, :], bank[1][:, t * E:(t + 1) * E], ALU.add).then_inc(link_sem, 1)
                    V.tensor_copy(route[:, 0:E, 2 + t], gate[:, t, :]).then_inc(link_sem, 1)
                    chain[0] += 2
                link(V.tensor_reduce(cnt[:, 0:1], bank[1][:, 16:24], axis=AX.X, op=ALU.max))
                V.tensor_scalar(route[:, E, 0:2], route[:, 0, 0:2], -float(CAP), None, ALU.add).then_inc(link_sem, 1)
                V.tensor_copy(route[:, E, 2:4], route[:, 0, 2:4]).then_inc(link_sem, 1)
                chain[0] += 2
                V.tensor_scalar(rounds_sb[:, 0:1], cnt[:, 0:1], float(CAP), 1.0, ALU.is_gt, ALU.add).then_inc(rounds_ready, 1)

            def one_hot(lk, entry):
                lk(V.tensor_copy(nxt, entry))
                V.tensor_scalar(G[:, 0, :], col(C_IOTA, CAP), nxt[:, 0:1], None, ALU.is_equal)
                return V.tensor_scalar(G[:, 1, :], col(C_IOTA, CAP), nxt[:, 1:2], None, ALU.is_equal)

            def take(n):
                for j in range(2):
                    dve.wait_ge(e_xhi, n * 2 + j + 1)
                    d = slice(4 * j, 4 * j + 4)
                    x = V.tensor_tensor(x_lo[:, d, :], bank[7 - j][:, :].rearrange("p (a b) -> p a b", a=4),
                                        x_hi[:, d, :].bitcast(F32), ALU.subtract)
                x.then_inc(xg_ready, 1)

            def add_out(it, j):
                dve.wait_ge(sc_out, it * 4 + (j + 1))
                t, half = j // 2, j % 2
                a = acc[:, t, half * 512:(half + 1) * 512]
                V.tensor_tensor(a, a, bank[7 - half][:, :], ALU.add).then_inc(acc_added, 1)

            LINKS = 2

            def expert(it, e):
                links = [0]

                def lk(ins):
                    links[0] += 1
                    ins.then_inc(e_link, 1)
                    dve.wait_ge(e_link, it * LINKS + links[0])

                def low_of(m):
                    n, u = MOE_SPLIT + m, MOE_AT + m
                    dve.wait_ge(split_hi, it * FFN_UNITS + (n + 1))
                    V.tensor_tensor(w_lo[:, n % HSLOTS, :], ring[:, u % SLOTS, :], w_hi[:, n % HSLOTS, :].bitcast(F32),
                                    ALU.subtract).then_inc(split_lo, 1)

                def hidden(c):
                    dve.wait_ge(e_ahi, it * MOE_CHUNKS + c + 1)
                    V.tensor_tensor(ae_lo[c % 2], bank[6 if c < MOE_CHUNKS - 1 else 3][:, :], ae_hi[c % 2].bitcast(F32),
                                    ALU.subtract).then_inc(e_a, 1)

                for m in range(HSLOTS):
                    low_of(m)
                lk(V.tensor_copy(cur, route[:, e, :]))
                for t in range(2):
                    x = V.tensor_scalar(GW[:, t, :], col(C_IOTA, CAP), cur[:, t:t + 1], cur[:, 2 + t:3 + t], ALU.is_equal, ALU.mult)
                x.then_inc(gwt_in, 1)
                for m, (kind, c, i) in enumerate(MOE_ORDER[:-HSLOTS]):
                    if (kind, i) == ("u", 1):
                        dve.wait_ge(e_silu, it * MOE_CHUNKS + c + 1)
                        V.tensor_tensor(a_moe, bank[2 + c % 2][:, :], sil_moe, ALU.mult).then_inc(e_af, 1)
                    low_of(m + HSLOTS)
                    if i and c == 0 and kind != "d":
                        add_out(it, 2 if kind == "u" else 0)
                        add_out(it, 3 if kind == "u" else 1)
                    if (kind, i) == ("g", 1) and c:
                        hidden(c - 1)
                    if (kind, c, i) == ("g", 3, 1):
                        dve.wait_ge(gwt_done, it + 1)
                        V.tensor_copy(GWT, bank[7][:, 0:FRAMES]).then_inc(gwt_ready, 1)
                        one_hot(lk, route[:, e + 1, :]).then_inc(g_ready, 1)
                    if (kind, c, i) == ("u", MOE_CHUNKS - 1, 1):
                        take(it + 1)
                        hidden(c)
                assert links[0] == LINKS

            link(V.memset(rot, 0.0))
            for n in range(HSLOTS):
                low(n)
            norm(0)
            attention(0)
            norm(1)
            dense()
            norm(2)
            attention(1)
            norm(3)
            routing()
            one_hot(link, route[:, 0, :]).then_inc(g_ready, 1)
            dve.wait_ge(tok_free, 8)
            link(V.memset(bank[4][:, :], 0.0))
            V.memset(bank[5][:, :], 0.0).then_inc(y_zero, 1)
            V.memset(GWT, 0.0).then_inc(gwt_ready, 1)
            V.memset(cnt, 0.0).then_inc(acc_added, 1)
            take(0)
            dve.wait_ge(rounds_ready, 1)
            rounds = dve.value_load(rounds_sb[0:1, 0:1], min_val=1, max_val=2)
            with dve.Fori(0, rounds) as r:
                with dve.Fori(0, EXPERTS) as e:
                    expert(r * EXPERTS + e, e)
                V.tensor_scalar(route[:, :, 0:2], route[:, :, 0:2], -float(CAP), None, ALU.add).then_inc(round_shifted, 1)
                dve.wait_ge(round_shifted, r + 1)
            its = rounds * EXPERTS
            for j in range(4):
                add_out(its, j)
            dve.wait_ge(fstd, 1)
            link(V.reciprocal(fin[:, :, 1], fin[:, :, 1]))
            dve.wait_ge(fn_in, 16)
            for t in range(2):
                V.scalar_tensor_tensor(out=res[:, t, :], in0=acc[:, t, :], scalar=fin[:, t, 1:2], in1=fn_sb[:, :],
                                       op0=ALU.mult, op1=ALU.mult).then_inc(res_ready, 1)


def _tables():
    f = np.float32
    pos = np.arange(L, dtype=f)

    def angles(dim):
        inv = f(10000.0) ** (-np.arange(0, dim, 2, dtype=f) / f(dim))
        ang = (pos[:, None] * inv[None, :]).astype(f)
        return np.cos(ang).astype(f).T, np.sin(ang).astype(f).T

    c = np.zeros((P, C_COLS), f)
    cos, sin = angles(P)
    c[:, C_COS:C_COS + L], c[:, C_SIN:C_SIN + L] = np.tile(cos, (2, 1)), np.tile(sin, (2, 1))
    cos, sin = angles(ROPE)
    c[:, C_COS64:C_COS64 + L], c[:, C_SIN64:C_SIN64 + L] = np.tile(cos, (4, 1)), np.tile(sin, (4, 1))
    c[:, C_ID:C_ID + P] = np.eye(P)
    c[:, C_ONES:C_ONES + P] = 1.0
    c[:, C_TRI:C_TRI + P] = np.triu(np.ones((P, P)), 1)

    def swap(half):
        m = np.zeros((P, P), f)
        for b in range(0, P, 2 * half):
            for i in range(half):
                m[b + half + i, b + i] = -1.0
                m[b + i, b + half + i] = 1.0
        return m

    c[:, C_SW:C_SW + P], c[:, C_SW64:C_SW64 + P] = swap(P // 2), swap(ROPE // 2)
    c[:, C_IOTA:C_IOTA + CAP] = np.arange(CAP)
    c[:, C_LOW:] = np.tril(np.ones((EXPERTS, EXPERTS)), -1).ravel()

    gamma = np.log1p(-np.exp2(-5.0 - np.arange(HEADS, dtype=np.float64)))
    t1, t2 = np.zeros((P, T1_COLS), f), np.zeros((P, T2_COLS), f)
    j = np.arange(P)
    i = np.arange(2 * P)
    allowed = i[None, :] // CHUNK >= j[:, None] // CHUNK
    for h in range(HEADS):
        w = np.exp(gamma[h] * np.abs(i[None, :] - j[:, None])) * allowed * P ** -0.5
        t1[:, h * DECAY:h * DECAY + 2 * P] = w
        t1[:, h * DECAY + 2 * P:(h + 1) * DECAY] = w[:, :P]
        a = np.arange(L)
        t2[:META, h * L:(h + 1) * L] = np.exp(gamma[h] * np.abs(a[None, :] - np.arange(META)[:, None])) * P ** -0.5
    block = np.where(j[:, None] // CHUNK >= j[None, :] // CHUNK, 0.0, -BIG)
    m = t1[:, HEADS * DECAY:]
    m[:, META:META + P] = block
    m[:, META + P + META + P:] = block
    return c, t1, t2


def kernel(**inputs):
    import numpy as _np
    import concourse.bacc as _bacc
    from concourse import mybir as _mybir
    from concourse.bass_utils import run_bass_kernel_spmd as _run

    x = {k: _np.asarray(v) for k, v in inputs.items()}
    consts, t1, t2 = _tables()
    units = _np.zeros((N_UNITS, P, UNIT), _np.float32)

    def cols(w):
        return w.reshape(DK, P, 256).transpose(1, 0, 2).reshape(P, UNIT)

    for layer in range(2):
        at = 0 if layer == 0 else ATTN1_AT
        rq, rk, rv, rg, cq, ckv, kr = _np.split(x["w_in"][layer], [512, 1024, 1536, 2048, 2304, 2432], axis=1)
        units[at] = cols(_np.concatenate([ckv, kr, kr], axis=1))
        units[at + 1] = cols(cq)
        for i in range(2):
            units[at + 2 + i] = cols(rq[:, 256 * i:256 * (i + 1)])
            units[at + 4 + i] = cols(rk[:, 256 * i:256 * (i + 1)])
            units[at + U_RV + i] = rv[512 * i:512 * (i + 1)].reshape(4, P, 512).transpose(1, 0, 2).reshape(P, UNIT)
            units[at + U_RG + i] = cols(rg[:, 256 * i:256 * (i + 1)])
        uq = x["w_uq"][layer].reshape(QR, HEADS, P + ROPE)
        uq = _np.concatenate([uq[:, :, P:].reshape(QR, HEADS * ROPE), uq[:, :, :P].reshape(QR, HEADS * P)], axis=1)
        units[at + U_UQ, :, :UQ_COLS] = uq.reshape(2, P, 768).transpose(1, 0, 2).reshape(P, UQ_COLS)
        ukv = x["w_ukv"][layer].reshape(KVR, HEADS, 2, P).transpose(0, 2, 1, 3)
        units[at + U_UKV, :, :UKV_COLS] = ukv.reshape(KVR, UKV_COLS)
        units[at + U_T1, :, :T1_COLS], units[at + U_T2, :, :T2_COLS] = t1, t2
        for i in range(4):
            units[at + U_WO + i] = cols(x["w_out"][layer][:, 256 * i:256 * (i + 1)])

    def ffn(at, gate, up, down):
        for n, (kind, c) in enumerate(FFN_ORDER):
            if kind == "d":
                units[at + n] = down[256 * c:256 * (c + 1)].reshape(2, P, D).transpose(1, 0, 2).reshape(P, UNIT)
            else:
                units[at + n] = cols((gate if kind == "g" else up)[:, 256 * c:256 * (c + 1)])

    ffn(DENSE_AT, x["dense_w_gate"][0], x["dense_w_up"][0], x["dense_w_down"][0])
    for e in range(EXPERTS):
        for n, (kind, c, i) in enumerate(MOE_ORDER):
            if kind == "d":
                w = x["moe_w_down"][0, e][512 * c + 256 * i:512 * c + 256 * (i + 1)].reshape(2, P, D)
            else:
                w = x["moe_w_gate" if kind == "g" else "moe_w_up"][0, e][512 * i:512 * (i + 1), 512 * c:512 * (c + 1)].reshape(4, P, 512)
            units[MOE_AT + e * FFN_UNITS + n] = w.transpose(1, 0, 2).reshape(P, UNIT)

    def lanes(v):
        return v.reshape(-1, P).T

    gains = _np.concatenate([lanes(x[n]) for n in ("attn_norm", "ffn_norm", "ret_out_gain", "mla_out_gain", "q_norm", "kv_norm")], axis=1)
    h0 = _np.concatenate([x["meta_tokens"], x["x"][0]], axis=0).T.reshape(DK, P, L).transpose(1, 0, 2)
    arrays = {
        "stream": units, "h0": h0, "gains": gains,
        "router_w": x["router_w"][0].reshape(DK, P, EXPERTS).transpose(1, 0, 2),
        "fnorm": _np.broadcast_to(x["final_norm"], (P, D)), "consts": consts,
    }
    arrays = {k: _np.ascontiguousarray(v) for k, v in arrays.items()}
    nc = _bacc.Bacc("TRN2", target_bir_lowering=False, num_devices=1)
    args = [nc.dram_tensor(k, v.shape, _mybir.dt.float32, kind="ExternalInput").ap() for k, v in arrays.items()]
    args.append(nc.dram_tensor("out", (FRAMES, D), _mybir.dt.float32, kind="ExternalOutput").ap())
    build(nc, *args)
    r = _run(nc, [arrays], core_ids=[0])
    return _np.asarray(r.results[0]["out"]).reshape(1, FRAMES, D)
```

```python
from contextlib import ExitStack

import numpy as np

import concourse.bass as bass
from concourse import mybir

F32 = mybir.dt.float32
F32R = mybir.dt.float32r
I32 = mybir.dt.int32
ALU = mybir.AluOpType
ACT = mybir.ActivationFunctionType
AX = mybir.AxisListType

P = 128
D = 1024
DK = D // P
META = 16
FRAMES = 256
L = META + FRAMES
CHUNK = 64
EPS = 1e-6
HEADS = 4
QR, KVR = 256, 128
ROPE = 64
SCALE = (P + ROPE) ** -0.5
DFF = 3584
EXPERTS = 8
CAP = 128
BIG = 1e30
SCRATCH = 13632
GAIN_AT = 10144

UNIT = 2048
SLOTS = 6
HSLOTS = 3
MOE_SLOTS = SLOTS + 1
AHEAD = HSLOTS - 1
UQ_COLS, UKV_COLS = 1536, 1024
DECAY, MASK = 384, 416
T1_COLS, T2_COLS = HEADS * DECAY + MASK, HEADS * L
ATTN_UNITS = 18
CHUNKS = DFF // 256
FFN_UNITS = 3 * CHUNKS
DENSE_AT = ATTN_UNITS
ATTN1_AT = ATTN_UNITS + FFN_UNITS
MOE_AT = 2 * ATTN_UNITS + FFN_UNITS
N_UNITS = MOE_AT + EXPERTS * FFN_UNITS
MOE_CHUNKS = DFF // 512
U_UQ, U_UKV, U_RV, U_RG, U_T1, U_T2, U_WO = 6, 7, 8, 10, 12, 13, 14

G_ATTN, G_FFN, G_RET, G_MLA, G_Q, G_KV, G_COLS = 0, 16, 32, 40, 48, 52, 54
C_COS, C_SIN, C_COS64, C_SIN64 = 0, L, 2 * L, 3 * L
C_ID = 4 * L
C_TRI, C_SW, C_SW64, C_IOTA = C_ID + P, C_ID + 2 * P, C_ID + 3 * P, C_ID + 4 * P
C_LOW = C_IOTA + CAP
C_PACK = C_LOW + EXPERTS * EXPERTS
C_ROW = C_PACK + 7 * P // 4
C_COLS = C_ROW + HEADS * P

TILES = [(META, P), (META + P, P), (0, META)]

OUTS = (["ckv", "kpe", "cq0", "cq1", "q0", "sckv", "scq", "q1", "q2", "q3", "k0", "k1", "k2", "k3",
         "qpe0", "qpe1", "qn0", "qn1", "qn2", "qn3", "kn0", "kn1", "kn2", "kn3", "v0", "v1", "v2",
         "rv0", "rv1", "rv2", "g0", "yM0", "g1", "yM1", "g2", "yM2", "yM3", "yR0", "sM", "yR1", "yR2", "bM0", "bM1",
         "yR3", "bM2", "bM3", "g3", "sR", "bR0", "bR1", "bR2", "bR3"])
N_OUTS = len(OUTS)
GROUPS = [(0, 1), (1, 2), (2, 4), (4, 6), (6, 8)]
ROPES = ["kpe", "q0", "q1", "q2", "q3", "k0", "k1", "k2", "k3", "qpe0", "qpe1"]
N_ROPES = len(ROPES)


DIRECT = (U_UQ, U_UKV, U_T1, U_T2)


def ffn_order():
    order = [("g", 0), ("u", 0)]
    for c in range(1, CHUNKS):
        order += [("g", c), ("u", c), ("d", c - 1)]
    return order + [("d", CHUNKS - 1)]


def moe_order():
    order = [(kind, 0, i) for kind in "gu" for i in range(2)]
    for c in range(1, MOE_CHUNKS):
        order += [(kind, c, i) for kind in "gu" for i in range(2)] + [("d", c - 1, i) for i in range(2)]
    return order + [("d", MOE_CHUNKS - 1, i) for i in range(2)]


FFN_ORDER = ffn_order()
FFN_POS = {key: n for n, key in enumerate(FFN_ORDER)}
MOE_ORDER = moe_order()


def is_direct(n):
    return (n - (ATTN1_AT if n >= ATTN1_AT else 0)) in DIRECT


SPLIT_OF = {}
DIRECT_OF = {}
for _n in range(MOE_AT):
    _t = DIRECT_OF if is_direct(_n) else SPLIT_OF
    _t[_n] = len(_t)
MOE_SPLIT = len(SPLIT_OF)
UNIT_OF = {v: k for k, v in SPLIT_OF.items()} | {MOE_SPLIT + n: MOE_AT + n for n in range(AHEAD)}


def build(nc, stream, h0, gains, router_w, fnorm, consts, out):
    with ExitStack() as ctx:
        def sb(name, shape, dt=F32):
            return ctx.enter_context(nc.sbuf_tensor(name, shape, dt))

        def sem(name):
            return ctx.enter_context(nc.semaphore(name))

        ring = sb("ring", [P, SLOTS, UNIT])
        w_hi = sb("w_hi", [P, HSLOTS, UNIT], F32R)
        w_lo = sb("w_lo", [P, HSLOTS, UNIT], F32R)
        hT = sb("hT", [P, DK, L])
        sq = sb("sq", [P, 8 * L])
        sq3 = sq[:, :].rearrange("p (k t) -> p k t", k=8)
        scratch = sb("scratch", [P, SCRATCH])
        parts = sb("parts", [P, 24 * L], F32R)
        hi = parts[:, 0:8 * L].rearrange("p (k t) -> p k t", k=8)
        lo = parts[:, 8 * L:16 * L].rearrange("p (k t) -> p k t", k=8)
        ad = parts[:, 16 * L:24 * L].rearrange("p (b f t) -> p b f t", b=4, f=2)
        ad_hi, ad_lo = [ad[:, 0], ad[:, 1]], [ad[:, 2], ad[:, 3]]
        mla_hi, mla_lo = [parts[:, a * L:(a + 4) * L].rearrange("p (k t) -> p k t", k=4) for a in (16, 20)]
        x_hi = parts[:, 0:DK * CAP].rearrange("p (k c) -> p k c", k=DK)
        x_lo = parts[:, DK * CAP:2 * DK * CAP].rearrange("p (k c) -> p k c", k=DK)
        ae = parts[:, 2 * DK * CAP:4 * DK * CAP].rearrange("p (b n) -> p b n", b=4)
        ae_hi, ae_lo = [ae[:, 0, :], ae[:, 1, :]], [ae[:, 2, :], ae[:, 3, :]]
        g_sb = sb("g_sb", [P, G_COLS])
        c_sb = sb("c_sb", [P, C_COLS])
        rw_sb = sb("rw_sb", [P, DK, EXPERTS])
        rw_gain = sb("rw_gain", [P, DK, EXPERTS])
        ones = sb("ones", [P, P])[:, :]
        warm = sb("warm", [P, 1])
        eps_sb = sb("eps_sb", [P, 1])
        nmx = sb("nmx", [P, HEADS, 3])
        sums = sb("sums", [P, HEADS, 3])
        rounds_sb = sb("rounds_sb", [P, 1], I32)
        fn_sb = sb("fn_sb", [P, D])

        at = [0]

        def carve(n):
            a = scratch[:, at[0]:at[0] + n]
            at[0] += n
            assert at[0] <= SCRATCH, at[0]
            return a

        def carve3(a, b):
            return carve(a * b).rearrange("p (a b) -> p a b", a=a)

        qT, kT, rg = carve3(HEADS, L), carve3(HEADS, L), carve3(HEADS, L)
        qn, kn = carve3(HEADS, L), carve3(HEADS, L)
        rv, vm = carve3(3, 512), carve3(3, 512)
        qpe, kpe, ckv, cq = carve3(2, L), carve(L), carve(L), carve3(2, L)
        raw = carve3(3, L)
        rot = carve(L)
        std = carve3(HEADS, L)
        STx, STy = carve3(2, DECAY), carve3(2, L)

        at[0] = 0
        a_dense, sil_dense = carve3(2, L), carve3(2, L)
        at[0] = 0
        acc = carve3(2, D)
        hn_tok = carve3(2, D)
        sil_moe, a_moe = carve(512), carve(512)
        ye = carve(D)
        G, GW = carve3(2, CAP), carve3(2, CAP)
        GWT = carve(FRAMES)
        route = carve3(EXPERTS + 1, 4)
        cur, nxt = carve(4), carve(4)
        far = carve3(2, EXPERTS)
        logit, sel, gate = carve3(2, EXPERTS), carve3(2, EXPERTS), carve3(2, EXPERTS)
        cmp_a, cmp_b = carve3(2 * EXPERTS, EXPERTS), carve3(2 * EXPERTS, EXPERTS)
        rank = carve3(2, EXPERTS)
        oh1, oh2 = carve3(2, EXPERTS), carve3(2, EXPERTS)
        v12 = carve3(2, 4)
        cnt = carve(4)
        fin = carve3(2, 2)
        res = carve3(2, D)
        dev_tok = carve3(2, 4)
        assert at[0] <= GAIN_AT
        gain_row = scratch[:, GAIN_AT:GAIN_AT + D]

        bank = [ctx.enter_context(nc.psum_tensor(f"bank{i}", [P, 512], F32)) for i in range(8)]

        slot_in = [sem(f"slot_in{i}") for i in range(MOE_SLOTS)]
        direct_used, split_hi, split_lo, w_used = sem("direct_used"), sem("split_hi"), sem("split_lo"), sem("w_used")
        hnf_ready, hi_ready, af_ready, mixf_ready, mix_hi = (
            sem("hnf_ready"), sem("hi_ready"), sem("af_ready"), sem("mixf_ready"), sem("mix_hi"))
        a_hi_ready = sem("a_hi_ready")
        const_in, fn_in, out_stored = sem("const_in"), sem("fn_in"), sem("out_stored")
        x_in, gains_in, rw_in = [sem("x_in0"), sem("x_in1")], sem("gains_in"), sem("rw_in")
        round_shifted = sem("round_shifted")
        gain_in, rw_ready, tok_sum, tok_std, tokhn_ready = (
            sem("gain_in"), sem("rw_ready"), sem("tok_sum"), sem("tok_std"), sem("tokhn_ready"))
        pack_ready, tok_square = sem("pack_ready"), sem("tok_square")
        ones_set = sem("ones_set")
        sq_ready, ms_done, std_ready, hn_ready, h_added = (
            sem("sq_ready"), sem("ms_done"), sem("std_ready"), sem("hn_ready"), sem("h_added"))
        out_done, out_free = sem("out_done"), sem("out_free")
        swap_done, swap_read, rope_done = sem("swap_done"), sem("swap_read"), sem("rope_done")
        c_ready = sem("c_ready")
        sc_done, sc_free, p1_ready, exp_done, p2_ready = (
            sem("sc_done"), sem("sc_free"), sem("p1_ready"), sem("exp_done"), sem("p2_ready"))
        pt_done, pt_free, rs_done, decayed = sem("pt_done"), sem("pt_free"), sem("rs_done"), sem("decayed")
        silu_g, mix_ready, wo_done = sem("silu_g"), sem("mix_ready"), sem("wo_done")
        gu_done, silu_done, a_ready, d_done = sem("gu_done"), sem("silu_done"), sem("a_ready"), sem("d_done")
        link_sem = sem("vector_link")
        lg_done, sel_ready, pos_done = sem("lg_done"), sem("sel_ready"), sem("pos_done")
        gexp_in, gexp_out = sem("gexp_in"), sem("gexp_out")
        tok_done, tok_free = sem("tok_done"), sem("tok_free")
        rounds_ready = sem("rounds_ready")
        e_gu, e_silu, e_a = sem("e_gu"), sem("e_silu"), sem("e_a")
        e_af, at_done, e_ahi, e_xhi, y_zero = sem("e_af"), sem("at_done"), sem("e_ahi"), sem("e_xhi"), sem("y_zero")
        ye_ready, sc_out, acc_added = sem("ye_ready"), sem("sc_out"), sem("acc_added")
        gwt_in, gwt_done, gwt_ready, g_ready, gt_done, xg_ready = (
            sem("gw_ready"), sem("gwt_done"), sem("gwt_ready"), sem("g_ready"), sem("gt_done"), sem("xg_ready"))
        e_link = sem("expert_link")
        fsq, fstd, res_ready = sem("final_squares"), sem("final_std"), sem("res_ready")

        def col(c, n=P):
            return c_sb[:, c:c + n]

        ident, tri = col(C_ID), col(C_TRI)

        def gain(c):
            return g_sb[:, c:c + 1]

        def slot(unit):
            return ring[:, unit % SLOTS, :]

        def moe_slot(m):
            s = m % MOE_SLOTS
            return ring[:, s, :] if s < SLOTS else hT[:, :, :].rearrange("p k t -> p (k t)")[:, 0:UNIT]

        def moe_arrivals(m):
            s = m % MOE_SLOTS
            return 16 * ((MOE_AT // SLOTS if s < SLOTS else 0) + m // MOE_SLOTS + 1)

        def arrived(eng, unit):
            eng.wait_ge(slot_in[unit % SLOTS], 16 * (unit // SLOTS + 1))

        def split(eng, unit):
            n = SPLIT_OF[unit]
            eng.wait_ge(split_lo, n + 1)
            return w_hi[:, n % HSLOTS, :], w_lo[:, n % HSLOTS, :]

        def base_of(layer):
            return 0 if layer == 0 else ATTN1_AT

        def o_(name, layer):
            return layer * N_OUTS + OUTS.index(name)

        def norm_bank(n):
            return bank[(7, 4, 0)[n]]

        def p_of(h):
            return sq[:, h * 2 * L:h * 2 * L + MASK + META]

        used_cols = {U_UQ: UQ_COLS, U_UKV: UKV_COLS, U_T1: T1_COLS, U_T2: T2_COLS}

        block = ctx.enter_context(nc.Block())

        @block.sync
        def _(sp):
            def load(n, cols=UNIT):
                if n >= SLOTS:
                    old = n - SLOTS
                    if is_direct(old):
                        sp.wait_ge(direct_used, DIRECT_OF[old] + 1)
                    else:
                        sp.wait_ge(split_lo, SPLIT_OF[old] + 1)
                sp.dma_start(ring[:, n % SLOTS, 0:cols], stream[n, :, 0:cols]).then_inc(slot_in[n % SLOTS], 16)

            for half in range(2):
                sp.dma_start(hT[:, 4 * half:4 * half + 4, :], h0[:, 4 * half:4 * half + 4, :]).then_inc(x_in[half], 16)
            load(0)
            sp.dma_start(g_sb[:, :], gains).then_inc(gains_in, 16)
            load(1)
            sp.dma_start(c_sb[:, :], consts).then_inc(const_in, 16)
            load(2)
            sp.dma_start(rw_sb[:, :, :], router_w).then_inc(rw_in, 16)
            sp.dma_start(fn_sb[:, :], fnorm[:, 0, :]).then_inc(fn_in, 16)
            for n in range(3, MOE_AT):
                b = n - ATTN1_AT if n >= ATTN1_AT else n
                load(n, used_cols.get(b, UNIT) if b < ATTN_UNITS else UNIT)
                if n == ATTN1_AT + U_T2:
                    sp.wait_ge(rope_done, 2 * N_ROPES)
                    sp.dma_start(gain_row, fnorm[:, 1, :]).then_inc(gain_in, 16)

            def load_round(r):
                with sp.Fori(0, EXPERTS) as e:
                    it = r * EXPERTS + e
                    for m in range(FFN_UNITS):
                        if m == SLOTS:
                            sp.wait_ge(tok_free, 4)
                        before = SLOTS if 2 <= m < SLOTS else MOE_SLOTS
                        sp.wait_ge(split_lo, it * FFN_UNITS + (MOE_SPLIT + m - before + 1))
                        sp.dma_start(moe_slot(m), stream[e * FFN_UNITS + (MOE_AT + m), :, :]).then_inc(slot_in[m % MOE_SLOTS], 16)

            sp.wait_ge(direct_used, len(DIRECT_OF))
            load_round(0)
            sp.wait_ge(rounds_ready, 1)
            rounds = sp.value_load(rounds_sb[0:1, 0:1], min_val=1, max_val=2)
            with sp.If(rounds > 1):
                with sp.Fori(1, rounds) as r:
                    load_round(r)
            with sp.Else():
                sp.nop()
            for m in range(AHEAD):
                sp.wait_ge(split_lo, rounds * (EXPERTS * FFN_UNITS) + (MOE_SPLIT + m - MOE_SLOTS + 1))
                sp.dma_start(moe_slot(m), stream[MOE_AT + m, :, :]).then_inc(slot_in[m % MOE_SLOTS], 16)
            for j in range(2):
                sp.wait_ge(res_ready, j + 1)
                sp.dma_start(out[j * P:(j + 1) * P, :], res[:, j, :]).then_inc(out_stored, 16)
            sp.wait_ge(out_stored, 32)

        @block.gpsimd
        def _(pool):
            nc.gpsimd.memset(ones, 1.0).then_inc(ones_set, 1)
            nc.gpsimd.memset(eps_sb[:], EPS).then_inc(ones_set, 1)
            nc.gpsimd.memset(nmx[:], 0.0).then_inc(ones_set, 1)
            nc.gpsimd.memset(sums[:], 1.0).then_inc(ones_set, 1)
            pool.wait_ge(gains_in, 16)
            pool.wait_ge(rw_in, 16)
            g = g_sb[:, G_FFN + DK:G_FFN + 2 * DK].unsqueeze(2).to_broadcast([P, DK, EXPERTS])
            nc.gpsimd.tensor_tensor(rw_gain[:, :, :], rw_sb[:, :, :], g, ALU.mult).then_inc(rw_ready, 1)

        @block.tensor
        def _(pe):
            used_up = []

            def release(i, inc):
                if inc is not None:
                    i.then_inc(inc, 1)
                elif used_up:
                    i.then_inc(*used_up.pop(0))
                return i

            def mm(dst, lhsT, rhs, start, stop, inc=None):
                return release(nc.tensor.matmul(dst, lhsT, rhs, start=start, stop=stop), inc)

            def turn(dst, src, inc=None):
                n = src.shape[0]
                return release(nc.tensor.transpose(dst, src, ident[0:n, 0:n]), inc)

            def mm3(dst, sta, mov, start, stop, inc=None):
                mm(dst, sta[0], mov[0], start, False)
                mm(dst, sta[1], mov[0], False, False)
                mm(dst, sta[0], mov[1], False, stop, inc)

            def keep_clock(count, b=6):
                for _ in range(count):
                    mm(bank[b][:, 0:P], ones, ones, True, True)

            def square_sum(n, ks):
                for k in ks:
                    pe.wait_ge(sq_ready, DK * n + k + 1)
                    mm(norm_bank(n)[:, 0:L], ones, sq3[:, k, :], k == 0, k == DK - 1, ms_done if k == DK - 1 else None)

            def attention(layer):
                u0 = base_of(layer)

                def rot_bank(name, cols=L):
                    o = o_(name, layer)
                    if o >= 4:
                        pe.wait_ge(out_free, o - 3)
                    return bank[o % 4][:, 0:cols]

                def proj(name, unit, half):
                    dst = rot_bank(name)
                    w = [x.rearrange("p (k c) -> p k c", k=DK)[:, :, half * P:(half + 1) * P] for x in split(pe, u0 + unit)]
                    for k in range(DK):
                        mm3(dst, [x[:, k, :] for x in w], [hi[:, k, :], lo[:, k, :]], k == 0, k == DK - 1,
                            out_done if k == DK - 1 else None)
                    if half:
                        used_up.append((w_used, 1))

                def proj_first(names):
                    dst = [rot_bank(name) for name in names]
                    w = [x.rearrange("p (k c) -> p k c", k=DK) for x in split(pe, u0)]
                    for g, (k0, k1) in enumerate(GROUPS):
                        pe.wait_ge(hn_ready, 2 * layer * len(GROUPS) + g + 1)
                        for half in range(2):
                            for k in range(k0, k1):
                                mm3(dst[half], [x[:, k, half * P:(half + 1) * P] for x in w], [hi[:, k, :], lo[:, k, :]],
                                    k == 0, k == DK - 1, out_done if k == DK - 1 else None)
                    used_up.append((w_used, 1))

                def swap(r):
                    pe.wait_ge(out_free, o_(ROPES[r], layer) + 1)
                    if r >= 2:
                        pe.wait_ge(swap_read, layer * N_ROPES + r - 1)
                    m = col(C_SW64) if "pe" in ROPES[r] else col(C_SW)
                    mm(bank[4 + r % 2][:, 0:L], m, raw[:, r % 3, :], True, True, swap_done)

                def ones_sum(name, srcs):
                    dst = rot_bank(name)
                    for i, x in enumerate(srcs):
                        mm(dst, ones, x, i == 0, i == len(srcs) - 1, out_done if i == len(srcs) - 1 else None)

                def up_q(name, tile):
                    dst = rot_bank(name)
                    if tile == 0:
                        arrived(pe, u0 + U_UQ)
                        pe.wait_ge(c_ready, 3 * layer + 3)
                    w = slot(u0 + U_UQ)[:, 0:UQ_COLS].rearrange("p (k c) -> p k c", k=2)
                    for k in range(2):
                        mm(dst, w[:, k, tile * P:(tile + 1) * P], cq[:, k, :], k == 0, k == 1, out_done if k else None)

                def tok_rows(src, t):
                    p0, n = TILES[t]
                    return src[:, p0:p0 + n]

                def latent_scores(h):
                    dst = bank[6 + h % 2]
                    if h >= 2:
                        pe.wait_ge(sc_free, HEADS * layer + h - 1)
                    if h == 0:
                        pe.wait_ge(rope_done, N_ROPES * (layer + 1))
                        pe.wait_ge(out_free, o_("kn3", layer) + 1)
                    x = 64 * (h % 2)
                    for t, (c0, n) in enumerate([(0, META + P), (META + P, L), (MASK, META)]):
                        d = dst[0:TILES[t][1], c0:c0 + n]
                        mm(d, tok_rows(qn[:, h, :], t), kn[:, h, 0:n], True, False)
                        mm(d, tok_rows(qpe[x:x + 64, h // 2, :], t), kpe[x:x + 64, 0:n], False, True,
                           sc_done if t == 2 else None)

                def pair(u):
                    if u == 0:
                        pe.wait_ge(swap_read, N_ROPES * (layer + 1))
                    elif u == 1:
                        pe.wait_ge(sc_free, HEADS * (layer + 1))
                    elif u < 6:
                        pe.wait_ge(pt_free, HEADS * layer + u - 1)
                    else:
                        pe.wait_ge(decayed, HEADS * layer + u - 5)
                    return bank[4 + 2 * (u % 2)], bank[5 + 2 * (u % 2)]

                def prob_transposes(h):
                    x, y = pair(h)
                    pe.wait_ge(p2_ready, HEADS * layer + h + 1)
                    p = p_of(h)
                    a, b, m = p[:, 0:META + P], p[:, META + P:MASK], p[0:META, MASK:MASK + META]
                    turn(x[:, 0:P], a[:, META:META + P])
                    turn(x[:, P:2 * P], b[:, META:META + P])
                    turn(x[:, 2 * P:3 * P], b[:, META + P:L])
                    turn(y[0:META, 0:META], m)
                    turn(y[0:META, META:META + P], a[:, 0:META])
                    turn(y[0:META, META + P:L], b[:, 0:META], pt_done)

                def retention_scores(h):
                    x, y = pair(HEADS + h)
                    mm(x[:, 0:2 * P], kT[:, h, META:META + P], qT[:, h, META:L], True, True)
                    mm(x[:, 2 * P:3 * P], kT[:, h, META + P:L], qT[:, h, META + P:L], True, True)
                    mm(y[0:META, 0:L], kT[:, h, 0:META], qT[:, h, :], True, True, rs_done)

                def weigh(name, u, vals):
                    h = u % HEADS
                    dst = rot_bank(name)
                    if u < HEADS:
                        pe.wait_ge(pt_free, HEADS * layer + h + 1)
                    else:
                        pe.wait_ge(decayed, HEADS * layer + h + 1)
                    if u == 0:
                        pe.wait_ge(out_free, o_("rv2", layer) + 1)
                    if u == 2 * HEADS - 1:
                        used_up.append((direct_used, 2))
                    c = slice(h * P, (h + 1) * P)
                    b = u % 2
                    mm(dst, vals[0:META, 2, c], STy[0:META, b, :], True, False)
                    mm(dst[:, META:L], vals[:, 0, c], STx[:, b, 0:2 * P], False, False)
                    mm(dst[:, META + P:L], vals[:, 1, c], STx[:, b, 2 * P:3 * P], False, True, out_done)

                def pack_sum(name, odd):
                    dst = rot_bank(name)
                    pe.wait_ge(out_free, o_("yR3" if odd else "yM3", layer) + 1)
                    for h in range(HEADS):
                        mm(dst, col(C_PACK + 96 - 32 * h), sq3[:, 2 * h + odd, :], h == 0, h == HEADS - 1,
                           out_done if h == HEADS - 1 else None)

                def spread(name):
                    odd, h = name[1] == "R", int(name[2])
                    dst = rot_bank(name)
                    pe.wait_ge(pack_ready, 2 * layer + odd + 1)
                    mm(dst, col(C_ROW + h * P), sq3[:, 2 * odd, :], True, True, out_done)

                proj_first(("ckv", "kpe"))
                proj("cq0", 1, 0)
                pe.wait_ge(const_in, 16)
                swap(0)
                proj("cq1", 1, 1)
                proj("q0", 2, 0)
                pe.wait_ge(out_free, o_("cq1", layer) + 1)
                ones_sum("sckv", [sq3[:, 0, :]])
                ones_sum("scq", [sq3[:, 1, :], sq3[:, 2, :]])
                for r, name in enumerate(ROPES[2:9], start=1):
                    proj(name, 2 + r // 2, r % 2)
                    swap(r)
                up_q("qpe0", 0)
                up_q("qpe1", 1)
                swap(8)
                for h in range(HEADS):
                    up_q(f"qn{h}", 2 + h)
                    if h in (0, 2):
                        swap(9 + h // 2)
                used_up.append((direct_used, 1))
                arrived(pe, u0 + U_UKV)
                w = slot(u0 + U_UKV)
                for h in range(HEADS):
                    mm(rot_bank(f"kn{h}"), w[:, h * P:(h + 1) * P], ckv, True, True, out_done)
                for t in range(3):
                    dst = rot_bank(f"v{t}", 512)[0:TILES[t][1], :]
                    mm(dst, tok_rows(ckv, t), w[:, 512:1024], True, True, out_done)
                used_up.append((direct_used, 1))
                latent_scores(0)
                latent_scores(1)
                for t in range(3):
                    p0 = TILES[t][0]
                    dst = rot_bank(f"rv{t}", 512)
                    for k in range(DK):
                        w = [x.rearrange("p (k c) -> p k c", k=4)[:, k % 4, :] for x in split(pe, u0 + U_RV + k // 4)]
                        mm3(dst, [hi[:, k, p0:p0 + P], lo[:, k, p0:p0 + P]], w, k == 0, k == DK - 1,
                            out_done if k == DK - 1 else None)
                    if t < 2:
                        latent_scores(2 + t)
                used_up.append((w_used, 2))
                prob_transposes(0)
                proj("g0", U_RG, 0)
                prob_transposes(1)
                weigh("yM0", 0, vm)
                proj("g1", U_RG, 1)
                prob_transposes(2)
                weigh("yM1", 1, vm)
                proj("g2", U_RG + 1, 0)
                prob_transposes(3)
                weigh("yM2", 2, vm)
                retention_scores(0)
                weigh("yM3", 3, vm)
                retention_scores(1)
                weigh("yR0", 4, rv)
                pack_sum("sM", 0)
                retention_scores(2)
                weigh("yR1", 5, rv)
                retention_scores(3)
                weigh("yR2", 6, rv)
                spread("bM0")
                spread("bM1")
                weigh("yR3", 7, rv)
                spread("bM2")
                spread("bM3")
                proj("g3", U_RG + 1, 1)
                pack_sum("sR", 1)

                def wo(d, heads, last):
                    w = [x.rearrange("p (k c) -> p k c", k=DK)[:, :, (d % 2) * P:(d % 2 + 1) * P]
                         for x in split(pe, u0 + U_WO + d // 2)]
                    for k in heads:
                        if d == 0 and k < HEADS:
                            pe.wait_ge(mix_ready, 5 * layer + 2 + k)
                        m = [x[:, k % 4, p0:L] for x in ((hi, lo) if k < HEADS else (mla_hi, mla_lo))]
                        mm3(bank[(d + 4) % 8][:, p0:L], [x[:, k, :] for x in w], m,
                            k == 4, last and k == 3, wo_done if last and k == 3 else None)
                    if last and d % 2:
                        used_up.append((w_used, 1))

                p0 = 0 if layer == 0 else META
                latent, retained = range(4, 8), range(4)
                pe.wait_ge(decayed, HEADS * (layer + 1))
                pe.wait_ge(mix_ready, 5 * layer + 1)
                for d in range(3):
                    wo(d, latent, False)
                for h in range(HEADS):
                    spread(f"bR{h}")
                wo(3, latent, False)
                pe.wait_ge(out_free, (layer + 1) * N_OUTS)
                wo(4, latent, False)
                wo(5, latent, False)
                for d in range(6):
                    wo(d, retained, True)
                wo(6, [*latent, *retained], True)
                if layer == 0:
                    square_sum(1, range(5))
                else:
                    tokens(0)
                wo(7, [*latent, *retained], True)
                if layer == 0:
                    square_sum(1, range(5, DK))
                    keep_clock(16)
                else:
                    tokens(1)

            def tokens(part):
                added = 8 + DK * CHUNKS
                k0, k1 = (0, 6) if part == 0 else (6, 8)
                if part == 0:
                    pe.wait_ge(rw_ready, 1)
                for k in range(k0, k1):
                    pe.wait_ge(h_added, added + k + 1)
                    if k == 0:
                        pe.wait_ge(h_added, added + 6)
                    for t in range(2):
                        p0 = TILES[t][0]
                        mm(bank[t][:, 0:EXPERTS], hT[:, k, p0:p0 + P], rw_gain[:, k, :],
                           k == 0, k == DK - 1, lg_done if t == 1 and k == DK - 1 else None)
                for t in range(2):
                    p0 = TILES[t][0]
                    for i in range(4):
                        turn(bank[4 + 2 * part + t][:, i * P:(i + 1) * P], hT[:, part * 4 + i, p0:p0 + P],
                             tok_done if i == 3 else None)

            def dense():
                def gate_up(c):
                    if c >= 1:
                        pe.wait_ge(af_ready, c)
                    for j, kind in enumerate("gu"):
                        w = [x.rearrange("p (k c) -> p k c", k=DK) for x in split(pe, DENSE_AT + FFN_POS[kind, c])]
                        first = c == 0 and j == 0
                        for g, (k0, k1) in enumerate(GROUPS if first else [(0, DK)]):
                            if first:
                                pe.wait_ge(hn_ready, len(GROUPS) + g + 1)
                            for f in range(2):
                                for k in range(k0, k1):
                                    last = f == 1 and k == DK - 1 and j == 1
                                    mm3(bank[2 * j + f][:, 0:L], [x[:, k, f * P:(f + 1) * P] for x in w],
                                        [hi[:, k, :], lo[:, k, :]], k == 0, k == DK - 1, gu_done if last else None)
                        used_up.append((w_used, 1))

                def down(c):
                    w = [x.rearrange("p (f n) -> p f n", f=2) for x in split(pe, DENSE_AT + FFN_POS["d", c])]
                    pe.wait_ge(a_ready, c + 1)
                    for d in range(DK):
                        if c == CHUNKS - 1 and d == DK - 1:
                            square_sum(2, range(4))
                        if c or d >= 4:
                            pe.wait_ge(h_added, 8 + c * DK + d - 3)
                        for f in range(2):
                            mm3(bank[4 + d % 4][:, 0:L], [x[:, f, d * P:(d + 1) * P] for x in w],
                                [ad_hi[c % 2][:, f, :], ad_lo[c % 2][:, f, :]], f == 0, f == 1, d_done if f == 1 else None)
                    used_up.append((w_used, 1))

                gate_up(0)
                for c in range(1, CHUNKS):
                    gate_up(c)
                    down(c - 1)
                down(CHUNKS - 1)
                square_sum(2, range(4, DK))
                keep_clock(16)

            def routing():
                pe.wait_ge(sel_ready, 1)
                pe.wait_ge(h_added, 16 + DK * CHUNKS)
                b = bank[2]
                mm(b[:, 0:8], tri, sel[:, 0, :], True, True)
                mm(b[:, 8:16], ones, sel[:, 0, :], True, False)
                mm(b[:, 8:16], tri, sel[:, 1, :], False, True)
                mm(b[:, 16:24], ones, sel[:, 0, :], True, False)
                mm(b[:, 16:24], ones, sel[:, 1, :], False, True, pos_done)

            def gather(n):
                if isinstance(n, int):
                    pe.wait_ge(tok_free, 4)
                pe.wait_ge(g_ready, n + 1)
                for d in range(DK):
                    if isinstance(n, int) and d % 4 == 0:
                        pe.wait_ge(tokhn_ready, 2 * (d // 4) + 2)
                    for t in range(2):
                        mm(bank[7 - d // 4][:, (d % 4) * CAP:(d % 4 + 1) * CAP], hn_tok[:, t, d * P:(d + 1) * P],
                           G[:, t, :], t == 0, t == 1, gt_done if d % 4 == 3 and t == 1 else None)

            def scatter_out(it, j):
                t, half = j // 2, j % 2
                if j == 0:
                    pe.wait_ge(ye_ready, it + 1)
                    pe.wait_ge(gwt_ready, it + 1)
                if j >= 2:
                    pe.wait_ge(acc_added, it * 4 + j)
                mm(bank[7 - half][:, :], GWT[:, t * P:(t + 1) * P], ye[:, half * 512:(half + 1) * 512],
                   True, True, sc_out)

            def expert(it):
                def ready(key):
                    m = MOE_SPLIT + MOE_ORDER.index(key)
                    pe.wait_ge(split_lo, it * FFN_UNITS + (m + 1))
                    return w_hi[:, m % HSLOTS, :], w_lo[:, m % HSLOTS, :]

                def into(kind, c):
                    dst = bank[(0 if kind == "g" else 2) + c % 2]
                    for i in range(2):
                        w = [x.rearrange("p (k c) -> p k c", k=4) for x in ready((kind, c, i))]
                        for kk in range(4):
                            k = 4 * i + kk
                            last = k == DK - 1
                            mm3(dst[:, :], [x_hi[:, k, :], x_lo[:, k, :]], [x[:, kk, :] for x in w], k == 0, last,
                                e_gu if last and kind == "u" else None)
                        used_up.append((w_used, 1))

                def turn_hidden(c):
                    pe.wait_ge(e_af, it * MOE_CHUNKS + c + 1)
                    if c == 0:
                        pe.wait_ge(acc_added, it * 4 + 5)
                    for f in range(4):
                        turn(bank[6 if c < MOE_CHUNKS - 1 else 3][:, f * CAP:(f + 1) * CAP], a_moe[:, f * P:(f + 1) * P],
                             at_done if f == 3 else None)

                def down(c):
                    for i in range(2):
                        w = [x.rearrange("p (f n) -> p f n", f=2) for x in ready(("d", c, i))]
                        if i == 0:
                            pe.wait_ge(e_a, it * MOE_CHUNKS + c + 1)
                        for ff in range(2):
                            f = 2 * i + ff
                            a = [x[c % 2][:, f * CAP:(f + 1) * CAP] for x in (ae_hi, ae_lo)]
                            for half in range(2):
                                end = c == MOE_CHUNKS - 1 and f == 3
                                mm3(bank[4 + half][:, :], a, [x[:, ff, half * 512:(half + 1) * 512] for x in w],
                                    c == 0 and f == 0, end, w_used if end and half == 1 else None)
                        if not (c == MOE_CHUNKS - 1 and i == 1):
                            used_up.append((w_used, 1))

                pe.wait_ge(xg_ready, it + 1)
                into("g", 0)
                scatter_out(it, 0)
                scatter_out(it, 1)
                into("u", 0)
                scatter_out(it, 2)
                scatter_out(it, 3)
                for c in range(1, MOE_CHUNKS):
                    into("g", c)
                    if c == 3:
                        pe.wait_ge(gwt_in, it + 1)
                        for t in range(2):
                            turn(bank[7][:, t * P:(t + 1) * P], GW[:, t, :], gwt_done if t else None)
                    turn_hidden(c - 1)
                    into("u", c)
                    if c == MOE_CHUNKS - 1:
                        pe.wait_ge(gwt_ready, it + 2)
                        pe.wait_ge(e_a, it * MOE_CHUNKS + c)
                        gather(it + 1)
                        turn_hidden(c)
                    down(c - 1)
                down(MOE_CHUNKS - 1)
                assert not used_up

            pe.wait_ge(ones_set, 4)
            keep_clock(10)
            square_sum(0, range(DK))
            keep_clock(24)
            attention(0)
            dense()
            attention(1)
            routing()
            keep_clock(8, 3)
            gather(0)
            pe.wait_ge(rounds_ready, 1)
            rounds = pe.value_load(rounds_sb[0:1, 0:1], min_val=1, max_val=2)
            with pe.Fori(0, rounds) as r:
                with pe.Fori(0, EXPERTS) as e:
                    expert(r * EXPERTS + e)
            its = rounds * EXPERTS
            for j in range(4):
                scatter_out(its, j)

        @block.scalar
        def _(act):
            A = nc.scalar.activation

            def high(n):
                arrived(act, UNIT_OF[n])
                if n >= HSLOTS:
                    act.wait_ge(w_used, n - HSLOTS + 1)
                A(w_hi[:, n % HSLOTS, :], slot(UNIT_OF[n]), ACT.Copy).then_inc(split_hi, 1)

            def norm(n, late=(), mid=(), after=()):
                act.wait_ge(ones_set, 4)
                if n == 0:
                    A(warm[:, :], eps_sb[:, :], ACT.Sqrt)
                for k in range(DK):
                    if late and k in (2, 4):
                        high(late[k // 2 - 1])
                    if n == 0:
                        if k % 4 == 0:
                            act.wait_ge(x_in[k // 4], 16)
                    else:
                        act.wait_ge(h_added, [0, 0, 8 + DK * (CHUNKS - 1)][n] + k + 1)
                    A(sq3[:, k, :], hT[:, k, :], ACT.Square).then_inc(sq_ready, 1)
                    if k == 5 and n:
                        A(warm[:, :], eps_sb[:, :], ACT.Sqrt)
                act.wait_ge(ms_done, n + 1)
                A(std[:, 0, :], norm_bank(n)[:, 0:L], ACT.Sqrt, bias=eps_sb[:, 0:1], scale=1.0 / D).then_inc(std_ready, 1)
                for u in mid:
                    high(u)
                for k0, k1 in GROUPS:
                    act.wait_ge(hnf_ready, n * DK + k1)
                    A(hi[:, k0:k1, :], sq3[:, k0:k1, :], ACT.Copy).then_inc(hi_ready, 1)
                for u in after:
                    high(u)

            def attention(layer):
                def src(name, rows=P, cols=L):
                    o = o_(name, layer)
                    act.wait_ge(out_done, o + 1)
                    return bank[o % 4][0:rows, 0:cols]

                b = SPLIT_OF[base_of(layer)]

                def keep(name, dst, rows=P, cols=L):
                    A(dst, src(name, rows, cols), ACT.Copy).then_inc(out_free, 1)

                def keep_square(name, dst, sq_dst):
                    s = src(name)
                    A(dst, s, ACT.Copy)
                    A(sq_dst, s, ACT.Square).then_inc(out_free, 1)

                def root(name, dst, n):
                    A(dst, src(name), ACT.Sqrt, bias=eps_sb[:, 0:1], scale=1.0 / n).then_inc(out_free, 1)

                def keep_raw(name):
                    r = ROPES.index(name)
                    if r >= 3:
                        act.wait_ge(rope_done, layer * N_ROPES + r - 2)
                    keep(name, raw[:, r % 3, :])

                def exps(h):
                    act.wait_ge(p1_ready, HEADS * layer + h + 1)
                    p = p_of(h)
                    for t, (rows, c0, c1) in enumerate([(P, 0, META + P), (P, META + P, MASK), (META, MASK, MASK + META)]):
                        x = A(p[0:rows, c0:c1], p[0:rows, c0:c1], ACT.Exp, bias=nmx[0:rows, h, t:t + 1], scale=SCALE,
                              accum_out=sums[0:rows, h, t:t + 1])
                    x.then_inc(exp_done, 1)

                def tables(h):
                    act.wait_ge(pt_done, HEADS * layer + h + 1)
                    x, y = bank[4 + 2 * (h % 2)], bank[5 + 2 * (h % 2)]
                    A(STx[:, h % 2, :], x[:, 0:3 * P], ACT.Copy)
                    A(STy[0:META, h % 2, :], y[0:META, 0:L], ACT.Copy).then_inc(pt_free, 1)

                keep_square("ckv", ckv, sq3[:, 0, :])
                keep_raw("kpe")
                high(b + 3)
                keep_square("cq0", cq[:, 0, :], sq3[:, 1, :])
                keep_square("cq1", cq[:, 1, :], sq3[:, 2, :])
                high(b + 4)
                keep_raw("q0")
                root("sckv", std[:, 0, :], KVR)
                root("scq", std[:, 1, :], QR)
                for name in ROPES[2:]:
                    keep_raw(name)
                    if name in ("q1", "q3", "k1", "k3"):
                        high(b + 5 + ["q1", "q3", "k1", "k3"].index(name))
                for h in range(HEADS):
                    keep(f"qn{h}", qn[:, h, :])
                for h in range(HEADS):
                    keep(f"kn{h}", kn[:, h, :])
                for t, (_, rows) in enumerate(TILES):
                    keep(f"v{t}", vm[0:rows, t, :], rows, 512)
                exps(0)
                exps(1)
                for t, (_, rows) in enumerate(TILES):
                    keep(f"rv{t}", rv[0:rows, t, :], rows, 512)
                    if t < 2:
                        exps(2 + t)
                high(b + 9)
                for name in OUTS[OUTS.index("g0"):]:
                    h = int(name[-1]) if name[-1].isdigit() else 0
                    if name[0] == "g":
                        keep(name, rg[:, h, :])
                        if h == 0:
                            tables(0)
                            tables(1)
                        elif h < 3:
                            tables(h + 1)
                    elif name[:2] == "yM":
                        keep_square(name, qn[:, h, :], sq3[:, 2 * h, :])
                    elif name[:2] == "yR":
                        keep_square(name, qT[:, h, :], sq3[:, 2 * h + 1, :])
                    elif name[0] == "b":
                        keep(name, std[:, h, :])
                    else:
                        root(name, sq3[:, 2 * (name == "sR"), :], P)
                    if name == "yM0":
                        high(b + 10)
                    elif name == "yM1":
                        high(b + 11)
                    elif name == "bM3":
                        act.wait_ge(mixf_ready, 5 * layer + 1)
                        A(mla_hi, qn[:, :, :], ACT.Copy).then_inc(mix_hi, 1)
                    elif name == "sR":
                        high(b + 12)
                        act.wait_ge(out_free, o_("g3", layer) + 1)
                        A(rg[:, :, :], rg[:, :, :], ACT.Silu).then_inc(silu_g, 1)
                for h in range(HEADS):
                    act.wait_ge(mixf_ready, 5 * layer + 2 + h)
                    A(hi[:, h, :], qT[:, h, :], ACT.Copy).then_inc(mix_hi, 1)

            def dense():
                for m, (kind, c) in enumerate(FFN_ORDER):
                    n = SPLIT_OF[DENSE_AT] + m + HSLOTS
                    if kind == "u":
                        act.wait_ge(gu_done, c + 1)
                        A(sil_dense[:, 0, :], bank[0][:, 0:L], ACT.Silu)
                        A(sil_dense[:, 1, :], bank[1][:, 0:L], ACT.Silu).then_inc(silu_done, 1)
                        act.wait_ge(af_ready, c + 1)
                        A(ad_hi[c % 2], a_dense, ACT.Copy).then_inc(a_hi_ready, 1)
                    if m < FFN_UNITS - 1:
                        high(n)

            def turn_copies():
                def copy(n):
                    part, t = n // 2, n % 2
                    A(acc[:, t, part * 512:(part + 1) * 512], bank[4 + n][:, :], ACT.Copy).then_inc(tok_free, 1)

                def square(n):
                    part, t = n // 2, n % 2
                    act.wait_ge(tok_done, n + 1)
                    A(sq[:, n * 512:(n + 1) * 512], bank[4 + n][:, :], ACT.Square,
                      accum_out=dev_tok[:, t, part:part + 1]).then_inc(tok_square, 1)

                for n in range(2):
                    square(n)
                    copy(n)
                A(warm[:, :], eps_sb[:, :], ACT.Sqrt)
                square(2)
                square(3)
                act.wait_ge(tok_sum, 1)
                A(dev_tok[:, :, 2:3], dev_tok[:, :, 2:3], ACT.Sqrt, bias=eps_sb[:, 0:1], scale=1.0 / D).then_inc(tok_std, 1)
                copy(2)
                copy(3)

            def scatter_copy(it):
                act.wait_ge(w_used, it * FFN_UNITS + MOE_SPLIT)
                A(ye[:, 0:512], bank[4][:, :], ACT.Copy)
                A(ye[:, 512:1024], bank[5][:, :], ACT.Copy).then_inc(ye_ready, 1)

            def take(n):
                for j in range(2):
                    act.wait_ge(gt_done, n * 2 + j + 1)
                    A(x_hi[:, 4 * j:4 * j + 4, :], bank[7 - j][:, :].rearrange("p (a b) -> p a b", a=4), ACT.Copy).then_inc(e_xhi, 1)

            def expert(it):
                def high_of(m):
                    n = MOE_SPLIT + m
                    act.wait_ge(slot_in[m % MOE_SLOTS], it * (16 * FFN_UNITS // MOE_SLOTS) + moe_arrivals(m))
                    act.wait_ge(w_used, it * FFN_UNITS + (n - HSLOTS + 1))
                    A(w_hi[:, n % HSLOTS, :], moe_slot(m), ACT.Copy).then_inc(split_hi, 1)

                def hidden(c):
                    act.wait_ge(at_done, it * MOE_CHUNKS + c + 1)
                    A(ae_hi[c % 2], bank[6 if c < MOE_CHUNKS - 1 else 3][:, :], ACT.Copy).then_inc(e_ahi, 1)

                scatter_copy(it)
                high_of(AHEAD)
                for m, (kind, c, i) in enumerate(MOE_ORDER[:-1]):
                    if (kind, i) == ("u", 1):
                        act.wait_ge(e_gu, it * MOE_CHUNKS + c + 1)
                        A(sil_moe, bank[c % 2][:, :], ACT.Silu).then_inc(e_silu, 1)
                    high_of(m + HSLOTS)
                    if (kind, i) == ("g", 1) and c:
                        hidden(c - 1)
                    if (kind, c, i) == ("u", MOE_CHUNKS - 1, 1):
                        take(it + 1)
                        hidden(c)

            norm(0, mid=(0,), after=range(1, HSLOTS))
            attention(0)
            n = SPLIT_OF[DENSE_AT]
            norm(1, late=(n - 1, n), mid=(n + 1,), after=(n + 2,))
            dense()
            norm(2, after=(SPLIT_OF[ATTN1_AT] + 2,))
            attention(1)
            high(MOE_SPLIT - 1)
            for n in range(AHEAD):
                high(MOE_SPLIT + n)
            turn_copies()
            act.wait_ge(gexp_in, 1)
            A(v12[:, :, 2:3], v12[:, :, 2:3], ACT.Exp).then_inc(gexp_out, 1)
            A(warm[:, :], eps_sb[:, :], ACT.Silu)
            take(0)
            act.wait_ge(y_zero, 1)
            act.wait_ge(rounds_ready, 1)
            rounds = act.value_load(rounds_sb[0:1, 0:1], min_val=1, max_val=2)
            with act.Fori(0, rounds) as r:
                with act.Fori(0, EXPERTS) as e:
                    expert(r * EXPERTS + e)
            its = rounds * EXPERTS
            scatter_copy(its)
            A(warm[:, :], eps_sb[:, :], ACT.Sqrt)
            for t in range(2):
                act.wait_ge(acc_added, its * 4 + (2 * t + 3))
                A(res[:, t, :], acc[:, t, :], ACT.Square, accum_out=fin[:, t, 0:1]).then_inc(fsq, 1)
                act.wait_ge(fsq, t + 1)
                A(fin[:, t, 1:2], fin[:, t, 0:1], ACT.Sqrt, bias=eps_sb[:, 0:1], scale=1.0 / D).then_inc(fstd, 1)

        @block.vector
        def _(dve):
            V = nc.vector
            chain = [0]

            def link(ins, inc=None):
                if inc is not None:
                    ins.then_inc(inc, 1)
                    dve.wait_ge(inc, 1)
                    return
                chain[0] += 1
                ins.then_inc(link_sem, 1)
                dve.wait_ge(link_sem, chain[0])

            def low(n):
                dve.wait_ge(split_hi, n + 1)
                V.tensor_tensor(w_lo[:, n % HSLOTS, :], slot(UNIT_OF[n]), w_hi[:, n % HSLOTS, :].bitcast(F32),
                                ALU.subtract).then_inc(split_lo, 1)

            def norm(n, after):
                dve.wait_ge(std_ready, n + 1)
                link(V.reciprocal(std[:, 0, :], std[:, 0, :]))
                g0 = (G_ATTN if n % 2 == 0 else G_FFN) + DK * (n // 2)

                def rest(g):
                    k0, k1 = GROUPS[g]
                    dve.wait_ge(hi_ready, n * len(GROUPS) + g + 1)
                    V.tensor_tensor(lo[:, k0:k1, :], sq3[:, k0:k1, :], hi[:, k0:k1, :].bitcast(F32),
                                    ALU.subtract).then_inc(hn_ready, 1)

                for g, (k0, k1) in enumerate(GROUPS):
                    for k in range(k0, k1):
                        V.scalar_tensor_tensor(out=sq3[:, k, :], in0=hT[:, k, :], scalar=gain(g0 + k), in1=std[:, 0, :],
                                               op0=ALU.mult, op1=ALU.mult).then_inc(hnf_ready, 1)
                    if g:
                        rest(g - 1)
                    if n == 0 and g == 1:
                        low(0)
                rest(len(GROUPS) - 1)
                for u in after:
                    low(u)

            def attention(layer):
                u0 = base_of(layer)
                b = SPLIT_OF[u0]

                def rope(r):
                    name = ROPES[r]
                    if name == "kpe":
                        dst = kpe
                    elif name.startswith("qpe"):
                        dst = qpe[:, int(name[3]), :]
                    else:
                        dst = (qT if name[0] == "q" else kT)[:, int(name[1]), :]
                    cos, sin = (C_COS64, C_SIN64) if "pe" in name else (C_COS, C_SIN)
                    dve.wait_ge(out_free, o_(name, layer) + 1)
                    V.tensor_tensor(dst, raw[:, r % 3, :], col(cos, L), ALU.mult).then_inc(link_sem, 1)
                    chain[0] += 1
                    dve.wait_ge(swap_done, layer * N_ROPES + r + 1)
                    if layer or r:
                        dve.wait_ge(rope_done, layer * N_ROPES + r)
                    V.tensor_tensor(rot, bank[4 + r % 2][:, 0:L], col(sin, L), ALU.mult).then_inc(swap_read, 1)
                    dve.wait_ge(link_sem, chain[0])
                    dve.wait_ge(swap_read, layer * N_ROPES + r + 1)
                    V.tensor_tensor(dst, dst, rot, ALU.add).then_inc(rope_done, 1)

                def latent_norm():
                    dve.wait_ge(out_free, o_("scq", layer) + 1)
                    link(V.reciprocal(std[:, 0:2, :], std[:, 0:2, :]))
                    for x, g, s in [(ckv, G_KV + layer, 0), (cq[:, 0, :], G_Q + 2 * layer, 1), (cq[:, 1, :], G_Q + 2 * layer + 1, 1)]:
                        V.scalar_tensor_tensor(out=x, in0=x, scalar=gain(g), in1=std[:, s, :],
                                               op0=ALU.mult, op1=ALU.mult).then_inc(c_ready, 1)

                def mask_max(h):
                    dve.wait_ge(sc_done, HEADS * layer + h + 1)
                    ps, p = bank[6 + h % 2], p_of(h)
                    mask = slot(u0 + U_T1)[:, HEADS * DECAY:HEADS * DECAY + MASK]
                    link(V.tensor_tensor(p[:, 0:MASK], ps[:, 0:MASK], mask, ALU.add))
                    V.tensor_copy(p[0:META, MASK:MASK + META], ps[0:META, MASK:MASK + META]).then_inc(sc_free, 1)
                    dve.wait_ge(sc_free, HEADS * layer + h + 1)
                    for t, (rows, c0, c1) in enumerate([(P, 0, META + P), (P, META + P, MASK), (META, MASK, MASK + META)]):
                        link(V.tensor_reduce(nmx[0:rows, h, t:t + 1], p[0:rows, c0:c1], axis=AX.X, op=ALU.max))
                    V.tensor_scalar(nmx[:, h, :], nmx[:, h, :], -SCALE, None, ALU.mult).then_inc(p1_ready, 1)

                def normalise(h):
                    dve.wait_ge(exp_done, HEADS * layer + h + 1)
                    link(V.reciprocal(sums[:, h, :], sums[:, h, :]))
                    p = p_of(h)
                    for t, (rows, c0, c1) in enumerate([(P, 0, META + P), (P, META + P, MASK), (META, MASK, MASK + META)]):
                        x = V.tensor_scalar(p[0:rows, c0:c1], p[0:rows, c0:c1], sums[0:rows, h, t:t + 1], None, ALU.mult)
                    x.then_inc(p2_ready, 1)

                def decay(h):
                    dve.wait_ge(rs_done, HEADS * layer + h + 1)
                    s = h % 2
                    t1, t2 = slot(u0 + U_T1), slot(u0 + U_T2)
                    V.tensor_tensor(STx[:, s, :], bank[4 + 2 * s][:, 0:3 * P], t1[:, h * DECAY:(h + 1) * DECAY], ALU.mult)
                    V.tensor_tensor(STy[0:META, s, :], bank[5 + 2 * s][0:META, 0:L], t2[0:META, h * L:(h + 1) * L],
                                    ALU.mult).then_inc(decayed, 1)

                def rest(j):
                    dve.wait_ge(mix_hi, 5 * layer + j + 1)
                    if j == 0:
                        dst, full, high_part = mla_lo, qn[:, :, :], mla_hi
                    else:
                        dst, full, high_part = lo[:, j - 1, :], qT[:, j - 1, :], hi[:, j - 1, :]
                    V.tensor_tensor(dst, full, high_part.bitcast(F32), ALU.subtract).then_inc(mix_ready, 1)

                for n in range(1, HSLOTS) if layer == 0 else ():
                    low(n)
                dve.wait_ge(const_in, 16)
                rope(0)
                low(b + 3)
                latent_norm()
                low(b + 4)
                rope(1)
                low(b + 5)
                rope(2)
                rope(3)
                low(b + 6)
                rope(4)
                rope(5)
                low(b + 7)
                rope(6)
                rope(7)
                low(b + 8)
                for r in range(8, N_ROPES):
                    rope(r)
                dve.wait_ge(ones_set, 4)
                arrived(dve, u0 + U_T1)
                for h in range(HEADS):
                    mask_max(h)
                for h in range(HEADS):
                    normalise(h)
                low(b + 9)
                low(b + 10)
                low(b + 11)
                arrived(dve, u0 + U_T2)
                decay(0)
                decay(1)
                dve.wait_ge(out_free, o_("sM", layer) + 1)
                V.reciprocal(sq3[:, 0, :], sq3[:, 0, :]).then_inc(pack_ready, 1)
                decay(2)
                decay(3)
                for h in range(HEADS):
                    m = qn[:, h, :]
                    dve.wait_ge(out_free, o_(f"bM{h}", layer) + 1)
                    x = V.scalar_tensor_tensor(out=m, in0=m, scalar=gain(G_MLA + 4 * layer + h), in1=std[:, h, :],
                                               op0=ALU.mult, op1=ALU.mult)
                x.then_inc(mixf_ready, 1)
                rest(0)
                dve.wait_ge(out_free, o_("sR", layer) + 1)
                V.reciprocal(sq3[:, 2, :], sq3[:, 2, :]).then_inc(pack_ready, 1)
                low(b + 12)
                dve.wait_ge(silu_g, layer + 1)
                for h in range(HEADS):
                    m = qT[:, h, :]
                    x = V.scalar_tensor_tensor(out=m, in0=m, scalar=gain(G_RET + 4 * layer + h), in1=rg[:, h, :],
                                               op0=ALU.mult, op1=ALU.mult)
                link(x)

                for h in range(HEADS):
                    dve.wait_ge(out_free, o_(f"bR{h}", layer) + 1)
                    V.tensor_tensor(qT[:, h, :], qT[:, h, :], std[:, h, :], ALU.mult).then_inc(mixf_ready, 1)
                    if h:
                        rest(h)
                rest(HEADS)
                p0 = 0 if layer == 0 else META
                for d in range(DK):
                    dve.wait_ge(wo_done, DK * layer + d + 1)
                    V.tensor_tensor(hT[:, d, p0:L], hT[:, d, p0:L], bank[(d + 4) % 8][:, p0:L], ALU.add).then_inc(h_added, 1)
                    if d in (2, 4) or (d == 6 and layer == 1):
                        low(b + 12 + d // 2)

            def dense():
                def add(c, ds):
                    for d in ds:
                        dve.wait_ge(d_done, c * DK + d + 1)
                        if d == 0:
                            dve.wait_ge(h_added, 8 + c * DK)
                        V.tensor_tensor(hT[:, d, :], hT[:, d, :], bank[4 + d % 4][:, 0:L], ALU.add).then_inc(h_added, 1)

                for m, (kind, c) in enumerate(FFN_ORDER):
                    n = SPLIT_OF[DENSE_AT] + m + HSLOTS
                    if kind == "u":
                        dve.wait_ge(silu_done, c + 1)
                        if c:
                            dve.wait_ge(a_ready, c)
                        V.tensor_tensor(a_dense[:, 0, :], bank[2][:, 0:L], sil_dense[:, 0, :], ALU.mult)
                        V.tensor_tensor(a_dense[:, 1, :], bank[3][:, 0:L], sil_dense[:, 1, :], ALU.mult).then_inc(af_ready, 1)
                        if c:
                            add(c - 1, range(4))
                        dve.wait_ge(a_hi_ready, c + 1)
                        V.tensor_tensor(ad_lo[c % 2], a_dense, ad_hi[c % 2].bitcast(F32), ALU.subtract).then_inc(a_ready, 1)
                        if c:
                            add(c - 1, range(4, 8))
                    if m < FFN_UNITS - 2:
                        low(n)
                add(CHUNKS - 1, range(DK))

            def routing():
                E = EXPERTS
                dve.wait_ge(lg_done, 1)
                for t in range(2):
                    x = V.tensor_copy(logit[:, t, :], bank[t][:, 0:E])
                link(x)
                la = logit.unsqueeze(2).to_broadcast([P, 2, E, E])
                lb = logit.unsqueeze(3).to_broadcast([P, 2, E, E])
                low = col(C_LOW, E * E).rearrange("p (a b) -> p a b", a=E).unsqueeze(1).to_broadcast([P, 2, E, E])
                ca, cb = [x.rearrange("p (t a) b -> p t a b", t=2) for x in (cmp_a, cmp_b)]
                V.tensor_tensor(ca, la, lb, ALU.is_gt)
                link(V.tensor_tensor(cb, la, lb, ALU.is_equal))
                link(V.tensor_tensor(cb, cb, low, ALU.mult))
                link(V.tensor_tensor(ca, ca, cb, ALU.add))
                link(V.tensor_reduce(rank, ca, axis=AX.X, op=ALU.add))
                link(V.tensor_scalar(sel, rank, 2.0, None, ALU.is_lt), sel_ready)
                V.tensor_scalar(far, sel, -4096.0, 4096.0, ALU.mult, ALU.add)
                V.tensor_scalar(oh1, rank, 0.0, None, ALU.is_equal)
                link(V.tensor_scalar(oh2, rank, 1.0, None, ALU.is_equal))
                dve.wait_ge(tok_square, 4)
                V.tensor_tensor(dev_tok[:, :, 2:3], dev_tok[:, :, 0:1], dev_tok[:, :, 1:2], ALU.add).then_inc(tok_sum, 1)
                dve.wait_ge(pos_done, 1)
                for t in range(2):
                    x = V.tensor_tensor(route[:, 0:E, t], far[:, t, :], bank[2][:, t * E:(t + 1) * E], ALU.add)
                link(x)
                for t in range(2):
                    x = V.tensor_scalar(G[:, t, :], col(C_IOTA, CAP), route[:, 0, t:t + 1], None, ALU.is_equal)
                x.then_inc(g_ready, 1)
                dve.wait_ge(tok_std, 1)
                link(V.reciprocal(dev_tok[:, :, 3:4], dev_tok[:, :, 2:3]))
                dve.wait_ge(gain_in, 16)
                for half in range(2):
                    dve.wait_ge(tok_free, 2 * half + 2)
                    for t in range(2):
                        s = slice(half * 512, (half + 1) * 512)
                        V.scalar_tensor_tensor(out=hn_tok[:, t, s], in0=acc[:, t, s], scalar=dev_tok[:, t, 3:4],
                                               in1=gain_row[:, s], op0=ALU.mult, op1=ALU.mult).then_inc(tokhn_ready, 1)
                link(V.tensor_reduce(cnt[:, 0:1], bank[2][:, 16:24], axis=AX.X, op=ALU.max))
                V.tensor_scalar(rounds_sb[:, 0:1], cnt[:, 0:1], float(CAP), 1.0, ALU.is_gt, ALU.add).then_inc(rounds_ready, 1)
                for i, oh in ((0, oh1), (1, oh2)):
                    link(V.tensor_tensor(gate, oh, logit, ALU.mult))
                    link(V.tensor_reduce(v12[:, :, i:i + 1], gate, axis=AX.X, op=ALU.add))
                link(V.tensor_tensor(v12[:, :, 2:3], v12[:, :, 1:2], v12[:, :, 0:1], ALU.subtract))
                V.tensor_tensor(v12[:, :, 2:3], v12[:, :, 2:3], dev_tok[:, :, 3:4], ALU.mult).then_inc(gexp_in, 1)
                link(V.memset(bank[4][:, :], 0.0))
                V.memset(bank[5][:, :], 0.0).then_inc(y_zero, 1)
                V.memset(GWT, 0.0).then_inc(gwt_ready, 1)
                V.memset(cnt, 0.0).then_inc(acc_added, 1)
                take(0)
                dve.wait_ge(gexp_out, 1)
                link(V.tensor_scalar(v12[:, :, 3:4], v12[:, :, 2:3], 1.0, None, ALU.add))
                link(V.reciprocal(v12[:, :, 3:4], v12[:, :, 3:4]))
                link(V.tensor_tensor(v12[:, :, 2:3], v12[:, :, 2:3], v12[:, :, 3:4], ALU.mult))
                for t in range(2):
                    link(V.tensor_scalar(oh1[:, t, :], oh1[:, t, :], v12[:, t, 3:4], None, ALU.mult))
                    link(V.scalar_tensor_tensor(out=route[:, 0:E, 2 + t], in0=oh2[:, t, :], scalar=v12[:, t, 2:3], in1=oh1[:, t, :],
                                                op0=ALU.mult, op1=ALU.add))
                V.tensor_scalar(route[:, E, 0:2], route[:, 0, 0:2], -float(CAP), None, ALU.add)
                link(V.tensor_copy(route[:, E, 2:4], route[:, 0, 2:4]))

            def one_hot(lk, entry):
                lk(V.tensor_copy(nxt, entry))
                V.tensor_scalar(G[:, 0, :], col(C_IOTA, CAP), nxt[:, 0:1], None, ALU.is_equal)
                return V.tensor_scalar(G[:, 1, :], col(C_IOTA, CAP), nxt[:, 1:2], None, ALU.is_equal)

            def take(n):
                for j in range(2):
                    dve.wait_ge(e_xhi, n * 2 + j + 1)
                    d = slice(4 * j, 4 * j + 4)
                    x = V.tensor_tensor(x_lo[:, d, :], bank[7 - j][:, :].rearrange("p (a b) -> p a b", a=4),
                                        x_hi[:, d, :].bitcast(F32), ALU.subtract)
                x.then_inc(xg_ready, 1)

            def add_out(it, j):
                dve.wait_ge(sc_out, it * 4 + (j + 1))
                t, half = j // 2, j % 2
                a = acc[:, t, half * 512:(half + 1) * 512]
                V.tensor_tensor(a, a, bank[7 - half][:, :], ALU.add).then_inc(acc_added, 1)

            LINKS = 2

            def expert(it, e):
                links = [0]

                def lk(ins):
                    links[0] += 1
                    ins.then_inc(e_link, 1)
                    dve.wait_ge(e_link, it * LINKS + links[0])

                def low_of(m):
                    n = MOE_SPLIT + m
                    dve.wait_ge(split_hi, it * FFN_UNITS + (n + 1))
                    V.tensor_tensor(w_lo[:, n % HSLOTS, :], moe_slot(m), w_hi[:, n % HSLOTS, :].bitcast(F32),
                                    ALU.subtract).then_inc(split_lo, 1)

                def hidden(c):
                    dve.wait_ge(e_ahi, it * MOE_CHUNKS + c + 1)
                    V.tensor_tensor(ae_lo[c % 2], bank[6 if c < MOE_CHUNKS - 1 else 3][:, :], ae_hi[c % 2].bitcast(F32),
                                    ALU.subtract).then_inc(e_a, 1)

                low_of(AHEAD)
                lk(V.tensor_copy(cur, route[:, e, :]))
                for t in range(2):
                    x = V.tensor_scalar(GW[:, t, :], col(C_IOTA, CAP), cur[:, t:t + 1], cur[:, 2 + t:3 + t], ALU.is_equal, ALU.mult)
                x.then_inc(gwt_in, 1)
                for m, (kind, c, i) in enumerate(MOE_ORDER[:-1]):
                    if (kind, i) == ("u", 1):
                        dve.wait_ge(e_silu, it * MOE_CHUNKS + c + 1)
                        V.tensor_tensor(a_moe, bank[2 + c % 2][:, :], sil_moe, ALU.mult).then_inc(e_af, 1)
                    low_of(m + HSLOTS)
                    if i and c == 0 and kind != "d":
                        add_out(it, 2 if kind == "u" else 0)
                        add_out(it, 3 if kind == "u" else 1)
                    if (kind, i) == ("g", 1) and c:
                        hidden(c - 1)
                    if (kind, c, i) == ("g", 3, 1):
                        dve.wait_ge(gwt_done, it + 1)
                        V.tensor_copy(GWT, bank[7][:, 0:FRAMES]).then_inc(gwt_ready, 1)
                        one_hot(lk, route[:, e + 1, :]).then_inc(g_ready, 1)
                    if (kind, c, i) == ("u", MOE_CHUNKS - 1, 1):
                        take(it + 1)
                        hidden(c)
                assert links[0] == LINKS

            link(V.memset(rot, 0.0))
            dve.wait_ge(gains_in, 16)
            norm(0, ())
            attention(0)
            norm(1, range(SPLIT_OF[DENSE_AT] + 1, SPLIT_OF[DENSE_AT] + HSLOTS))
            dense()
            norm(2, range(SPLIT_OF[ATTN1_AT] + 1, SPLIT_OF[ATTN1_AT] + HSLOTS))
            attention(1)
            routing()
            dve.wait_ge(rounds_ready, 1)
            rounds = dve.value_load(rounds_sb[0:1, 0:1], min_val=1, max_val=2)
            with dve.Fori(0, rounds) as r:
                with dve.Fori(0, EXPERTS) as e:
                    expert(r * EXPERTS + e, e)
                V.tensor_scalar(route[:, :, 0:2], route[:, :, 0:2], -float(CAP), None, ALU.add).then_inc(round_shifted, 1)
                dve.wait_ge(round_shifted, r + 1)
            its = rounds * EXPERTS
            for j in range(4):
                add_out(its, j)
            dve.wait_ge(fn_in, 16)
            for t in range(2):
                dve.wait_ge(fstd, t + 1)
                link(V.reciprocal(fin[:, t, 1:2], fin[:, t, 1:2]))
                V.scalar_tensor_tensor(out=res[:, t, :], in0=acc[:, t, :], scalar=fin[:, t, 1:2], in1=fn_sb[:, :],
                                       op0=ALU.mult, op1=ALU.mult).then_inc(res_ready, 1)


def _tables():
    f = np.float32
    pos = np.arange(L, dtype=f)

    def angles(dim):
        inv = f(10000.0) ** (-np.arange(0, dim, 2, dtype=f) / f(dim))
        ang = (pos[:, None] * inv[None, :]).astype(f)
        return np.cos(ang).astype(f).T, np.sin(ang).astype(f).T

    c = np.zeros((P, C_COLS), f)
    cos, sin = angles(P)
    c[:, C_COS:C_COS + L], c[:, C_SIN:C_SIN + L] = np.tile(cos, (2, 1)), np.tile(sin, (2, 1))
    cos, sin = angles(ROPE)
    c[:, C_COS64:C_COS64 + L], c[:, C_SIN64:C_SIN64 + L] = np.tile(cos, (4, 1)), np.tile(sin, (4, 1))
    c[:, C_ID:C_ID + P] = np.eye(P)
    c[:, C_TRI:C_TRI + P] = np.triu(np.ones((P, P)), 1)

    def swap(half):
        m = np.zeros((P, P), f)
        for b in range(0, P, 2 * half):
            for i in range(half):
                m[b + half + i, b + i] = -1.0
                m[b + i, b + half + i] = 1.0
        return m

    c[:, C_SW:C_SW + P], c[:, C_SW64:C_SW64 + P] = swap(P // 2), swap(ROPE // 2)
    c[:, C_IOTA:C_IOTA + CAP] = np.arange(CAP)
    c[:, C_LOW:C_PACK] = np.tril(np.ones((EXPERTS, EXPERTS)), -1).ravel()
    c[:, C_PACK + 96:C_PACK + P] = 1.0
    for h in range(HEADS):
        c[32 * h, C_ROW + h * P:C_ROW + (h + 1) * P] = 1.0

    gamma = np.log1p(-np.exp2(-5.0 - np.arange(HEADS, dtype=np.float64)))
    t1, t2 = np.zeros((P, T1_COLS), f), np.zeros((P, T2_COLS), f)
    j = np.arange(P)
    i = np.arange(2 * P)
    allowed = i[None, :] // CHUNK >= j[:, None] // CHUNK
    for h in range(HEADS):
        w = np.exp(gamma[h] * np.abs(i[None, :] - j[:, None])) * allowed * P ** -0.5
        t1[:, h * DECAY:h * DECAY + 2 * P] = w
        t1[:, h * DECAY + 2 * P:(h + 1) * DECAY] = w[:, :P]
        a = np.arange(L)
        t2[:META, h * L:(h + 1) * L] = np.exp(gamma[h] * np.abs(a[None, :] - np.arange(META)[:, None])) * P ** -0.5
    block = np.where(j[:, None] // CHUNK >= j[None, :] // CHUNK, 0.0, -BIG)
    m = t1[:, HEADS * DECAY:]
    m[:, META:META + P] = block
    m[:, META + P + META + P:] = block
    return c, t1, t2


def kernel(**inputs):
    import numpy as _np
    import concourse.bacc as _bacc
    from concourse import mybir as _mybir
    from concourse.bass_utils import run_bass_kernel_spmd as _run

    x = {k: _np.asarray(v) for k, v in inputs.items()}
    consts, t1, t2 = _tables()
    units = _np.zeros((N_UNITS, P, UNIT), _np.float32)

    def cols(w):
        return w.reshape(DK, P, 256).transpose(1, 0, 2).reshape(P, UNIT)

    for layer in range(2):
        at = 0 if layer == 0 else ATTN1_AT
        rq, rk, rv, rg, cq, ckv, kr = _np.split(x["w_in"][layer], [512, 1024, 1536, 2048, 2304, 2432], axis=1)
        units[at] = cols(_np.concatenate([ckv, kr, kr], axis=1))
        units[at + 1] = cols(cq)
        for i in range(2):
            units[at + 2 + i] = cols(rq[:, 256 * i:256 * (i + 1)])
            units[at + 4 + i] = cols(rk[:, 256 * i:256 * (i + 1)])
            units[at + U_RV + i] = rv[512 * i:512 * (i + 1)].reshape(4, P, 512).transpose(1, 0, 2).reshape(P, UNIT)
            units[at + U_RG + i] = cols(rg[:, 256 * i:256 * (i + 1)])
        uq = x["w_uq"][layer].reshape(QR, HEADS, P + ROPE)
        uq = _np.concatenate([uq[:, :, P:].reshape(QR, HEADS * ROPE), uq[:, :, :P].reshape(QR, HEADS * P)], axis=1)
        units[at + U_UQ, :, :UQ_COLS] = uq.reshape(2, P, 768).transpose(1, 0, 2).reshape(P, UQ_COLS)
        ukv = x["w_ukv"][layer].reshape(KVR, HEADS, 2, P).transpose(0, 2, 1, 3)
        units[at + U_UKV, :, :UKV_COLS] = ukv.reshape(KVR, UKV_COLS)
        units[at + U_T1, :, :T1_COLS], units[at + U_T2, :, :T2_COLS] = t1, t2
        for i in range(4):
            units[at + U_WO + i] = cols(x["w_out"][layer][:, 256 * i:256 * (i + 1)])

    def ffn(at, gate, up, down):
        for n, (kind, c) in enumerate(FFN_ORDER):
            if kind == "d":
                units[at + n] = down[256 * c:256 * (c + 1)].reshape(2, P, D).transpose(1, 0, 2).reshape(P, UNIT)
            else:
                units[at + n] = cols((gate if kind == "g" else up)[:, 256 * c:256 * (c + 1)])

    ffn(DENSE_AT, x["dense_w_gate"][0], x["dense_w_up"][0], x["dense_w_down"][0])
    for e in range(EXPERTS):
        for n, (kind, c, i) in enumerate(MOE_ORDER):
            if kind == "d":
                w = x["moe_w_down"][0, e][512 * c + 256 * i:512 * c + 256 * (i + 1)].reshape(2, P, D)
            else:
                w = x["moe_w_gate" if kind == "g" else "moe_w_up"][0, e][512 * i:512 * (i + 1), 512 * c:512 * (c + 1)].reshape(4, P, 512)
            units[MOE_AT + e * FFN_UNITS + n] = w.transpose(1, 0, 2).reshape(P, UNIT)

    def lanes(v):
        return v.reshape(-1, P).T

    gains = _np.concatenate([lanes(x[n]) for n in ("attn_norm", "ffn_norm", "ret_out_gain", "mla_out_gain", "q_norm", "kv_norm")], axis=1)
    h0 = _np.concatenate([x["meta_tokens"], x["x"][0]], axis=0).T.reshape(DK, P, L).transpose(1, 0, 2)
    arrays = {
        "stream": units, "h0": h0, "gains": gains,
        "router_w": x["router_w"][0].reshape(DK, P, EXPERTS).transpose(1, 0, 2),
        "fnorm": _np.broadcast_to(_np.stack([x["final_norm"], x["ffn_norm"][1]]), (P, 2, D)), "consts": consts,
    }
    arrays = {k: _np.ascontiguousarray(v) for k, v in arrays.items()}
    nc = _bacc.Bacc("TRN2", target_bir_lowering=False, num_devices=1)
    args = [nc.dram_tensor(k, v.shape, _mybir.dt.float32, kind="ExternalInput").ap() for k, v in arrays.items()]
    args.append(nc.dram_tensor("out", (FRAMES, D), _mybir.dt.float32, kind="ExternalOutput").ap())
    build(nc, *args)
    r = _run(nc, [arrays], core_ids=[0])
    return _np.asarray(r.results[0]["out"]).reshape(1, FRAMES, D)
```
